# Optimizing a Trainium2 kernel written in Bass

```python
import math
import jax, jax.numpy as jnp
from jax import lax
import numpy as np
import jax
import jax.numpy as jnp

D_MODEL = 1024
BATCH = 1
SEQ = 256
DEPTH = 2

CHUNK = 64
N_A_LAYERS = DEPTH // 2
N_B_LAYERS = DEPTH - N_A_LAYERS

SSM_EXPAND = 2
D_INNER = SSM_EXPAND * D_MODEL
SSM_HEAD_DIM = 64
SSM_HEADS = D_INNER // SSM_HEAD_DIM
SSM_GROUPS = 8
SSM_HEADS_PER_GROUP = SSM_HEADS // SSM_GROUPS
D_STATE = 128
D_CONV = 4
CONV_DIM = D_INNER + 2 * SSM_GROUPS * D_STATE
D_IN_PROJ = 2 * D_INNER + 2 * SSM_GROUPS * D_STATE + SSM_HEADS
DT_MIN = 1e-3
DT_MAX = 1e-1

SB_HEADS = 16
SB_HEAD_DIM = D_MODEL // SB_HEADS
SB_WIDTH = SB_HEADS * SB_HEAD_DIM
Q_BLOCK = 128

D_FF = 4 * D_MODEL

DEEPNORM_ALPHA = (2 * DEPTH) ** 0.25
DEEPNORM_BETA = (8 * DEPTH) ** -0.25
LN_EPS = 1e-5
RMS_EPS = 1e-5


def layer_norm(x, g, b):
    xf = x.astype(jnp.float32)
    mu = jnp.mean(xf, axis=-1, keepdims=True)
    var = jnp.mean(jnp.square(xf - mu), axis=-1, keepdims=True)
    return ((xf - mu) * lax.rsqrt(var + LN_EPS) * g.astype(jnp.float32) + b.astype(jnp.float32)).astype(x.dtype)

def causal_depthwise_conv(u, w, b):
    c = u.shape[-1]
    y = lax.conv_general_dilated(
        u, w[:, None, :], window_strides=(1,), padding=[(D_CONV - 1, 0)],
        dimension_numbers=("NWC", "WIO", "NWC"), feature_group_count=c)
    return y + b

def segsum(a):
    t = a.shape[-1]
    cs = jnp.cumsum(a, axis=-1)
    diff = cs[..., :, None] - cs[..., None, :]
    mask = jnp.tril(jnp.ones((t, t), dtype=bool))
    return jnp.where(mask, diff, -jnp.inf)

def ssd_chunked_scan(x, da, bm, cm):
    b, l, h, p = x.shape
    c = l // CHUNK
    g, r, n = SSM_GROUPS, SSM_HEADS_PER_GROUP, D_STATE
    xc = x.reshape(b, c, CHUNK, g, r, p)
    bc = bm.reshape(b, c, CHUNK, g, n)
    cc = cm.reshape(b, c, CHUNK, g, n)
    a = da.astype(jnp.float32).reshape(b, c, CHUNK, g, r).transpose(0, 1, 3, 4, 2)
    a_cs = jnp.cumsum(a, axis=-1)
    decay_mat = jnp.exp(segsum(a))
    cb = jnp.einsum("bclgn,bcsgn->bcgls", cc, bc)
    y_diag = jnp.einsum("bcgls,bcgrls,bcsgrp->bclgrp", cb, decay_mat, xc)
    decay_states = jnp.exp(a_cs[..., -1:] - a_cs)
    states = jnp.einsum("bclgn,bcgrl,bclgrp->bcgrpn", bc, decay_states, xc).astype(jnp.float32)
    block_decay = jnp.exp(a_cs[..., -1])

    def step(carry, inp):
        s_c, d_c = inp
        return carry * d_c[..., None, None] + s_c, carry

    init = jnp.zeros((b, g, r, p, n), jnp.float32)
    _, prev = lax.scan(step, init, (jnp.moveaxis(states, 1, 0), jnp.moveaxis(block_decay, 1, 0)))
    prev = jnp.moveaxis(prev, 0, 1)
    y_off = jnp.einsum("bclgn,bcgrpn,bcgrl->bclgrp", cc, prev, jnp.exp(a_cs))
    return (y_diag + y_off).reshape(b, l, h, p).astype(x.dtype)

def mamba2_mixer(u, w_in, conv_w, conv_b, dt_bias, a_log, d_skip, norm_w, w_out):
    b, l, _ = u.shape
    zxbcdt = u @ w_in
    z = zxbcdt[..., :D_INNER]
    xbc = zxbcdt[..., D_INNER:D_INNER + CONV_DIM]
    dt_raw = zxbcdt[..., D_INNER + CONV_DIM:]
    xbc = jax.nn.silu(causal_depthwise_conv(xbc, conv_w, conv_b))
    xs = xbc[..., :D_INNER]
    bm = xbc[..., D_INNER:D_INNER + SSM_GROUPS * D_STATE].reshape(b, l, SSM_GROUPS, D_STATE)
    cm = xbc[..., D_INNER + SSM_GROUPS * D_STATE:].reshape(b, l, SSM_GROUPS, D_STATE)
    dt = jax.nn.softplus((dt_raw + dt_bias).astype(jnp.float32))
    a = -jnp.exp(a_log.astype(jnp.float32))
    xh = xs.reshape(b, l, SSM_HEADS, SSM_HEAD_DIM)
    y = ssd_chunked_scan(xh * dt[..., None].astype(xh.dtype), dt * a, bm, cm)
    y = (y + xh * d_skip[:, None]).reshape(b, l, D_INNER)
    yg = (y * jax.nn.silu(z)).astype(jnp.float32).reshape(b, l, SSM_GROUPS, D_INNER // SSM_GROUPS)
    yg = yg * lax.rsqrt(jnp.mean(jnp.square(yg), axis=-1, keepdims=True) + RMS_EPS)
    y = (yg.reshape(b, l, D_INNER) * norm_w.astype(jnp.float32)).astype(u.dtype)
    return y @ w_out

def shared_kv(h, w_k, w_v):
    b, l, _ = h.shape
    k = (h @ w_k).reshape(b, l, SB_HEADS, SB_HEAD_DIM).transpose(0, 2, 1, 3)
    v = (h @ w_v).reshape(b, l, SB_HEADS, SB_HEAD_DIM).transpose(0, 2, 1, 3)
    return k, v

def stick_breaking_attention(u, w_q, k, v, w_o):
    b, l, _ = u.shape
    q = (u @ w_q).reshape(b, l, SB_HEADS, SB_HEAD_DIM).transpose(0, 2, 1, 3) * (SB_HEAD_DIM ** -0.5)
    nb = l // Q_BLOCK
    kb = jnp.moveaxis(k.reshape(b, SB_HEADS, nb, Q_BLOCK, SB_HEAD_DIM), 2, 0)
    vb = jnp.moveaxis(v.reshape(b, SB_HEADS, nb, Q_BLOCK, SB_HEAD_DIM), 2, 0)
    idx = jnp.arange(Q_BLOCK)
    diag_mask = idx[None, :] < idx[:, None]
    later = (idx[:, None] > idx[None, :]).astype(jnp.float32)

    outs = []
    for i in range(nb):
        qi = q[:, :, i * Q_BLOCK:(i + 1) * Q_BLOCK]

        def step(carry, inp, qi=qi):
            acc, o = carry
            kj, vj, is_diag = inp
            z = jnp.einsum("bhqd,bhkd->bhqk", qi, kj).astype(jnp.float32)
            valid = jnp.logical_or(jnp.logical_not(is_diag), diag_mask)
            lo = jnp.where(valid, jax.nn.log_sigmoid(-z), 0.0)
            after = jnp.einsum("bhqj,js->bhqs", lo, later) + acc[..., None]
            logw = jnp.where(valid, z + lo + after, -jnp.inf)
            o = o + jnp.einsum("bhqk,bhkd->bhqd", jnp.exp(logw).astype(vj.dtype), vj).astype(jnp.float32)
            acc = acc + jnp.sum(lo, axis=-1)
            return (acc, o), None

        init = (jnp.zeros((b, SB_HEADS, Q_BLOCK), jnp.float32),
                jnp.zeros((b, SB_HEADS, Q_BLOCK, SB_HEAD_DIM), jnp.float32))
        xs = (kb[:i + 1][::-1], vb[:i + 1][::-1], jnp.arange(i + 1) == 0)
        (_, o_i), _ = lax.scan(step, init, xs)
        outs.append(o_i.astype(u.dtype))
    o = jnp.concatenate(outs, axis=2)
    o = o.transpose(0, 2, 1, 3).reshape(b, l, SB_WIDTH)
    return o @ w_o

def squared_relu_mlp(h, w1, w2):
    return jnp.square(jax.nn.relu(h @ w1)) @ w2

def first_inputs(seed: int = 0) -> dict:
    key = jax.random.key(seed)
    ks = jax.random.split(key, 20)
    f32 = jnp.float32

    def nrm(k, shape, scale):
        return jax.random.normal(k, shape, f32) * scale

    x = nrm(ks[0], (BATCH, SEQ, D_MODEL), 1.0)
    ssm_w_in = nrm(ks[1], (N_A_LAYERS, D_MODEL, D_IN_PROJ), D_MODEL ** -0.5)
    ssm_conv_w = jax.random.uniform(ks[2], (N_A_LAYERS, D_CONV, CONV_DIM), f32, -0.5, 0.5)
    ssm_conv_b = nrm(ks[3], (N_A_LAYERS, CONV_DIM), 0.02)
    dt = jnp.exp(jax.random.uniform(ks[4], (N_A_LAYERS, SSM_HEADS), f32)
                 * (math.log(DT_MAX) - math.log(DT_MIN)) + math.log(DT_MIN))
    dt = jnp.maximum(dt, 1e-4)
    ssm_dt_bias = dt + jnp.log(-jnp.expm1(-dt))
    ssm_a_log = jnp.log(jax.random.uniform(ks[5], (N_A_LAYERS, SSM_HEADS), f32, 1.0, 16.0))
    ssm_d = 1.0 + nrm(ks[6], (N_A_LAYERS, SSM_HEADS), 0.1)
    ssm_norm_w = 1.0 + nrm(ks[7], (N_A_LAYERS, D_INNER), 0.1)
    ssm_w_out = nrm(ks[8], (N_A_LAYERS, D_INNER, D_MODEL), D_INNER ** -0.5 * DEEPNORM_BETA)
    sb_w_k = nrm(ks[9], (D_MODEL, SB_WIDTH), D_MODEL ** -0.5)
    sb_w_v = nrm(ks[10], (D_MODEL, SB_WIDTH), D_MODEL ** -0.5 * DEEPNORM_BETA)
    sb_w_q = nrm(ks[11], (N_B_LAYERS, D_MODEL, SB_WIDTH), D_MODEL ** -0.5)
    sb_w_o = nrm(ks[12], (N_B_LAYERS, SB_WIDTH, D_MODEL), SB_WIDTH ** -0.5 * DEEPNORM_BETA)
    mlp_w1 = nrm(ks[13], (DEPTH, D_MODEL, D_FF), D_MODEL ** -0.5)
    mlp_w2 = nrm(ks[14], (DEPTH, D_FF, D_MODEL), D_FF ** -0.5 * DEEPNORM_BETA)
    ln_mix_g = 1.0 + nrm(ks[15], (DEPTH, D_MODEL), 0.05)
    ln_mix_b = nrm(ks[16], (DEPTH, D_MODEL), 0.02)
    ln_mlp_g = 1.0 + nrm(ks[17], (DEPTH, D_MODEL), 0.05)
    ln_mlp_b = nrm(ks[18], (DEPTH, D_MODEL), 0.02)
    return {"x": x, "ssm_w_in": ssm_w_in, "ssm_conv_w": ssm_conv_w, "ssm_conv_b": ssm_conv_b,
            "ssm_dt_bias": ssm_dt_bias, "ssm_a_log": ssm_a_log, "ssm_d": ssm_d,
            "ssm_norm_w": ssm_norm_w, "ssm_w_out": ssm_w_out, "sb_w_k": sb_w_k, "sb_w_v": sb_w_v,
            "sb_w_q": sb_w_q, "sb_w_o": sb_w_o, "mlp_w1": mlp_w1, "mlp_w2": mlp_w2,
            "ln_mix_g": ln_mix_g, "ln_mix_b": ln_mix_b, "ln_mlp_g": ln_mlp_g, "ln_mlp_b": ln_mlp_b}

def first_block(x, ssm_w_in, ssm_conv_w, ssm_conv_b, ssm_dt_bias, ssm_a_log, ssm_d, ssm_norm_w,
              ssm_w_out, sb_w_k, sb_w_v, sb_w_q, sb_w_o, mlp_w1, mlp_w2,
              ln_mix_g, ln_mix_b, ln_mlp_g, ln_mlp_b):
    h = x
    k = v = None
    for layer in range(DEPTH):
        if layer < N_A_LAYERS:
            i = layer
            mix = mamba2_mixer(h, ssm_w_in[i], ssm_conv_w[i], ssm_conv_b[i], ssm_dt_bias[i],
                               ssm_a_log[i], ssm_d[i], ssm_norm_w[i], ssm_w_out[i])
        else:
            if layer == N_A_LAYERS:
                k, v = shared_kv(h, sb_w_k, sb_w_v)
            j = layer - N_A_LAYERS
            mix = stick_breaking_attention(h, sb_w_q[j], k, v, sb_w_o[j])
        h = layer_norm(DEEPNORM_ALPHA * h + mix, ln_mix_g[layer], ln_mix_b[layer])
        h = layer_norm(DEEPNORM_ALPHA * h + squared_relu_mlp(h, mlp_w1[layer], mlp_w2[layer]),
                       ln_mlp_g[layer], ln_mlp_b[layer])
    return h


DEPTH_2 = 1

H_A = 8
HD_A = 64
W_A = H_A * HD_A
MOBA_BLOCK = 256
MOBA_TOPK = 3
Q_CHUNK = 64
NUM_BUCKETS = 32
MAX_EXACT = NUM_BUCKETS // 2
MAX_DISTANCE = 128
H_B = 4
HD_B = 128
W_B = H_B * HD_B
CONV_K = 4
DN_CHUNK = 64
N_GROUPS = 4
EXPERTS_PER_GROUP = 8
TOPK_IN_GROUP = 2
D_FF_EXPERT = 256
D_IN = 3 * W_A + 4 * W_B + 2 * H_B + 2 * D_MODEL
N_MOD = 6
EPS = 1e-6
NEG = -1e30


def rms_norm(x, w):
    xf = x.astype(jnp.float32)
    y = xf * lax.rsqrt(jnp.mean(xf * xf, axis=-1, keepdims=True) + EPS)
    return (y * w.astype(jnp.float32)).astype(x.dtype)

def l2_normalize(t):
    return t * lax.rsqrt(jnp.sum(t * t, axis=-1, keepdims=True) + EPS)

def t5_bucket(dist):
    n = jnp.maximum(dist, 0)
    nf = jnp.maximum(n, 1).astype(jnp.float32)
    large = MAX_EXACT + (jnp.log(nf / MAX_EXACT) / math.log(MAX_DISTANCE / MAX_EXACT)
                         * (NUM_BUCKETS - MAX_EXACT)).astype(jnp.int32)
    large = jnp.minimum(large, NUM_BUCKETS - 1)
    return jnp.where(n < MAX_EXACT, n, large)

def moba_attention(q, k, v, rel_bias):
    B, H, S, hd = q.shape
    L = MOBA_BLOCK
    Sp = -(-S // L) * L
    pad = ((0, 0), (0, 0), (0, Sp - S), (0, 0))
    q, k, v = jnp.pad(q, pad), jnp.pad(k, pad), jnp.pad(v, pad)
    NB, NQ = Sp // L, Sp // Q_CHUNK
    topk = min(MOBA_TOPK, NB)
    scale = HD_A ** -0.5
    k_blocks = k.reshape(B, H, NB, L, hd)
    v_blocks = v.reshape(B, H, NB, L, hd)
    k_mean = jnp.mean(k_blocks.astype(jnp.float32), axis=3)
    q_blk = jnp.arange(Sp) // L
    gate = jnp.einsum('bhsd,bhnd->bhsn', q.astype(jnp.float32), k_mean)
    gate = jnp.where(jnp.arange(NB)[None, :] < q_blk[:, None], gate, NEG)
    _, sel = lax.top_k(gate, topk)
    q_c = q.reshape(B, H, NQ, Q_CHUNK, hd).transpose(2, 0, 1, 3, 4)
    sel_c = sel.reshape(B, H, NQ, Q_CHUNK, topk).transpose(2, 0, 1, 3, 4)
    bi = jnp.arange(B)[:, None, None, None]
    hi = jnp.arange(H)[None, :, None, None]
    hi5 = hi[..., None]
    offs = jnp.arange(L)

    def one_chunk(args):
        q_i, sel_i, i = args
        qb = (i * Q_CHUNK) // L
        q_pos = i * Q_CHUNK + jnp.arange(Q_CHUNK)
        k_sel = k_blocks[bi, hi, sel_i]
        v_sel = v_blocks[bi, hi, sel_i]
        dist_sel = q_pos[None, None, :, None, None] - (sel_i[..., None] * L + offs)
        bias_sel = rel_bias[t5_bucket(dist_sel), hi5].astype(jnp.float32)
        s_sel = jnp.einsum('bhqd,bhqkld->bhqkl', q_i, k_sel).astype(jnp.float32) * scale + bias_sel
        s_sel = jnp.where((sel_i < qb)[..., None], s_sel, NEG)
        k_own = lax.dynamic_index_in_dim(k_blocks, qb, axis=2, keepdims=False)
        v_own = lax.dynamic_index_in_dim(v_blocks, qb, axis=2, keepdims=False)
        dist_own = q_pos[:, None] - (qb * L + offs)[None, :]
        bias_own = rel_bias[t5_bucket(dist_own)].transpose(2, 0, 1).astype(jnp.float32)
        s_own = jnp.einsum('bhqd,bhld->bhql', q_i, k_own).astype(jnp.float32) * scale + bias_own
        s_own = jnp.where(dist_own >= 0, s_own, NEG)
        p = jax.nn.softmax(jnp.concatenate(
            [s_sel.reshape(B, H, Q_CHUNK, topk * L), s_own], axis=-1), axis=-1)
        p_sel = p[..., :topk * L].reshape(B, H, Q_CHUNK, topk, L).astype(v.dtype)
        p_own = p[..., topk * L:].astype(v.dtype)
        return (jnp.einsum('bhqkl,bhqkld->bhqd', p_sel, v_sel)
                + jnp.einsum('bhql,bhld->bhqd', p_own, v_own))

    o = lax.map(one_chunk, (q_c, sel_c, jnp.arange(NQ)))
    o = o.transpose(1, 2, 0, 3, 4).reshape(B, H, Sp, hd)
    return o[:, :, :S]

def causal_depthwise_conv_2(x, w):
    C = x.shape[-1]
    return lax.conv_general_dilated(
        x, w[:, None, :].astype(x.dtype), window_strides=(1,), padding=[(CONV_K - 1, 0)],
        dimension_numbers=('NWC', 'WIO', 'NWC'), feature_group_count=C)

def gated_delta_rule(q, k, v, beta, g):
    out_dtype = v.dtype
    B, S, H, DK = q.shape
    DV = v.shape[-1]
    C = DN_CHUNK
    N = S // C
    f32 = jnp.float32
    q = l2_normalize(q.astype(f32)) * (DK ** -0.5)
    k = l2_normalize(k.astype(f32))
    v = v.astype(f32)

    def chunk(t):
        return t.reshape(B, N, C, H, -1).transpose(0, 3, 1, 2, 4)

    q, k, v = chunk(q), chunk(k), chunk(v)
    beta = beta.astype(f32).reshape(B, N, C, H).transpose(0, 3, 1, 2)
    G = jnp.cumsum(g.astype(f32).reshape(B, N, C, H).transpose(0, 3, 1, 2), axis=-1)
    tril = jnp.tril(jnp.ones((C, C), bool))
    strict = jnp.tril(jnp.ones((C, C), bool), -1)
    dec = jnp.exp(jnp.where(tril, G[..., :, None] - G[..., None, :], -jnp.inf))
    kb = k * beta[..., None]
    A = jnp.eye(C, dtype=f32) + jnp.where(strict, jnp.einsum('bhnid,bhnjd->bhnij', kb, k) * dec, 0.0)
    u = lax.linalg.triangular_solve(A, v * beta[..., None], left_side=True, lower=True, unit_diagonal=True)
    w = lax.linalg.triangular_solve(A, kb * jnp.exp(G)[..., None], left_side=True, lower=True, unit_diagonal=True)
    P = jnp.einsum('bhnid,bhnjd->bhnij', q, k) * dec
    qg = q * jnp.exp(G)[..., None]
    kd = k * jnp.exp(G[..., -1:] - G)[..., None]
    gl = jnp.exp(G[..., -1])
    xs = tuple(jnp.moveaxis(t, 2, 0) for t in (u, w, qg, P, kd, gl))

    def step(state, inp):
        u_n, w_n, qg_n, P_n, kd_n, gl_n = inp
        v_new = u_n - jnp.einsum('bhck,bhkv->bhcv', w_n, state)
        o_n = jnp.einsum('bhck,bhkv->bhcv', qg_n, state) + jnp.einsum('bhcj,bhjv->bhcv', P_n, v_new)
        state = state * gl_n[..., None, None] + jnp.einsum('bhck,bhcv->bhkv', kd_n, v_new)
        return state, o_n

    _, o = lax.scan(step, jnp.zeros((B, H, DK, DV), f32), xs)
    return o.transpose(1, 0, 3, 2, 4).reshape(B, S, H, DV).astype(out_dtype)

def token_mixer(h, rel_bias, w_in, conv_w, a_log, dt_bias, onorm_w, w_up_a, w_up_b, w_out):
    B, S, _ = h.shape
    proj = h @ w_in
    sizes = (W_A, W_A, W_A, 3 * W_B, W_B, H_B, H_B, D_MODEL, D_MODEL)
    offs = np.cumsum(sizes)[:-1].tolist()
    qa, ka, va, qkv_b, z_b, b_b, a_b, gate_a, gate_b = jnp.split(proj, offs, axis=-1)
    heads_a = lambda t: t.reshape(B, S, H_A, HD_A).transpose(0, 2, 1, 3)
    y_a = moba_attention(heads_a(qa), heads_a(ka), heads_a(va), rel_bias)
    y_a = y_a.transpose(0, 2, 1, 3).reshape(B, S, W_A)
    qkv_b = jax.nn.silu(causal_depthwise_conv_2(qkv_b, conv_w))
    q_b, k_b, v_b = (t.reshape(B, S, H_B, HD_B) for t in jnp.split(qkv_b, 3, axis=-1))
    beta = jax.nn.sigmoid(b_b)
    g = -jnp.exp(a_log) * jax.nn.softplus(a_b + dt_bias)
    o_b = gated_delta_rule(q_b, k_b, v_b, beta, g)
    o_b = rms_norm(o_b, onorm_w) * jax.nn.silu(z_b.reshape(B, S, H_B, HD_B))
    y_b = o_b.reshape(B, S, W_B)
    m = jax.nn.sigmoid(gate_a) * (y_a @ w_up_a) + jax.nn.sigmoid(gate_b) * (y_b @ w_up_b)
    return m @ w_out

def hier_moe(h, w_rg, b_rg, w_re, b_re, w_e_gate, w_e_up, w_e_down):
    B, S, D = h.shape
    t = h.reshape(-1, D)
    T = t.shape[0]
    pg = jax.nn.softmax((t @ w_rg + b_rg).astype(jnp.float32), axis=-1)
    p_top, g_top = lax.top_k(pg, 1)
    oh_g = jax.nn.one_hot(g_top[:, 0], N_GROUPS, dtype=jnp.float32)
    le = (t @ w_re + b_re).astype(jnp.float32).reshape(T, N_GROUPS, EXPERTS_PER_GROUP)
    le_g = jnp.einsum('tge,tg->te', le, oh_g)
    v2, e2 = lax.top_k(le_g, TOPK_IN_GROUP)
    w2 = jax.nn.softmax(v2, axis=-1) * p_top
    comb_e = jnp.sum(w2[..., None] * jax.nn.one_hot(e2, EXPERTS_PER_GROUP, dtype=jnp.float32), axis=1)
    comb = (oh_g[:, :, None] * comb_e[:, None, :]).astype(t.dtype)
    y = jnp.zeros_like(t)
    for gi in range(N_GROUPS):
        a = jax.nn.silu(jnp.einsum('td,edf->tef', t, w_e_gate[gi])) * jnp.einsum('td,edf->tef', t, w_e_up[gi])
        y = y + jnp.einsum('tef,te,efd->td', a, comb[:, gi], w_e_down[gi])
    return y.reshape(B, S, D)

def second_inputs(seed: int = 0) -> dict:
    key = jax.random.key(seed)
    ks = iter(jax.random.split(key, 32))
    L, D = DEPTH_2, D_MODEL
    G, E, F = N_GROUPS, EXPERTS_PER_GROUP, D_FF_EXPERT

    def nrm(shape, std):
        return std * jax.random.normal(next(ks), shape, jnp.float32)

    x = nrm((BATCH, SEQ, D), 1.0)
    c = nrm((BATCH, D), 1.0)
    rel_bias = nrm((NUM_BUCKETS, H_A), 0.5)
    final_norm_w = 1.0 + nrm((D,), 0.02)
    norm1_w = 1.0 + nrm((L, D), 0.02)
    norm2_w = 1.0 + nrm((L, D), 0.02)
    w_mod = nrm((L, D, N_MOD * D), 0.5 * D ** -0.5)
    b_mod = nrm((L, N_MOD * D), 0.02)
    w_in = nrm((L, D, D_IN), D ** -0.5)
    conv_w = nrm((L, CONV_K, 3 * W_B), CONV_K ** -0.5)
    a_log = jnp.log(jax.random.uniform(next(ks), (L, H_B), jnp.float32, 1.0, 16.0))
    dt = jnp.exp(jax.random.uniform(next(ks), (L, H_B), jnp.float32, math.log(1e-3), math.log(1e-1)))
    dt_bias = dt + jnp.log(-jnp.expm1(-dt))
    onorm_w = 1.0 + nrm((L, HD_B), 0.02)
    w_up_a = nrm((L, W_A, D), W_A ** -0.5)
    w_up_b = nrm((L, W_B, D), W_B ** -0.5)
    w_out = nrm((L, D, D), D ** -0.5)
    w_rg = nrm((L, D, G), D ** -0.5)
    b_rg = nrm((L, G), 0.01)
    w_re = nrm((L, D, G * E), D ** -0.5)
    b_re = nrm((L, G * E), 0.01)
    w_e_gate = nrm((L, G, E, D, F), D ** -0.5)
    w_e_up = nrm((L, G, E, D, F), D ** -0.5)
    w_e_down = nrm((L, G, E, F, D), F ** -0.5)
    return {"x": x, "c": c, "rel_bias": rel_bias, "final_norm_w": final_norm_w,
            "norm1_w": norm1_w, "norm2_w": norm2_w, "w_mod": w_mod, "b_mod": b_mod,
            "w_in": w_in, "conv_w": conv_w, "a_log": a_log, "dt_bias": dt_bias,
            "onorm_w": onorm_w, "w_up_a": w_up_a, "w_up_b": w_up_b, "w_out": w_out,
            "w_rg": w_rg, "b_rg": b_rg, "w_re": w_re, "b_re": b_re,
            "w_e_gate": w_e_gate, "w_e_up": w_e_up, "w_e_down": w_e_down}

def second_block(x, c, rel_bias, final_norm_w, norm1_w, norm2_w, w_mod, b_mod, w_in, conv_w,
              a_log, dt_bias, onorm_w, w_up_a, w_up_b, w_out, w_rg, b_rg, w_re, b_re,
              w_e_gate, w_e_up, w_e_down):
    c_act = jax.nn.silu(c)
    for l in range(DEPTH_2):
        mod = (c_act @ w_mod[l] + b_mod[l])[:, None, :]
        sh1, sc1, g1, sh2, sc2, g2 = jnp.split(mod, N_MOD, axis=-1)
        h = rms_norm(x, norm1_w[l]) * (1.0 + sc1) + sh1
        x = x + g1 * token_mixer(h, rel_bias, w_in[l], conv_w[l], a_log[l], dt_bias[l],
                                 onorm_w[l], w_up_a[l], w_up_b[l], w_out[l])
        h = rms_norm(x, norm2_w[l]) * (1.0 + sc2) + sh2
        x = x + g2 * hier_moe(h, w_rg[l], b_rg[l], w_re[l], b_re[l],
                              w_e_gate[l], w_e_up[l], w_e_down[l])
    return rms_norm(x, final_norm_w)


def setup_inputs(seed=0):
    out = dict(first_inputs(seed))
    for name, value in second_inputs(seed + 1).items():
        if name != "x":
            out[name + "_2"] = value
    return out


def reference(
    x, ssm_w_in, ssm_conv_w, ssm_conv_b, ssm_dt_bias, ssm_a_log, ssm_d, ssm_norm_w, ssm_w_out,
    sb_w_k, sb_w_v, sb_w_q, sb_w_o, mlp_w1, mlp_w2, ln_mix_g, ln_mix_b, ln_mlp_g, ln_mlp_b, c_2,
    rel_bias_2, final_norm_w_2, norm1_w_2, norm2_w_2, w_mod_2, b_mod_2, w_in_2, conv_w_2,
    a_log_2, dt_bias_2, onorm_w_2, w_up_a_2, w_up_b_2, w_out_2, w_rg_2, b_rg_2, w_re_2, b_re_2,
    w_e_gate_2, w_e_up_2, w_e_down_2,
):
    x = first_block(
        x, ssm_w_in, ssm_conv_w, ssm_conv_b, ssm_dt_bias, ssm_a_log, ssm_d, ssm_norm_w,
        ssm_w_out, sb_w_k, sb_w_v, sb_w_q, sb_w_o, mlp_w1, mlp_w2, ln_mix_g, ln_mix_b, ln_mlp_g,
        ln_mlp_b,
    )
    return second_block(
        x, c_2, rel_bias_2, final_norm_w_2, norm1_w_2, norm2_w_2, w_mod_2, b_mod_2, w_in_2,
        conv_w_2, a_log_2, dt_bias_2, onorm_w_2, w_up_a_2, w_up_b_2, w_out_2, w_rg_2, b_rg_2,
        w_re_2, b_re_2, w_e_gate_2, w_e_up_2, w_e_down_2,
    )


_drawn_inputs = setup_inputs


def setup_inputs(seed=0):
    import zlib

    import numpy as np

    out = dict(_drawn_inputs(seed))
    spreads = {}
    factors = {'ssm_conv_b': 3.473,
     'rel_bias_2': 3.225,
     'final_norm_w_2': 7.716,
     'norm1_w_2': 8.0,
     'norm2_w_2': 5.204,
     'b_mod_2': 3.135,
     'onorm_w_2': 8.0,
     'b_rg_2': 8.0,
     'b_re_2': 45.626}
    for name, (base, spread) in spreads.items():
        noise = np.random.default_rng([zlib.crc32(name.encode()), seed]).standard_normal(out[name].shape)
        drawn = base * np.exp(spread * noise) if base else spread * noise
        out[name] = jnp.asarray(drawn.astype(out[name].dtype))
    for name, factor in factors.items():
        out[name] = (out[name] * factor).astype(out[name].dtype)
    return out
```

```python
from contextlib import ExitStack

import concourse.bass as bass
from concourse import mybir

F32 = mybir.dt.float32
F32R = mybir.dt.float32r
ACT = mybir.ActivationFunctionType
ALU = mybir.AluOpType
AX_X = mybir.AxisListType.X

P = 128
T = 256
TT = T // P
D = 1024
KD = D // P
ALPHA = 4.0 ** 0.25
LN_EPS = 1e-5
RMS_EPS = 1e-5
EPS2 = 1e-6
NEG = -1e30

D_INNER = 2048
XT_TILES = D_INNER // P
GROUPS = 8
PAIRS = 16
CHUNKS = 16
SB_PAIRS = 8
EXPERTS = 32
H_A = 8
H_B = 4

UNIT = 2048
RING = 4

COUNTS = [("in", 24), ("out", 8), ("mod0", 4), ("mlp0", 32), ("mod1", 4), ("k", 4), ("q", 4), ("v", 4), ("o", 4),
          ("mod2", 4), ("mlp1", 32), ("mod3", 4), ("qa", 2), ("ka", 2), ("va", 2), ("conv2", 6), ("zb", 2), ("gate", 8),
          ("mod4", 4), ("up_a", 2), ("up_b", 2), ("wout2", 4), ("mod5", 4), ("moe", 96)]
FIRST = {}
_n = 0
for _name, _count in COUNTS:
    FIRST[_name] = _n
    _n += _count
UNITS = _n

CONST = {}
_n = 0
for _name, _count in [("ident", 128), ("anti", 128), ("triu_ones", 256), ("mask_neg", 256), ("later", 128),
                      ("before", 128), ("rank", 8)]:
    CONST[_name] = (_n, _n + _count)
    _n += _count
CONST_W = _n
COLS = {}
_n = 0
for _name, _count in [("conv_w", 128), ("conv_b", 32), ("skip", 16), ("norm_w", 16), ("conv2_w", 48), ("c", 8)]:
    COLS[_name] = (_n, _n + _count)
    _n += _count
COLS_W = _n
ROWS = {}
_n = 0
for _name, _count in [("dt_bias", 32), ("a_log", 32), ("a_log2", 4), ("dt_bias2", 4), ("onorm", 128),
                      ("b_route", 36)]:
    ROWS[_name] = (_n, _n + _count)
    _n += _count
ROWS_W = _n
SMALL_W = 76
TABLE_W = 384
LAST = "moe"


def unit(first, p, i=0, per=0):
    u = first + p
    return u // RING + i * (per // RING), u % RING


def wait(eng, sem, value):
    if isinstance(value, int) and value <= 0:
        return
    eng.wait_ge(sem, value)


class Steps:

    def __init__(self, eng, sem):
        self.eng, self.sem, self.n = eng, sem, 0

    def __call__(self, instruction):
        self.n += 1
        instruction.then_inc(self.sem, 1)
        self.eng.wait_ge(self.sem, self.n)


def build(nc, x, weights, small, consts, levels, onehot, cols, rows, ln_rows, rms_rows, b_mod, rel_bias, out):
    with ExitStack() as ctx:
        def at(name, kib, shape, dt=F32):
            return nc.alloc_sbuf_tensor_at(name, shape, dt, offset=16512 + int(kib * 1024))

        def sem(name):
            return ctx.enter_context(nc.semaphore(name))

        ctx.enter_context(nc.sbuf_tensor("arena", [P, 212800 // 4], F32))
        PS = ctx.enter_context(nc.psum_tensor("banks", [P, 8, 512], F32))
        table_dram = nc.dram_tensor("bias_table", (H_A, TABLE_W), F32)
        comb_dram = nc.dram_tensor("combine_table", (EXPERTS, T), F32)

        raw = [at(f"raw{j}", 8 * j, [P, UNIT]) for j in range(RING)]
        hi = [at(f"w_hi{j}", 32 + 8 * j, [P, UNIT], F32R) for j in range(RING)]
        lo = [at(f"w_lo{j}", 64 + 8 * j, [P, UNIT], F32R) for j in range(RING)]
        h = at("h", 96, [P, TT, D])
        hTh = at("hT_hi", 104, [P, KD, T], F32R)
        hTl = at("hT_lo", 112, [P, KD, T], F32R)
        const = at("const", 120, [P, CONST_W])
        col = at("col", 124.25, [P, COLS_W])
        row = at("row", 125.25, [P, ROWS_W])
        tiny = at("tiny", 126.25, [P, 384])
        ln_row = at("ln_gain_bias", 128, [P, 2, D])
        ident = const[:, slice(*CONST["ident"])]
        anti = const[:, slice(*CONST["anti"])]
        triu_ones = const[:, slice(*CONST["triu_ones"])]
        triu, ones = triu_ones[:, 0:128], triu_ones[:, 128:256]
        mask_neg = const[:, slice(*CONST["mask_neg"])]
        later = const[:, slice(*CONST["later"])]
        before = const[:, slice(*CONST["before"])]
        rank = const[:, slice(*CONST["rank"])]
        cc = {n: col[:, a:b] for n, (a, b) in COLS.items()}
        rr = {n: row[:, a:b] for n, (a, b) in ROWS.items()}
        stats = tiny[:, 0:24].rearrange("p (t c s) -> p t c s", t=2, c=2)
        mv = tiny[:, 24:28].rearrange("p (t s) -> p t s", t=2)
        veps, rstd, nmean = tiny[:, 28:30], tiny[:, 30:32], tiny[:, 32:34]
        mhalf = tiny[:, 34:42]
        ms8, rs8 = tiny[:, 42:50], tiny[:, 50:58]
        ncs = tiny[:, 64:128]
        sx, st, su, sv = tiny[:, 128:192], tiny[:, 192:256], tiny[:, 256:320], tiny[:, 320:384]
        sw = at("softplus_ln", 202.75, [P, 64])[:, :]
        dt_all = at("dt", 202.25, [P, 64])[:, :]
        da_all = at("da", 202.5, [P, 64])[:, :]
        small_raw = at("w_small", 188, [P, KD * SMALL_W])
        small_hi = at("w_small_hi", 203, [P, KD * SMALL_W], F32R)
        small_lo = at("w_small_lo", 205.375, [P, KD * SMALL_W], F32R)
        wsh = small_hi[:, :].rearrange("p (k n) -> p k n", k=KD)
        wsl = small_lo[:, :].rearrange("p (k n) -> p k n", k=KD)

        xbcT = at("xbcT", 136, [P, 32, T])
        zT = at("zT", 168, [P, XT_TILES, T])
        X = at("X", 184, [P, TT, D_INNER])
        yTh = at("yT_hi", 152, [P, 2, GROUPS, T], F32R)
        yTl = at("yT_lo", 136, [P, XT_TILES, T], F32R)
        acc = [at(f"conv{b}", 184 + 2 * b, [P, 2, T]) for b in range(2)]
        dec = [at(f"decay{b}", 104 + 3 * b, [P, 2, 384]) for b in range(3)]
        cbs = [at(f"cb{b}", 113 + 1.5 * b, [P, 384]) for b in range(2)]
        ysq = [at(f"y_sq{b}", 116 + 2 * b, [P, 2, T]) for b in range(2)]
        ysk = [at(f"y_skip{b}", 200 + b, [P, T]) for b in range(2)]

        rbuf = [at(f"relu{b}", 160 + 2 * b, [P, 512]) for b in range(2)]
        sbuf = [at(f"relu_sq{b}", 164 + 2 * b, [P, 512]) for b in range(2)]
        aTh = [at(f"act_hi{b}", 168 + 2 * b, [P, 2, T], F32R) for b in range(2)]
        aTl = [at(f"act_lo{b}", 172 + 2 * b, [P, 2, T], F32R) for b in range(2)]
        pre = at("pre_norm", 176, [P, TT, D])

        kT = at("kT", 160, [P, 8, T])
        qT = at("qT", 168, [P, 8, T])
        V = at("v", 176, [P, TT, D])
        oTh = at("oT_hi", 184, [P, 8, T], F32R)
        oTl = at("oT_lo", 192, [P, 8, T], F32R)
        abuf = [at("soft0", 200, [P, 2, 384]), at("soft1", 104, [P, 2, 384])]
        nbuf = [at(f"neg_log{b}", 107 + 3 * b, [P, 2, 384]) for b in range(2)]
        wbuf = [at(f"weight{b}", 113 + 3 * b, [P, 2, 384]) for b in range(2)]

        mod = at("mod", 136, [P, 6, D])
        c_hi = at("c_hi", 126.1875, [P, KD], F32R)
        c_lo = at("c_lo", 126.21875, [P, KD], F32R)
        rms_row = [at("rms_gain0", 184, [P, D]), at("rms_gain1", 116, [P, D])]
        hn = at("normed", 128, [P, TT, D])
        qaT = at("qaT", 160, [P, 4, T])
        kaT = at("kaT", 164, [P, 4, T])
        va = at("va", 168, [P, TT, 512])
        zb = at("z_b", 172, [P, TT, 512])
        qkvT = at("qkvT", 176, [P, 12, T])
        acc2 = [at(f"conv2_{b}", 188 + 2 * b, [P, 2, T]) for b in range(2)]
        gate_a = at("gate_a", 128, [P, TT, D])
        gate_b = at("gate_b", 188, [P, TT, D])
        yaTh = at("yaT_hi", 160, [P, 4, T], F32R)
        yaTl = at("yaT_lo", 164, [P, 4, T], F32R)
        hank = at("bias_rows", 104, [P, H_A, 384])
        prob = [at(f"prob{b}", 196 + 1.5 * b, [P, 384]) for b in range(2)]
        pTb = [at(f"probT{b}", 199 + 1.5 * b, [P, 384]) for b in range(2)]
        tabs = at("bias_table_sb", 196, [33, 2 * TABLE_W])
        relb = at("rel_bias_sb", 199, [33, H_A])
        tiny2 = at("tiny2", 127.75, [P, 64])
        mx, nmx, sums, l2r = (tiny2[:, 16 * n:16 * n + 16] for n in range(4))
        yrs = mx

        bg = tiny[:, 64:80].rearrange("p (t n) -> p t n", t=2)
        beta = tiny[:, 80:88]
        gdec = tiny[:, 88:96]
        ncum = tiny[:, 96:104]
        necum = tiny[:, 104:112]
        ecum = tiny[:, 112:120]
        rn = at("l2_rstd", 104, [P, 8, T])
        XiT = at("inverse_T", 104, [P, 8, P])
        Xi = at("inverse", 108, [P, 8, P])
        NT = at("system_T", 112, [P, 8, P])
        Ub = at("half_product", 116, [P, 8, P])
        lev = at("level_masks", 136, [P, 8, P])
        LT = at("level_T", 140, [P, 8, P])
        PT = at("score_T", 168, [P, 8, P])
        kd = at("k_decayed", 196, [P, 4, P])
        R = at("right_side", 198, [P, 4, P])
        S1 = at("state", 200, [P, 4, P])
        v1 = at("v_tile1", 184, [P, 4, P])
        vn0 = at("v_new0", 186, [P, 4, P])
        ob = at("o_delta", 112, [P, TT, 512])
        osq = at("o_sq", 108, [P, TT, 512])
        ybTh = at("ybT_hi", 104, [P, 4, T], F32R)
        ybTl = at("ybT_lo", 116, [P, 4, T], F32R)
        mm_a = at("mix", 176, [P, TT, D])

        lg = at("logits", 176, [P, TT, 36])
        route = at("route_tmp", 176.5, [P, 5, TT, 8])
        rsc = tiny[:, 128:144]
        le = at("route_le", 177.75, [P, TT, 32])
        comb = at("combine", 178, [P, TT, 32])
        combT = at("combine_T", 179, [32, T])
        cbc = at("combine_rows", 160, [P, EXPERTS, T])
        gbuf = [at(f"gate_silu{b}", 192 + 2 * b, [P, 512]) for b in range(2)]
        ubuf = [at(f"gated{b}", 196 + 2 * b, [P, 512]) for b in range(2)]
        eTh = [at(f"exp_hi{b}", 136 + 2 * b, [P, 2, T], F32R) for b in range(2)]
        eTl = [at(f"exp_lo{b}", 140 + 2 * b, [P, 2, T], F32R) for b in range(2)]
        final_row = at("final_gain", 128, [P, D])
        fin = at("result", 144, [P, TT, D])

        class Signals(dict):

            def __missing__(self, name):
                self[name] = sem(name)
                return self[name]

        S = Signals()
        raw_ready = [S[f"raw_ready{j}"] for j in range(RING)]

        def bank(n, m=1):
            return PS[:, n, :] if m == 1 else PS[:, n:n + m, :]

        def tr_bank(n, b):
            return PS[:, b, :].rearrange("p (c t) -> p c t", c=4)

        block = ctx.enter_context(nc.Block())

        @block.sync
        def _(sp):
            sp.dma_start(h[:, :, :], x.rearrange("(t p) d -> p t d", p=P)).then_inc(S["x_in"], 16)
            sp.dma_start(const[:, :], consts).then_inc(S["const_in"], 16)
            sp.dma_start(small_raw[:, :], small).then_inc(S["const_in"], 16)
            sp.dma_start(col[:, :], cols).then_inc(S["const_in"], 16)
            sp.dma_start(row[:, :], rows.to_broadcast([P, ROWS_W])).then_inc(S["const_in"], 16)
            for j in range(RING):
                sp.dma_start(raw[j][:, :], weights[j]).then_inc(raw_ready[j], 16)

            def load(q, j):
                sp.wait_ge(S["w_lo_done"], 4 * q + j - 3)
                sp.dma_start(raw[j][:, :], weights[bass.ds(4 * q + j, 1), :, :].rearrange("o p n -> (o p) n")
                             ).then_inc(raw_ready[j], 16)

            with sp.Fori(1, UNITS // RING) as q:
                for j in range(RING):
                    load(q, j)
            for j in range(UNITS % RING):
                load(UNITS // RING, j)

            for t in range(TT):
                sp.wait_ge(S["fin_ready"], t + 1)
                sp.dma_start(out[t * P:(t + 1) * P, :], fin[:, t, :]).then_inc(S["out_done"], 16)
            sp.wait_ge(S["out_done"], 16 * TT)

        @block.scalar
        def _(act):
            A = act.activation
            step = Steps(act, S["act_step"])

            def split(q, j):
                if isinstance(q, int) and 4 * q + j >= UNITS:
                    return
                act.wait_ge(raw_ready[j], 16 * q + 16)
                wait(act, S["unit_done"], 4 * q + j - 3)
                A(hi[j][:, :], raw[j][:, :], ACT.Copy).then_inc(S["w_hi_done"], 1)

            def to_T(r, banks=4):
                for n in range(4):
                    act.wait_ge(S["tr_done"], 4 * r + n + 1)
                    A(hTh[:, 4 * (n % 2):4 * (n % 2) + 4, n // 2 * P:(n // 2 + 1) * P],
                      tr_bank(n, banks + n), ACT.Copy).then_inc(S["tr_hi"], 1)

            def softplus(n, ready, before=0):
                act.wait_ge(S[ready[0]], ready[1])
                step(A(st[:, 0:n], sx[:, 0:n], ACT.Abs))
                A(st[:, 0:n], st[:, 0:n], ACT.Exp, scale=-1.0).then_inc(S[ready[2]], 1)
                act.wait_ge(S[ready[2]], before + 1)
                A(sw[:, 0:n], st[:, 0:n], ACT.Ln, bias=1.0).then_inc(S[ready[2]], 1)

            act.wait_ge(S["const_in"], 64)
            A(small_hi[:, :], small_raw[:, :], ACT.Copy).then_inc(S["small_hi_done"], 1)
            for j in range(RING):
                split(0, j)
            to_T(0)
            A(cc["c"], cc["c"], ACT.Silu).then_inc(S["c_ready"], 1)
            act.wait_ge(S["c_ready"], 1)
            A(c_hi[:, :], cc["c"], ACT.Copy).then_inc(S["c_ready"], 1)

            step(A(rr["a_log"], rr["a_log"], ACT.Exp))
            softplus(64, ("dt_read", 1, "dt_exp"))

            def conv(i, j, q):
                u0 = FIRST["in"] + j
                act.wait_ge(S["unit_done"], 4 * i + j + 1)
                for c in range(2):
                    ct = 8 * i + 2 * j + c
                    b = cc["conv_b"][:, bass.ds(ct, 1)]
                    w = cc["conv_w"][:, bass.ds(4 * ct + 3, 1)]
                    A(acc[j % 2][:, c, :], PS[:, j, c * T:(c + 1) * T], ACT.Identity, bias=b, scale=w
                      ).then_inc(S["conv_first"], 1)
                split(i + 1, j)
                act.wait_ge(S["conv_done"], 4 * i + j + 1)
                A(xbcT[:, bass.ds(8 * i + 2 * j, 2), :], acc[j % 2][:, :, :], ACT.Silu).then_inc(S["silu_done"], 1)

            with act.Fori(0, 4) as i:
                for j in range(RING):
                    conv(i, j, None)
            for i in range(4, 6):
                for j in range(RING):
                    n = 4 * i + j - 16
                    act.wait_ge(S["unit_done"], 4 * i + j + 1)
                    A(zT[:, 2 * n:2 * n + 2, :], PS[:, j, :].rearrange("p (c t) -> p c t", c=2), ACT.Silu
                      ).then_inc(S["z_done"], 1)
                    split(i + 1, j)

            def y_square(g):
                act.wait_ge(S["yg_done"], 2 * g + 2)
                wait(act, S["ms_done"], g - 1)
                A(ysq[g % 2][:, :, :], zT[:, 2 * g:2 * g + 2, :], ACT.Square).then_inc(S["sq_done"], 1)

            def y_high(g):
                for c in range(2):
                    act.wait_ge(S["yn_done"], 2 * g + c + 1)
                    A(yTh[:, c, g, :], zT[:, 2 * g + c, :], ACT.Copy).then_inc(S["yhi"], 1)

            for hp in range(PAIRS):
                g = hp // 2
                if hp % 2 == 0:
                    act.wait_ge(S["cb_mm"], g + 1)
                    wait(act, S["m_ready"], 2 * g - 2)
                    A(cbs[g % 2][:, :], PS[:, g % 2, 0:384], ACT.Copy).then_inc(S["cb_read"], 1)
                act.wait_ge(S["d_read"], hp + 1)
                A(dec[hp % 3][:, :, :], dec[hp % 3][:, :, :], ACT.Exp).then_inc(S["exp_done"], 1)
                if hp % 2 == 1 and hp >= 3:
                    y_square((hp - 3) // 2)
                if hp % 2 == 0 and hp >= 8:
                    y_high((hp - 8) // 2)
            y_square(GROUPS - 1)
            for g in range(4, GROUPS):
                y_high(g)

            def plain_splits(first, count):
                for p in range(count):
                    q, j = unit(first, p)
                    split(q + 1, j)

            def layer_norm(r):
                for t in range(TT):
                    act.wait_ge(S["ln_norm_in"], TT * r + t + 1)
                    A(pre[:, t, :], pre[:, t, :], ACT.Identity, bias=nmean[:, t:t + 1], scale=rstd[:, t:t + 1]
                      ).then_inc(S["ln_norm"], 1)

            def mlp(m, first):
                def relu(j, q, s, i, n):
                    act.wait_ge(S["unit_done"], 4 * q + s + 1)
                    A(rbuf[n % 2][:, :], PS[:, n % 4, :], ACT.Relu).then_inc(S["relu_done"], 1)

                def high(j, n):
                    act.wait_ge(S["sq2_done"], j + 1)
                    A(aTh[n % 2][:, :, :], sbuf[n % 2][:, :].rearrange("p (c t) -> p c t", c=2), ACT.Copy
                      ).then_inc(S["act_hi"], 1)

                j0 = CHUNKS * m
                q, s = unit(first, 0)
                relu(j0, q, s, 0, 0)
                split(q + 1, s)
                high(j0, 0)

                def round_of(i, n, k):
                    for e in range(n, n + k):
                        q, s = unit(first, 2 * e - 1, i, 8)
                        relu(None, q, s, i, e)
                        split(q + 1, s)
                        high(j0 + e + 4 * i, e)
                        q, s = unit(first, 2 * e, i, 8)
                        split(q + 1, s)

                with act.Fori(0, 3) as i:
                    round_of(i, 1, 4)
                round_of(3, 1, 3)
                q, s = unit(first, 31)
                split(q + 1, s)

            plain_splits(FIRST["out"], 8)
            layer_norm(0)
            to_T(1, 0)
            plain_splits(FIRST["mod0"], 4)
            mlp(0, FIRST["mlp0"])
            layer_norm(1)
            to_T(2)
            plain_splits(FIRST["mod1"], 4)

            for n in range(8):
                q, j = unit(FIRST["k"], n)
                act.wait_ge(S["unit_done"], 4 * q + j + 1)
                dst, scale = ((kT, 1.0), (qT, 0.125))[n // 4]
                A(dst[:, 2 * (n % 4):2 * (n % 4) + 2, :], PS[:, n % 4, :].rearrange("p (c t) -> p c t", c=2),
                  ACT.Copy, scale=scale).then_inc(S["kq_read"], 1)
                split(q + 1, j)
            for c in range(2):
                for p in range(2):
                    q, j = unit(FIRST["v"], 2 * c + p)
                    split(q + 1, j) if p == 0 else None
                act.wait_ge(S["unit_done"], 4 * q + j + 1)
                for t in range(TT):
                    A(V[:, t, 512 * c:512 * c + 512], PS[:, 4 + 2 * c + t, :], ACT.Copy).then_inc(S["v_read"], 1)
                split(q + 1, j)

            def o_high(p):
                act.wait_ge(S["sb_o"], p + 1)
                A(oTh[:, p, :], PS[:, 6 + p % 2, 0:T], ACT.Copy).then_inc(S["oT_hi_done"], 1)

            for p in range(SB_PAIRS):
                z = PS[:, 2 * (p % 2):2 * (p % 2) + 2, 0:384]
                a = abuf[p % 2]
                act.wait_ge(S["sb_z"], p + 1)
                wait(act, S["sb_nlo"], p - 1)
                step(A(a[:, :, :], z, ACT.Abs))
                step(A(a[:, :, :], a[:, :, :], ACT.Exp, scale=-1.0))
                A(a[:, :, :], a[:, :, :], ACT.Ln, bias=1.0).then_inc(S["sb_abs"], 1)
                if p >= 1:
                    act.wait_ge(S["sb_lw"], p)
                    A(wbuf[(p - 1) % 2][:, :, :], wbuf[(p - 1) % 2][:, :, :], ACT.Exp).then_inc(S["sb_w"], 1)
                if p >= 2:
                    o_high(p - 2)
            act.wait_ge(S["sb_lw"], SB_PAIRS)
            A(wbuf[1][:, :, :], wbuf[1][:, :, :], ACT.Exp).then_inc(S["sb_w"], 1)
            o_high(SB_PAIRS - 2)
            o_high(SB_PAIRS - 1)
            plain_splits(FIRST["o"], 4)

            layer_norm(2)
            to_T(3, 0)
            plain_splits(FIRST["mod2"], 4)
            mlp(1, FIRST["mlp1"])
            layer_norm(3)

            def rms(r):
                for t in range(TT):
                    if r == 0:
                        act.wait_ge(S["h_ready"], 6 + t + 1)
                    else:
                        act.wait_ge(S["res_done"], TT * (r - 1) + t + 1)
                    A(pre[:, t, :], h[:, t, :], ACT.Square, accum_out=ms8[:, t:t + 1]).then_inc(S["rms_sq"], 1)

            rms(0)
            to_T(4)
            plain_splits(FIRST["mod3"], 4)

            act.wait_ge(S["ba_read"], 1)
            A(beta.rearrange("p (t n) -> p t n", t=TT), bg[:, :, 0:4], ACT.Sigmoid).then_inc(S["beta_done"], 1)
            step(A(rr["a_log2"], rr["a_log2"], ACT.Exp))
            softplus(8, ("ba_read", 2, "dt_exp"), 2)

            for n in range(4):
                q, j = unit(FIRST["qa"], n)
                act.wait_ge(S["unit_done"], 4 * q + j + 1)
                A((qaT, kaT)[n // 2][:, 2 * (n % 2):2 * (n % 2) + 2, :],
                  PS[:, n, :].rearrange("p (c t) -> p c t", c=2), ACT.Copy, scale=(0.125, 1.0)[n // 2]
                  ).then_inc(S["qk_read"], 1)
                split(q + 1, j)
            plain_splits(FIRST["va"], 1)
            q, j = unit(FIRST["va"], 1)
            act.wait_ge(S["unit_done"], 4 * q + j + 1)
            for t in range(TT):
                A(va[:, t, :], PS[:, 4 + t, :], ACT.Copy).then_inc(S["v_read"], 1)
            split(q + 1, j)
            for n in range(6):
                q, j = unit(FIRST["conv2"], n)
                act.wait_ge(S["unit_done"], 4 * q + j + 1)
                for c in range(2):
                    w = cc["conv2_w"][:, 4 * (2 * n + c) + 3:4 * (2 * n + c) + 4]
                    A(acc2[n % 2][:, c, :], PS[:, n % 4, c * T:(c + 1) * T], ACT.Copy, scale=w
                      ).then_inc(S["conv_first"], 1)
                split(q + 1, j)
                act.wait_ge(S["conv_done"], 16 + n + 1)
                A(qkvT[:, 2 * n:2 * n + 2, :], acc2[n % 2][:, :, :], ACT.Silu).then_inc(S["silu_done"], 1)
            plain_splits(FIRST["zb"], 1)
            q, j = unit(FIRST["zb"], 1)
            act.wait_ge(S["unit_done"], 4 * q + j + 1)
            for t in range(TT):
                A(zb[:, t, :], PS[:, 6 + t, :], ACT.Silu).then_inc(S["z_done"], 1)
            split(q + 1, j)
            for c in range(4):
                plain_splits(FIRST["gate"] + 2 * c, 1)
                q, j = unit(FIRST["gate"], 2 * c + 1)
                act.wait_ge(S["unit_done"], 4 * q + j + 1)
                for t in range(TT):
                    A((gate_a, gate_b)[c // 2][:, t, 512 * (c % 2):512 * (c % 2) + 512],
                      PS[:, 4 + 2 * (c % 2) + t, :], ACT.Sigmoid).then_inc(S["gate_read"], 1)
                split(q + 1, j)

            plain_splits(FIRST["mod4"], 4)

            def probT(n):
                act.wait_ge(S["s_tr"], n + 1)
                wait(act, S["s_o"], n - 1)
                A(pTb[n % 2][:, :], PS[:, 2 + n % 2, 0:384], ACT.Copy).then_inc(S["s_pT"], 1)

            def ya_high(p):
                act.wait_ge(S["s_o"], 2 * p + 2)
                A(yaTh[:, p, :], PS[:, 4 + p % 2, 0:T], ACT.Copy).then_inc(S["ya_hi"], 1)

            for n in range(H_A):
                act.wait_ge(S["s_max"], n + 1)
                wait(act, S["s_tr"], n - 1)
                for c, (a, b) in enumerate(((0, P), (P, 384))):
                    A(prob[n % 2][:, a:b], PS[:, n % 2, a:b], ACT.Exp, bias=nmx[:, 2 * n + c:2 * n + c + 1],
                      accum_out=sums[:, 2 * n + c:2 * n + c + 1]).then_inc(S["s_exp"], 1)
                if n >= 1:
                    probT(n - 1)
                if n % 2 == 1 and n >= 3:
                    ya_high((n - 3) // 2)
            probT(H_A - 1)
            ya_high(3)

            for n in range(4):
                A(rn[:, 2 * n:2 * n + 2, :], qkvT[:, 2 * n:2 * n + 2, :], ACT.Square).then_inc(S["l2_sq"], 1)
            act.wait_ge(S["gcum_read"], 1)
            A(ecum, ncum, ACT.Exp, scale=-1.0).then_inc(S["gexp"], 1)
            for t in range(TT):
                act.wait_ge(S["dec_arg"], t + 1)
                d = LT[:, 4 * t:4 * t + 4, :]
                A(d, d, ACT.Exp).then_inc(S["dec_exp"], 1)
            for t in range(TT):
                act.wait_ge(S["n_tr"], t + 1)
                A(NT[:, 4 * t:4 * t + 4, :], tr_bank(0, 6 + t), ACT.Copy).then_inc(S["n_read"], 1)
            for m in range(1, 7):
                for t in range(TT):
                    act.wait_ge(S["u_mm"], 2 * m + t - 1)
                    if m >= 2:
                        act.wait_ge(S["vt_mm"], 2 * (m - 1) + t - 1)
                    A(Ub[:, 4 * t:4 * t + 4, :], tr_bank(0, t), ACT.Copy).then_inc(S["u_read"], 1)
            for n, dst, b in ((1, vn0, 6), (2, S1, 7), (3, R, 2)):
                act.wait_ge(S["vn_mm"], n)
                A(dst[:, :, :], tr_bank(0, b), ACT.Copy).then_inc(S["vn_sb"], 1)
            for t in range(TT):
                act.wait_ge(S["o_mm"], t + 1)
                A(ob[:, t, :], PS[:, 3 + t, :], ACT.Copy).then_inc(S["o_part"], 1)
            for t in range(TT):
                act.wait_ge(S["yb_tr"], t + 1)
                A(ybTh[:, :, t * P:(t + 1) * P], tr_bank(0, 5 + t), ACT.Copy).then_inc(S["yb_hi"], 1)
            plain_splits(FIRST["up_a"], 4)
            to_T(5)
            plain_splits(FIRST["wout2"], 4)
            rms(1)
            to_T(6, 0)
            plain_splits(FIRST["mod5"], 4)

            act.wait_ge(S["rt_max"], 1)
            for t in range(TT):
                A(route[:, 1, t, 0:4], lg[:, t, 0:4], ACT.Exp, bias=rsc[:, 2 + t:3 + t], accum_out=rsc[:, 4 + t:5 + t]
                  ).then_inc(S["rt_exp"], 1)
            act.wait_ge(S["rt_max"], 2)
            A(rsc[:, 10:12], rsc[:, 10:12], ACT.Exp).then_inc(S["rt_exp"], 1)
            act.wait_ge(S["small_mm"], 7 + 1)
            A(combT[:, :], PS[0:32, 1, 0:T], ACT.Copy).then_inc(S["cbT_sb"], 1)

            b = FIRST["moe"]

            def gate_silu(q, s, e, n):
                act.wait_ge(S["unit_done"], 4 * q + s + 1)
                wait(act, S["gu_done"], e - 1)
                A(gbuf[n % 2][:, :], PS[:, n % 2, :], ACT.Silu).then_inc(S["g_silu"], 1)

            def expert_high(e, n):
                act.wait_ge(S["ga_done"], e + 1)
                A(eTh[n % 2][:, :, :], ubuf[n % 2][:, :].rearrange("p (c t) -> p c t", c=2), ACT.Copy
                  ).then_inc(S["act_hi"], 1)

            def experts(i, n0, k):
                for n in range(n0, n0 + k):
                    g, u, d = (unit(b, 3 * n + m, i, 12) for m in (-1, 0, 1))
                    gate_silu(*g, 4 * i + n, n)
                    split(g[0] + 1, g[1])
                    split(u[0] + 1, u[1])
                    expert_high(4 * i + n, n)
                    split(d[0] + 1, d[1])

            g, u = unit(b, 0), unit(b, 1)
            gate_silu(*g, 0, 0)
            split(g[0] + 1, g[1])
            split(u[0] + 1, u[1])
            expert_high(0, 0)
            experts(0, 1, 4)
            with act.Fori(1, 7) as i:
                experts(i, 1, 4)
            experts(7, 1, 3)
            rms(2)

        @block.tensor
        def _(pe):
            mm = pe.matmul

            def product(out, a, b, start, stop):
                mm(out, a[0], b[0], start=start, stop=False)
                mm(out, a[0], b[1], start=False, stop=False)
                return mm(out, a[1], b[0], start=False, stop=stop)

            def unit_T(q, j, xT, outs):
                pe.wait_ge(S["w_lo_done"], 4 * q + j + 1)
                w = [t[:, :].rearrange("p (k f) -> p k f", k=KD) for t in (hi[j], lo[j])]
                for c in range(2):
                    for k in range(KD):
                        last = product(outs[c], [t[:, k, c * P:(c + 1) * P] for t in w],
                                       [f(k) for f in xT], k == 0, k == KD - 1)
                last.then_inc(S["unit_done"], 1)

            def unit_N(q, j, xT, k0, ks, outs, start, stop):
                pe.wait_ge(S["w_lo_done"], 4 * q + j + 1)
                w = [t[:, :].rearrange("p (k f) -> p k f", k=ks) for t in (hi[j], lo[j])]
                for t in range(TT):
                    for c in range(4 // ks):
                        for k in range(ks):
                            last = product(outs[c][t], [f(k0 + k)[:, t * P:(t + 1) * P] for f in xT],
                                           [s[:, k, 512 * c:512 * c + 512] for s in w],
                                           start and k == 0, stop and k == ks - 1)
                last.then_inc(S["unit_done"], 1)

            def to_T(r, source, ready, value, banks=4, per=1):
                for n in range(4):
                    t, k = n // 2, 4 * (n % 2)
                    if k == 0:
                        pe.wait_ge(S[ready], value + per * t)
                    for c in range(4):
                        last = pe.transpose(tr_bank(n, banks + n)[:, c, :], source[:, t, (k + c) * P:(k + c + 1) * P],
                                            ident)
                    last.then_inc(S["tr_done"], 1)
                pe.wait_ge(S["tr_lo"], 4 * r + 4)

            def tiles(*parts):
                return [lambda k, s=s: s[:, k, :] for s in parts]

            hT = tiles(hTh, hTl)
            pe.wait_ge(S["const_in"], 64)
            to_T(0, h, "x_in", 16, per=0)

            def small_product(outs, c0, n):
                for t in range(TT):
                    for k in range(KD):
                        last = product(outs[t], [f(k)[:, t * P:(t + 1) * P] for f in hT],
                                       [s[:, k, c0:c0 + n] for s in (wsh, wsl)], k == 0, k == KD - 1)
                return last

            pe.wait_ge(S["small_lo_done"], 1)
            small_product([PS[:, 4, 0:32], PS[:, 4, 32:64]], 0, 32).then_inc(S["small_mm"], 1)

            def in_unit(q, j):
                unit_T(q, j, hT, [PS[:, j, c * T:(c + 1) * T] for c in range(2)])

            for j in range(RING):
                in_unit(0, j)
            with pe.Fori(1, 5) as i:
                for j in range(RING):
                    pe.wait_ge(S["conv_done"], 4 * i + j - 3)
                    in_unit(i, j)
            for j in range(RING):
                pe.wait_ge(S["z_done"], j + 1)
                in_unit(5, j)

            da = da_all.rearrange("p (t n) -> p t n", t=TT)
            pe.wait_ge(S["da_done"], 1)
            mm(PS[:, 5, 0:32], triu, da[:, 0, :], start=True, stop=True)
            mm(PS[:, 5, 32:64], ones, da[:, 0, :], start=True, stop=False)
            mm(PS[:, 5, 32:64], triu, da[:, 1, :], start=False, stop=True).then_inc(S["small_mm"], 1)
            pe.wait_ge(S["cs_read"], 1)

            pe.wait_ge(S["silu_done"], 16)
            for n in range(8):
                wait(pe, S["x_read"], n - 3)
                t, k = n // 4, 4 * (n % 4)
                for c in range(4):
                    last = pe.transpose(tr_bank(n, 4 + n % 4)[:, c, :], xbcT[:, k + c, t * P:(t + 1) * P], ident)
                last.then_inc(S["xtr_done"], 1)
            pe.wait_ge(S["x_read"], 8)
            pe.wait_ge(S["z_done"], 8)

            def scores(g):
                wait(pe, S["cb_read"], g - 1)
                b, c = xbcT[:, 16 + g, :], xbcT[:, 24 + g, :]
                mm(PS[:, g % 2, 0:256], b[:, 0:P], c, start=True, stop=True)
                mm(PS[:, g % 2, 256:384], b[:, P:T], c[:, P:T], start=True, stop=True).then_inc(S["cb_mm"], 1)

            def running(hp):
                wait(pe, S["d_read"], hp - 1)
                for c in range(2):
                    o, n = PS[:, 2 + hp % 2, c * T:(c + 1) * T], 2 * hp + c
                    mm(o, da[:, 0, n:n + 1].to_broadcast([P, P]), triu_ones, start=True, stop=False)
                    last = mm(o[:, P:T], da[:, 1, n:n + 1].to_broadcast([P, P]), triu, start=False, stop=True)
                last.then_inc(S["csb_done"], 1)

            def head_y(hp):
                pe.wait_ge(S["m_ready"], hp + 1)
                wait(pe, S["y_read"], hp - 1)
                for c in range(2):
                    o, n, m = PS[64 * c:64 * c + 64, 4 + hp % 2, 0:T], 2 * hp + c, dec[hp % 3][:, c, :]
                    mm(o, X[:, 0, 64 * n:64 * n + 64], m[:, 0:T], start=True, stop=False)
                    last = mm(o[:, P:T], X[:, 1, 64 * n:64 * n + 64], m[:, T:T + P], start=False, stop=True)
                last.then_inc(S["y_done"], 1)

            def group_sums(g):
                pe.wait_ge(S["sq_done"], g + 1)
                wait(pe, S["yn_done"], 2 * g - 2)
                for t in range(TT):
                    for c in range(2):
                        last = mm(PS[:, 6 + g % 2, t:t + 1], ysq[g % 2][:, c, t * P:(t + 1) * P], ones[:, 0:1],
                                  start=c == 0, stop=c == 1)
                last.then_inc(S["ms_done"], 1)

            def group_scale(g):
                pe.wait_ge(S["y_rstd"], g + 1)
                for t in range(TT):
                    last = mm(PS[:, 6 + g % 2, T + t * P:T + (t + 1) * P],
                              yrs[:, 2 * g + t:2 * g + t + 1].to_broadcast([P, P]), ident, start=True, stop=True)
                last.then_inc(S["ms_wide"], 1)

            scores(0)
            running(0)
            for hp in range(PAIRS):
                if hp % 2 == 1 and hp < PAIRS - 1:
                    scores((hp + 1) // 2)
                if hp < PAIRS - 1:
                    running(hp + 1)
                head_y(hp)
                if hp % 2 == 1 and hp >= 5:
                    group_sums((hp - 5) // 2)
                if hp % 2 == 0 and hp >= 6:
                    group_scale((hp - 6) // 2)

            def out_unit(n):
                pe.wait_ge(S["ylo"], 4 * (n % 4) + 4)
                q, j = unit(FIRST["out"], n)
                unit_N(q, j, [lambda k: yTh[:, k % 2, k // 2, :], lambda k: yTl[:, k, :]], 4 * (n % 4), 4,
                       [[PS[:, 2 * (n // 4) + t, :] for t in range(TT)]], n % 4 == 0, n % 4 == 3)

            group_scale(GROUPS - 3)
            group_sums(GROUPS - 2)
            pe.wait_ge(S["cb_read"], GROUPS)
            out_unit(0)
            group_scale(GROUPS - 2)
            group_sums(GROUPS - 1)
            out_unit(1)
            group_scale(GROUPS - 1)
            for n in range(2, 8):
                out_unit(n)

            def mod_units(k, bank):
                for n in range(4):
                    q, j = unit(FIRST[f"mod{k}"], n)
                    pe.wait_ge(S["w_lo_done"], 4 * q + j + 1)
                    for s in range(4):
                        a = [c[:, 4 * (n % 2) + s:4 * (n % 2) + s + 1].to_broadcast([P, P]) for c in (c_hi, c_lo)]
                        last = product(PS[:, bank + n // 2, :], a, [w[:, 512 * s:512 * s + 512] for w in (hi[j], lo[j])],
                                       n % 2 == 0 and s == 0, n % 2 == 1 and s == 3)
                    last.then_inc(S["unit_done"], 1)

            pe.wait_ge(S["c_ready"], 3)
            pe.wait_ge(S["yn_done"], XT_TILES)
            mod_units(0, 4)

            def mlp(m, first):
                outs = [[PS[:, 4 + 2 * c + t, :] for t in range(TT)] for c in range(2)]

                def up(q, s, n):
                    unit_T(q, s, hT, [PS[:, n % 4, c * T:(c + 1) * T] for c in range(2)])

                def down(q, s, n, start=False, stop=False):
                    unit_N(q, s, tiles(aTh[n % 2], aTl[n % 2]), 0, 2, outs, start, stop)

                def round_of(i, n, k):
                    for e in range(n, n + k):
                        if not (isinstance(i, int) and 4 * i + e < 4):
                            pe.wait_ge(S["relu_done"], CHUNKS * m + 4 * i + e - 3)
                        up(*unit(first, 2 * e - 1, i, 8), e)
                        if isinstance(i, int) and 4 * i + e == 1:
                            pe.wait_ge(S["mod_read"], 2 if m == 0 else 6)
                        pe.wait_ge(S["act_lo"], CHUNKS * m + 4 * i + e)
                        down(*unit(first, 2 * e, i, 8), e - 1, isinstance(i, int) and 4 * i + e == 1)

                up(*unit(first, 0), 0)
                round_of(0, 1, 4)
                with pe.Fori(1, 3) as i:
                    round_of(i, 1, 4)
                round_of(3, 1, 3)
                pe.wait_ge(S["act_lo"], CHUNKS * m + CHUNKS)
                down(*unit(first, 31), 15, False, True)

            to_T(1, h, "h_ready", 1, 0)
            mlp(0, FIRST["mlp0"])
            pe.wait_ge(S["relu_done"], CHUNKS)
            mod_units(1, 2)
            to_T(2, h, "h_ready", 3)

            for n in range(8):
                wait(pe, S["kq_read"], n - 3)
                if n == 2:
                    pe.wait_ge(S["mod_read"], 4)
                unit_T(*unit(FIRST["k"], n), hT, [PS[:, n % 4, c * T:(c + 1) * T] for c in range(2)])
            for n in range(4):
                unit_N(*unit(FIRST["v"], n), hT, 4 * (n % 2), 4,
                       [[PS[:, 4 + 2 * (n // 2) + t, :] for t in range(TT)]], n % 2 == 0, n % 2 == 1)

            def sb_scores(p):
                wait(pe, S["sb_zl"], p - 1)
                for c in range(2):
                    k, r, o = kT[64 * c:64 * c + 64, p, :], qT[64 * c:64 * c + 64, p, :], PS[:, 2 * (p % 2) + c, :]
                    mm(o[:, 0:T], k[:, 0:P], r, start=True, stop=True)
                    last = mm(o[:, T:T + P], k[:, P:T], r[:, P:T], start=True, stop=True)
                last.then_inc(S["sb_z"], 1)

            def sb_sums(p):
                pe.wait_ge(S["sb_mask"], p + 1)
                wait(pe, S["sb_lw"], p)
                for c in range(2):
                    o, n = PS[:, 4 + c, :], nbuf[p % 2][:, c, :]
                    mm(o[:, 0:T], later, n[:, 0:T], start=True, stop=False)
                    mm(o[:, P:T], ones, n[:, T:T + P], start=False, stop=True)
                    last = mm(o[:, T:T + P], later, n[:, T:T + P], start=True, stop=True)
                last.then_inc(S["sb_after"], 1)

            def sb_values(p):
                pe.wait_ge(S["sb_wm"], p + 1)
                wait(pe, S["oT_lo_done"], p - 1)
                for c in range(2):
                    o, n, w = PS[64 * c:64 * c + 64, 6 + p % 2, 0:T], 64 * (2 * p + c), wbuf[p % 2][:, c, :]
                    mm(o, V[:, 0, n:n + 64], w[:, 0:T], start=True, stop=False)
                    last = mm(o[:, P:T], V[:, 1, n:n + 64], w[:, T:T + P], start=False, stop=True)
                last.then_inc(S["sb_o"], 1)

            pe.wait_ge(S["kq_read"], 8)
            pe.wait_ge(S["v_read"], 4)
            sb_scores(0)
            for p in range(SB_PAIRS):
                if p < SB_PAIRS - 1:
                    sb_scores(p + 1)
                sb_sums(p)
                if p >= 1:
                    sb_values(p - 1)
            sb_values(SB_PAIRS - 1)
            for n in range(4):
                pe.wait_ge(S["oT_lo_done"], 4 * (n % 2) + 4)
                unit_N(*unit(FIRST["o"], n), tiles(oTh, oTl), 4 * (n % 2), 4,
                       [[PS[:, 2 * (n // 2) + t, :] for t in range(TT)]], n % 2 == 0, n % 2 == 1)

            mod_units(2, 4)
            to_T(3, h, "h_ready", 5, 0)
            mlp(1, FIRST["mlp1"])
            pe.wait_ge(S["relu_done"], 2 * CHUNKS)
            mod_units(3, 0)

            to_T(4, hn, "hn_ready", 1)
            pe.wait_ge(S["mod_read"], 8)
            small_product([PS[:, 6, 0:8], PS[:, 6, 8:16]], 32, 8).then_inc(S["small_mm"], 1)
            pe.wait_ge(S["tab_in"], 32)
            pe.wait_ge(S["pool_init"], 1 + 1)
            mm(PS[0:H_A, 7, 0:TABLE_W], relb[:, :], tabs[:, 0:TABLE_W], start=True, stop=True
               ).then_inc(S["small_mm"], 1)
            for n in range(4):
                unit_T(*unit(FIRST["qa"], n), hT, [PS[:, n, c * T:(c + 1) * T] for c in range(2)])
            for n in range(2):
                unit_N(*unit(FIRST["va"], n), hT, 4 * n, 4, [[PS[:, 4 + t, :] for t in range(TT)]], n == 0, n == 1)
            for n in range(6):
                pe.wait_ge(*(S["qk_read"], n + 1) if n < 4 else (S["conv_done"], 16 + n - 3))
                unit_T(*unit(FIRST["conv2"], n), hT, [PS[:, n % 4, c * T:(c + 1) * T] for c in range(2)])
            pe.wait_ge(S["ba_read"], 1)
            pe.wait_ge(S["tab_sb"], 1)
            for n in range(2):
                unit_N(*unit(FIRST["zb"], n), hT, 4 * n, 4, [[PS[:, 6 + t, :] for t in range(TT)]], n == 0, n == 1)
            for n in range(8):
                c = n // 2
                if n % 2 == 0:
                    pe.wait_ge(*((S["v_read"], 4 + 2), (S["z_done"], 8 + 2), (S["gate_read"], 2), (S["gate_read"], 4))[c])
                unit_N(*unit(FIRST["gate"], n), hT, 4 * (n % 2), 4,
                       [[PS[:, 4 + 2 * (c % 2) + t, :] for t in range(TT)]], n % 2 == 0, n % 2 == 1)

            def s_scores(n):
                p, r = n // 2, slice(64 * (n % 2), 64 * (n % 2) + 64)
                wait(pe, S["s_exp"], 2 * n - 2)
                s = PS[:, n % 2, :]
                mm(s[:, 0:P], qaT[r, p, 0:P], kaT[r, p, 0:P], start=True, stop=False)
                mm(s[:, 0:P], anti, hank[:, n, 0:P], start=False, stop=True)
                mm(s[:, P:384], qaT[r, p, P:T], kaT[r, p, :], start=True, stop=False)
                mm(s[:, P:384], anti, hank[:, n, P:384], start=False, stop=True).then_inc(S["s_mm"], 1)

            def s_probT(n):
                pe.wait_ge(S["s_norm"], n + 1)
                wait(pe, S["s_pT"], n - 1)
                for c in range(3):
                    last = pe.transpose(tr_bank(0, 2 + n % 2)[:, c, :], prob[n % 2][:, c * P:(c + 1) * P], ident)
                last.then_inc(S["s_tr"], 1)

            def s_values(n):
                p = n // 2
                pe.wait_ge(S["s_pT"], n + 1)
                wait(pe, S["ya_lo"], p - 1)
                o, f = PS[64 * (n % 2):64 * (n % 2) + 64, 4 + p % 2, 0:T], slice(64 * n, 64 * n + 64)
                mm(o, va[:, 0, f], pTb[n % 2][:, 0:T], start=True, stop=False)
                mm(o[:, P:T], va[:, 1, f], pTb[n % 2][:, T:384], start=False, stop=True).then_inc(S["s_o"], 1)

            pe.wait_ge(S["conv_done"], 16 + 6)
            mod_units(4, 2)
            pe.wait_ge(S["mod_read"], 10)
            pe.wait_ge(S["gate_read"], 8)
            pe.wait_ge(S["conv_done"], 16 + 6)
            pe.wait_ge(S["hank_in"], 32)
            s_scores(0)
            for n in range(H_A):
                if n < H_A - 1:
                    s_scores(n + 1)
                s_probT(n)
                if n >= 1:
                    s_values(n - 1)
            s_values(H_A - 1)

            for n in range(8):
                pe.wait_ge(S["l2_sq"], n // 2 + 1)
                for t in range(TT):
                    last = mm(PS[:, 0, 2 * n + t:2 * n + t + 1], rn[:, n, t * P:(t + 1) * P], ones[:, 0:1],
                              start=True, stop=True)
            last.then_inc(S["small_mm"], 1)
            pe.wait_ge(S["g_done"], 1)
            pe.wait_ge(S["ya_lo"], 4)
            for t in range(TT):
                last = mm(PS[:, 1, 4 * t:4 * t + 4], triu, gdec[:, 4 * t:4 * t + 4], start=True, stop=True)
            last.then_inc(S["small_mm"], 1)
            for t in range(TT):
                for n in range(H_B):
                    last = mm(PS[:, 4 + t, n * P:(n + 1) * P], gdec[:, 4 * t + n:4 * t + n + 1].to_broadcast([P, P]),
                              triu, start=True, stop=True)
                last.then_inc(S["gb_mm"], 1)
            pe.wait_ge(S["l2_rstd"], 1)
            pe.wait_ge(S["gcum_read"], 1)
            for n in range(8):
                b = (0, 1, 2, 3)[n // 2]
                for t in range(TT):
                    last = mm(PS[:, b, (n % 2) * T + t * P:(n % 2) * T + (t + 1) * P],
                              l2r[:, 2 * n + t:2 * n + t + 1].to_broadcast([P, P]), ident, start=True, stop=True)
                if n % 2 == 1:
                    last.then_inc(S["l2_bc"], 1)
            pe.wait_ge(S["l2_done"], 4)

            def tile(n, t):
                return qkvT[:, n, t * P:(t + 1) * P]

            for t in range(TT):
                for n in range(H_B):
                    last = mm(tr_bank(0, t)[:, n, :], tile(4 + n, t), tile(4 + n, t), start=True, stop=True)
                last.then_inc(S["kk_mm"], 1)
            for t in range(TT):
                for n in range(H_B):
                    last = mm(tr_bank(0, 2 + t)[:, n, :], tile(4 + n, t), tile(n, t), start=True, stop=True)
                last.then_inc(S["qk_mm"], 1)
            pe.wait_ge(S["silu_done"], 16 + 6)
            for b, n0, t in ((6, 8, 0), (7, 8, 1), (0, 4, 0)):
                if b == 0:
                    pe.wait_ge(S["kk_read"], 1)
                for n in range(H_B):
                    last = pe.transpose(tr_bank(0, b)[:, n, :], tile(n0 + n, t), ident)
                last.then_inc(S["vk_tr"], 1)
            for t in range(TT):
                pe.wait_ge(S["kk_masked"], t + 1)
                for n in range(H_B):
                    last = pe.transpose(tr_bank(0, 4 + t)[:, n, :], Ub[:, 4 * t + n, :], ident)
                last.then_inc(S["m_tr"], 1)
            pe.wait_ge(S["vk_read"], 3)
            for t in range(TT):
                pe.wait_ge(S["m_read"], t + 1)
                for n in range(H_B):
                    last = pe.transpose(tr_bank(0, 6 + t)[:, n, :], Xi[:, 4 * t + n, :], ident)
                last.then_inc(S["n_tr"], 1)

            def four(b, t, lhsT, rhs):
                for n in range(H_B):
                    last = mm(tr_bank(0, b)[:, n, :], lhsT(4 * t + n), rhs(4 * t + n), start=True, stop=True)
                return last

            for m in range(1, 7):
                for t in range(TT):
                    pe.wait_ge(S["lt_done"], 2 * m + t - 1)
                    pe.wait_ge(S["x_upd"], 2 * m + t - 1)
                    four(t, t, lambda n: LT[:, n, :], lambda n: Xi[:, n, :]).then_inc(S["u_mm"], 1)
                for t in range(TT):
                    pe.wait_ge(S["u_read"], 2 * m + t - 1)
                    if m < 6:
                        four(2 + t, t, lambda n: XiT[:, n, :], lambda n: Ub[:, n, :])
                    four(4 + t, t, lambda n: Ub[:, n, :], lambda n: XiT[:, n, :]).then_inc(S["vt_mm"], 1)
            pe.wait_ge(S["x_upd"], 14)
            four(6, 0, lambda n: XiT[:, n, :], lambda n: R[:, n, :]).then_inc(S["vn_mm"], 1)
            pe.wait_ge(S["vn_sb"], 1)
            four(7, 0, lambda n: kd[:, n, :], lambda n: vn0[:, n, :]).then_inc(S["vn_mm"], 1)
            pe.wait_ge(S["vn_sb"], 2)
            four(0, 0, lambda n: tile(4 + n, 1), lambda n: S1[:, n, :]).then_inc(S["ks_mm"], 1)
            four(1, 0, lambda n: tile(n, 1), lambda n: S1[:, n, :]).then_inc(S["ks_mm"], 1)
            four(3, 0, lambda n: PT[:, n, :], lambda n: vn0[:, n, :]).then_inc(S["o_mm"], 1)
            pe.wait_ge(S["r1_done"], 1)
            four(2, 1, lambda n: XiT[:, n, :], lambda n: R[:, n - 4, :]).then_inc(S["vn_mm"], 1)
            pe.wait_ge(S["vn_sb"], 3)
            four(4, 1, lambda n: PT[:, n, :], lambda n: R[:, n - 4, :]).then_inc(S["o_mm"], 1)
            pe.wait_ge(S["o_scaled"], 1)
            for t in range(TT):
                for n in range(H_B):
                    last = pe.transpose(tr_bank(0, 5 + t)[:, n, :], ob[:, t, n * P:(n + 1) * P], ident)
                last.then_inc(S["yb_tr"], 1)
            pe.wait_ge(S["yb_lo"], 2)
            for n in range(4):
                unit_N(*unit(FIRST["up_a"], n), (tiles(yaTh, yaTl), tiles(ybTh, ybTl))[n // 2], 0, 4,
                       [[PS[:, 4 * (n // 2) + 2 * (n % 2) + t, :] for t in range(TT)]], True, True)
            to_T(5, mm_a, "mix_ready", 2, per=0)
            for n in range(4):
                unit_N(*unit(FIRST["wout2"], n), hT, 4 * (n % 2), 4,
                       [[PS[:, 2 * (n // 2) + t, :] for t in range(TT)]], n % 2 == 0, n % 2 == 1)
            mod_units(5, 4)
            to_T(6, hn, "hn_ready", 3, 0)
            small_product([PS[:, 0, 0:36], PS[:, 0, 64:100]], 40, 36).then_inc(S["small_mm"], 1)
            pe.wait_ge(S["rt_done"], 1)
            for t in range(TT):
                last = pe.transpose(PS[0:32, 1, t * P:(t + 1) * P], comb[:, t, :], ident)
            last.then_inc(S["small_mm"], 1)

            b = FIRST["moe"]
            outs = [[PS[:, 4 + 2 * c + t, :] for t in range(TT)] for c in range(2)]

            def gate_up(g, u, e, n):
                wait(pe, S["g_silu"], e - 1)
                unit_T(*g, hT, [PS[:, n % 2, c * T:(c + 1) * T] for c in range(2)])
                wait(pe, S["gu_done"], e - 1)
                unit_T(*u, hT, [PS[:, 2 + n % 2, c * T:(c + 1) * T] for c in range(2)])

            def down(q, s, n, start=False, stop=False):
                unit_N(q, s, tiles(eTh[n % 2], eTl[n % 2]), 0, 2, outs, start, stop)

            def experts(i, n0, k):
                for n in range(n0, n0 + k):
                    g, u, d = (unit(b, 3 * n + m, i, 12) for m in (-1, 0, 1))
                    gate_up(g, u, 4 * i + n, n)
                    pe.wait_ge(S["act_lo"], 32 + 4 * i + n)
                    if isinstance(i, int) and 4 * i + n == 1:
                        pe.wait_ge(S["mod_read"], 12)
                    down(*d, n - 1, isinstance(i, int) and 4 * i + n == 1)

            pe.wait_ge(S["cbT_sb"], 1)
            gate_up(unit(b, 0), unit(b, 1), 0, 0)
            experts(0, 1, 4)
            with pe.Fori(1, 7) as i:
                experts(i, 1, 4)
            experts(7, 1, 3)
            pe.wait_ge(S["act_lo"], 32 + EXPERTS)
            down(*unit(b, 95), EXPERTS - 1, False, True)

        @block.vector
        def _(dve):
            tt, ts, stt = dve.tensor_tensor, dve.tensor_scalar, dve.scalar_tensor_tensor
            step = Steps(dve, S["dve_step"])

            def split(q, j):
                if isinstance(q, int) and 4 * q + j >= UNITS:
                    return
                dve.wait_ge(S["w_hi_done"], 4 * q + j + 1)
                tt(lo[j][:, :], raw[j][:, :], hi[j][:, :].bitcast(F32), ALU.subtract).then_inc(S["w_lo_done"], 1)

            def to_T(r, banks=4):
                for n in range(4):
                    dve.wait_ge(S["tr_hi"], 4 * r + n + 1)
                    a = (slice(None), slice(4 * (n % 2), 4 * (n % 2) + 4), slice(n // 2 * P, (n // 2 + 1) * P))
                    tt(hTl[a], tr_bank(n, banks + n), hTh[a].bitcast(F32), ALU.subtract).then_inc(S["tr_lo"], 1)

            def softplus(out, n, s, before=0):
                dve.wait_ge(s, before + 1)
                step(ts(su[:, 0:n], st[:, 0:n], 1.0, None, ALU.add))
                step(ts(sv[:, 0:n], su[:, 0:n], -1.0, None, ALU.add))
                step(tt(sv[:, 0:n], st[:, 0:n], sv[:, 0:n], ALU.subtract))
                step(dve.reciprocal(su[:, 0:n], su[:, 0:n]))
                step(tt(sv[:, 0:n], sv[:, 0:n], su[:, 0:n], ALU.mult))
                dve.wait_ge(s, before + 2)
                step(tt(sv[:, 0:n], sv[:, 0:n], sw[:, 0:n], ALU.add))
                step(stt(out, sx[:, 0:n], 0.0, sv[:, 0:n], ALU.max, ALU.add))

            dve.wait_ge(S["small_hi_done"], 1)
            tt(small_lo[:, :], small_raw[:, :], small_hi[:, :].bitcast(F32), ALU.subtract
               ).then_inc(S["small_lo_done"], 1)
            for j in range(RING):
                split(0, j)
            to_T(0)
            dve.wait_ge(S["c_ready"], 2)
            tt(c_lo[:, :], cc["c"], c_hi[:, :].bitcast(F32), ALU.subtract).then_inc(S["c_ready"], 1)

            dve.wait_ge(S["small_mm"], 1)
            tt(sx.rearrange("p (t n) -> p t n", t=TT), PS[:, 4, 0:64].rearrange("p (t n) -> p t n", t=TT),
               rr["dt_bias"].rearrange("p (o n) -> p o n", o=1).to_broadcast([P, TT, 32]), ALU.add
               ).then_inc(S["dt_read"], 1)
            softplus(dt_all, 64, S["dt_exp"])
            stt(da_all.rearrange("p (t n) -> p t n", t=TT), dt_all.rearrange("p (t n) -> p t n", t=TT), -1.0,
                rr["a_log"].rearrange("p (o n) -> p o n", o=1).to_broadcast([P, TT, 32]), ALU.mult, ALU.mult
                ).then_inc(S["da_done"], 1)

            with dve.Fori(0, 4) as i:
                for j in range(RING):
                    dve.wait_ge(S["conv_first"], 8 * i + 2 * j + 2)
                    for c in range(2):
                        ct = 8 * i + 2 * j + c
                        for b in range(1, 4):
                            a = acc[j % 2][:, c, b:T]
                            last = stt(a, PS[:, j, c * T:(c + 1) * T - b], cc["conv_w"][:, bass.ds(4 * ct + 3 - b, 1)],
                                       a, ALU.mult, ALU.add)
                            if not (c == 1 and b == 3):
                                last.then_inc(S["conv_tap"], 1)
                                dve.wait_ge(S["conv_tap"], 20 * i + 5 * j + 3 * c + b)
                    last.then_inc(S["conv_done"], 1)
                    split(i + 1, j)
            for i in range(4, 6):
                for j in range(RING):
                    split(i + 1, j)

            dve.wait_ge(S["small_mm"], 1 + 1)
            ts(ncs, PS[:, 5, 0:64], -1.0, None, ALU.mult).then_inc(S["cs_read"], 1)
            for n in range(8):
                t, k = n // 4, 4 * (n % 4)
                dve.wait_ge(S["xtr_done"], n + 1)
                tt(X[:, t, k * P:(k + 4) * P].rearrange("p (n d) -> p n d", d=64),
                   PS[:, 4 + n % 4, :].rearrange("p (n d) -> p n d", d=64),
                   dt_all[:, 32 * t + 2 * k:32 * t + 2 * k + 8].rearrange("p (n o) -> p n o", o=1
                                                                         ).to_broadcast([P, 8, 64]),
                   ALU.mult).then_inc(S["x_read"], 1)

            def decay_arg(hp):
                dve.wait_ge(S["csb_done"], hp + 1)
                wait(dve, S["y_done"], hp - 2)
                for c in range(2):
                    n, o = 2 * hp + c, PS[:, 2 + hp % 2, c * T:(c + 1) * T]
                    stt(dec[hp % 3][:, c, 0:T], o, ncs[:, n:n + 1], mask_neg, ALU.add, ALU.add)
                    last = stt(dec[hp % 3][:, c, T:T + P], o[:, P:T], ncs[:, 32 + n:33 + n], mask_neg[:, 0:P],
                               ALU.add, ALU.add)
                last.then_inc(S["d_read"], 1)

            def skip(hp):
                dve.wait_ge(S["y_done"], hp + 1)
                wait(dve, S["yg_done"], hp - 1)
                stt(ysk[hp % 2][:, :], xbcT[:, hp, :], cc["skip"][:, hp:hp + 1], PS[:, 4 + hp % 2, 0:T], ALU.mult,
                    ALU.add).then_inc(S["y_read"], 1)

            def mean_square(g):
                dve.wait_ge(S["ms_done"], g + 1)
                ts(yrs[:, 2 * g:2 * g + 2], PS[:, 6 + g % 2, 0:2], 1.0 / 256, RMS_EPS, ALU.mult, ALU.add
                   ).then_inc(S["ms_read"], 1)

            def y_norm(g):
                dve.wait_ge(S["ms_wide"], g + 1)
                for c in range(2):
                    ct = 2 * g + c
                    stt(zT[:, ct, :], zT[:, ct, :], cc["norm_w"][:, ct:ct + 1], PS[:, 6 + g % 2, T:2 * T], ALU.mult,
                        ALU.mult).then_inc(S["yn_done"], 1)

            def y_low(g):
                for c in range(2):
                    dve.wait_ge(S["yhi"], 2 * g + c + 1)
                    tt(yTl[:, 2 * g + c, :], zT[:, 2 * g + c, :], yTh[:, c, g, :].bitcast(F32), ALU.subtract
                       ).then_inc(S["ylo"], 1)

            decay_arg(0)
            for hp in range(PAIRS):
                if hp < PAIRS - 1:
                    decay_arg(hp + 1)
                skip(hp)
                if hp % 2 == 1 and hp >= 5:
                    mean_square((hp - 5) // 2)
                if hp % 2 == 0 and hp >= 6:
                    y_norm((hp - 6) // 2)
                if hp % 2 == 1 and hp >= 9:
                    y_low((hp - 9) // 2)
            y_norm(GROUPS - 3)
            y_low(GROUPS - 4)
            mean_square(GROUPS - 2)
            y_low(GROUPS - 3)
            y_norm(GROUPS - 2)
            mean_square(GROUPS - 1)
            y_low(GROUPS - 2)
            y_norm(GROUPS - 1)
            y_low(GROUPS - 1)

            def plain_splits(first, count):
                for p in range(count):
                    q, j = unit(first, p)
                    split(q + 1, j)

            def layer_norm(r, last_unit, banks):
                dve.wait_ge(S["unit_done"], last_unit)
                for t in range(TT):
                    for c in range(2):
                        s = slice(512 * c, 512 * c + 512)
                        step(stt(pre[:, t, s], h[:, t, s], ALPHA, PS[:, banks + 2 * c + t, :], ALU.mult, ALU.add))
                        step(dve.bn_stats(stats[:, t, c, :], pre[:, t, s]))
                    step(dve.bn_aggr(mv[:, t, :], stats[:, t, :, :].rearrange("p c s -> p (c s)")))
                    ts(veps[:, t:t + 1], mv[:, t, 1:2], LN_EPS, None, ALU.add).then_inc(S["ln_var"], 1)
                for t in range(TT):
                    dve.wait_ge(S["ln_rstd"], TT * r + t + 1)
                    stt(nmean[:, t:t + 1], mv[:, t, 0:1], -1.0, rstd[:, t:t + 1], ALU.mult, ALU.mult
                        ).then_inc(S["ln_norm_in"], 1)
                dve.wait_ge(S["row_in"], 16 * r + 16)
                for t in range(TT):
                    dve.wait_ge(S["ln_norm"], TT * r + t + 1)
                    tt(pre[:, t, :], pre[:, t, :], ln_row[:, 0, :], ALU.mult).then_inc(S["ln_gain"], 1)

            def mlp(m, first):
                def square(j, n):
                    dve.wait_ge(S["relu_done"], j + 1)
                    tt(sbuf[n % 2][:, :], rbuf[n % 2][:, :], rbuf[n % 2][:, :], ALU.mult).then_inc(S["sq2_done"], 1)

                def low(j, n):
                    dve.wait_ge(S["act_hi"], j + 1)
                    tt(aTl[n % 2][:, :, :], sbuf[n % 2][:, :].rearrange("p (c t) -> p c t", c=2),
                       aTh[n % 2][:, :, :].bitcast(F32), ALU.subtract).then_inc(S["act_lo"], 1)

                j0 = CHUNKS * m
                square(j0, 0)
                q, s = unit(first, 0)
                split(q + 1, s)
                low(j0, 0)

                def round_of(i, n, k):
                    for e in range(n, n + k):
                        q, s = unit(first, 2 * e - 1, i, 8)
                        square(j0 + e + 4 * i, e)
                        split(q + 1, s)
                        low(j0 + e + 4 * i, e)
                        q, s = unit(first, 2 * e, i, 8)
                        split(q + 1, s)

                with dve.Fori(0, 3) as i:
                    round_of(i, 1, 4)
                round_of(3, 1, 3)
                q, s = unit(first, 31)
                split(q + 1, s)

            def mod_read(k, bank):
                dve.wait_ge(S["mod_in"], 16)
                dve.wait_ge(S["unit_done"], FIRST[f"mod{k}"] + 4)
                for c in range(2):
                    a = mod[:, k, 512 * c:512 * c + 512]
                    tt(a, a, PS[:, bank + c, :], ALU.add).then_inc(S["mod_read"], 1)
                plain_splits(FIRST[f"mod{k}"], 4)

            plain_splits(FIRST["out"], 8)
            layer_norm(0, FIRST["mod0"], 0)
            to_T(1, 0)
            mod_read(0, 4)
            mlp(0, FIRST["mlp0"])
            layer_norm(1, FIRST["mod1"], 4)
            to_T(2)
            mod_read(1, 2)
            plain_splits(FIRST["k"], 12)

            def o_low(p):
                dve.wait_ge(S["oT_hi_done"], p + 1)
                tt(oTl[:, p, :], PS[:, 6 + p % 2, 0:T], oTh[:, p, :].bitcast(F32), ALU.subtract
                   ).then_inc(S["oT_lo_done"], 1)

            for p in range(SB_PAIRS + 1):
                if p < SB_PAIRS:
                    z, n = PS[:, 2 * (p % 2):2 * (p % 2) + 2, 0:384], nbuf[p % 2]
                    dve.wait_ge(S["sb_abs"], p + 1)
                    wait(dve, S["sb_after"], p - 1)
                    stt(n[:, :, :], z, 0.0, abuf[p % 2][:, :, :], ALU.max, ALU.add).then_inc(S["sb_nlo"], 1)
                    dve.wait_ge(S["sb_nlo"], p + 1)
                    wait(dve, S["sb_o"], p - 1)
                    tt(wbuf[p % 2][:, :, :], z, n[:, :, :], ALU.subtract).then_inc(S["sb_zl"], 1)
                if p >= 1:
                    dve.wait_ge(S["sb_after"], p)
                    w = wbuf[(p - 1) % 2][:, :, :]
                    tt(w, w, PS[:, 4:6, 0:384], ALU.subtract).then_inc(S["sb_lw"], 1)
                if p >= 3:
                    o_low(p - 3)
            for p in range(SB_PAIRS - 2, SB_PAIRS):
                o_low(p)
            plain_splits(FIRST["o"], 4)
            layer_norm(2, FIRST["mod2"], 0)
            to_T(3, 0)
            mod_read(2, 4)
            mlp(1, FIRST["mlp1"])
            def norm_gain(r):
                dve.wait_ge(S["rms_rows_in"], 16 * r + 16)
                dve.wait_ge(S["mod_read"], 4 if r == 0 else 10)
                step(stt(mod[:, 3 * r + 1, :], mod[:, 3 * r + 1, :], 1.0, rms_row[r][:, :], ALU.add, ALU.mult))

            norm_gain(0)
            layer_norm(3, FIRST["mod3"], 4)

            def rms(r):
                for t in range(TT):
                    dve.wait_ge(S["rms_sq"], TT * r + t + 1)
                    ts(veps[:, t:t + 1], ms8[:, t:t + 1], 1.0 / D, EPS2, ALU.mult, ALU.add).then_inc(S["ln_var"], 1)
                for t in range(TT):
                    dve.wait_ge(S["ln_rstd"], 8 + TT * r + t + 1)
                    if r < 2:
                        stt(hn[:, t, :], h[:, t, :], rstd[:, t:t + 1], mod[:, 3 * r + 1, :], ALU.mult, ALU.mult
                            ).then_inc(S["rms_t"], 1)
                    else:
                        dve.wait_ge(S["final_in"], 16)
                        stt(fin[:, t, :], h[:, t, :], rstd[:, t:t + 1], final_row[:, :], ALU.mult, ALU.mult
                            ).then_inc(S["fin_ready"], 1)

            rms(0)
            to_T(4)
            mod_read(3, 0)
            dve.wait_ge(S["small_mm"], 2 + 1)
            dve.tensor_copy(bg, PS[:, 6, 0:16].rearrange("p (t n) -> p t n", t=TT)).then_inc(S["ba_read"], 1)
            dve.wait_ge(S["ba_read"], 1)
            tt(sx[:, 0:8].rearrange("p (t n) -> p t n", t=TT), bg[:, :, 4:8],
               rr["dt_bias2"].rearrange("p (o n) -> p o n", o=1).to_broadcast([P, TT, 4]), ALU.add
               ).then_inc(S["ba_read"], 1)
            softplus(gdec, 8, S["dt_exp"], 2)
            stt(gdec.rearrange("p (t n) -> p t n", t=TT), gdec.rearrange("p (t n) -> p t n", t=TT), -1.0,
                rr["a_log2"].rearrange("p (o n) -> p o n", o=1).to_broadcast([P, TT, 4]), ALU.mult, ALU.mult
                ).then_inc(S["g_done"], 1)
            dve.wait_ge(S["small_mm"], 3 + 1)
            dve.tensor_copy(tabs[0:H_A, TABLE_W:2 * TABLE_W], PS[0:H_A, 7, 0:TABLE_W]).then_inc(S["tab_sb"], 1)
            plain_splits(FIRST["qa"], 6)
            taps = 0
            for n in range(6):
                q, j = unit(FIRST["conv2"], n)
                dve.wait_ge(S["conv_first"], 32 + 2 * n + 2)
                for c in range(2):
                    for b in range(1, 4):
                        k = 4 * (2 * n + c) + 3 - b
                        a = acc2[n % 2][:, c, b:T]
                        last = stt(a, PS[:, n % 4, c * T:(c + 1) * T - b], cc["conv2_w"][:, k:k + 1], a, ALU.mult,
                                   ALU.add)
                        if not (c == 1 and b == 3):
                            step(last)
                last.then_inc(S["conv_done"], 1)
                split(q + 1, j)
            plain_splits(FIRST["zb"], 10)
            mod_read(4, 2)

            def s_max(n):
                dve.wait_ge(S["s_mm"], n + 1)
                for c, (a, b) in enumerate(((0, P), (P, 384))):
                    last = dve.reduce_max(mx[:, 2 * n + c:2 * n + c + 1], PS[:, n % 2, a:b], axis=AX_X)
                step(last)
                ts(nmx[:, 2 * n:2 * n + 2], mx[:, 2 * n:2 * n + 2], -1.0, None, ALU.mult).then_inc(S["s_max"], 1)

            def ya_low(p):
                dve.wait_ge(S["ya_hi"], p + 1)
                tt(yaTl[:, p, :], PS[:, 4 + p % 2, 0:T], yaTh[:, p, :].bitcast(F32), ALU.subtract
                   ).then_inc(S["ya_lo"], 1)

            s_max(0)
            for n in range(H_A):
                if n < H_A - 1:
                    s_max(n + 1)
                dve.wait_ge(S["s_exp"], 2 * n + 2)
                step(dve.reciprocal(sums[:, 2 * n:2 * n + 2], sums[:, 2 * n:2 * n + 2]))
                for c, (a, b) in enumerate(((0, P), (P, 384))):
                    last = ts(prob[n % 2][:, a:b], prob[n % 2][:, a:b], sums[:, 2 * n + c:2 * n + c + 1], None,
                              ALU.mult)
                last.then_inc(S["s_norm"], 1)
                if n % 2 == 1 and n >= 3:
                    ya_low((n - 3) // 2)
            ya_low(3)
            norm_gain(1)

            def per(v, n=P):
                return v.rearrange("p (n o) -> p n o", o=1).to_broadcast([P, v.shape[1], n])

            dve.wait_ge(S["small_mm"], 4 + 1)
            ts(l2r, PS[:, 0, 0:16], EPS2, None, ALU.add).then_inc(S["l2_ms"], 1)
            dve.wait_ge(S["small_mm"], 5 + 1)
            ts(ncum, PS[:, 1, 0:8], -1.0, None, ALU.mult).then_inc(S["gcum_read"], 1)
            dve.wait_ge(S["gcum_read"], 1)
            for t in range(TT):
                dve.wait_ge(S["gb_mm"], t + 1)
                for n in range(H_B):
                    m = 4 * t + n
                    last = stt(LT[:, m, :], tr_bank(0, 4 + t)[:, n, :], ncum[:, m:m + 1], mask_neg[:, 0:P], ALU.add,
                               ALU.add)
                last.then_inc(S["dec_arg"], 1)
            dve.wait_ge(S["gexp"], 1)
            step(ts(necum, ecum, -1.0, None, ALU.mult))
            dve.wait_ge(S["silu_done"], 16 + 4)
            for n in range(4):
                dve.wait_ge(S["l2_bc"], n + 1)
                a = qkvT[:, 2 * n:2 * n + 2, :]
                stt(a, a, 128.0 ** -0.5 if n < 2 else 1.0, PS[:, n, :].rearrange("p (c t) -> p c t", c=2), ALU.mult,
                    ALU.mult).then_inc(S["l2_done"], 1)
            dve.wait_ge(S["beta_done"], 1)
            for t in range(TT):
                dve.wait_ge(S["kk_mm"], t + 1)
                dve.wait_ge(S["dec_exp"], t + 1)
                b = slice(4 * t, 4 * t + 4)
                tt(Ub[:, b, :], tr_bank(0, t), LT[:, b, :], ALU.mult).then_inc(S["kk_read"], 1)
            for t in range(TT):
                dve.wait_ge(S["qk_mm"], t + 1)
                b = slice(4 * t, 4 * t + 4)
                tt(PT[:, b, :], tr_bank(0, 2 + t), LT[:, b, :], ALU.mult).then_inc(S["pt_done"], 1)
            dve.wait_ge(S["vk_tr"], 2)
            tt(R[:, :, :], tr_bank(0, 6), per(beta[:, 0:4]), ALU.mult).then_inc(S["vk_read"], 1)
            dve.tensor_copy(v1[:, :, :], tr_bank(0, 7)).then_inc(S["vk_read"], 1)
            dve.wait_ge(S["vk_tr"], 3)
            tt(kd[:, :, :], tr_bank(0, 0), LT[:, 0:4, P - 1:P].to_broadcast([P, 4, P]), ALU.mult
               ).then_inc(S["vk_read"], 1)
            for t in range(TT):
                dve.wait_ge(S["m_tr"], t + 1)
                tt(Xi[:, 4 * t:4 * t + 4, :], tr_bank(0, 4 + t), per(beta[:, 4 * t:4 * t + 4]), ALU.mult
                   ).then_inc(S["m_read"], 1)
            dve.wait_ge(S["lev_in"], 16)

            def wide(m):
                return m.rearrange("p (o n) -> p o n", o=1).to_broadcast([P, 4, P])

            for t in range(TT):
                dve.wait_ge(S["n_read"], t + 1)
                b = slice(4 * t, 4 * t + 4)
                step(tt(XiT[:, b, :], NT[:, b, :], wide(lev[:, 0, :]), ALU.mult))
                step(tt(XiT[:, b, :], wide(ident), XiT[:, b, :], ALU.subtract))
                step(tt(Xi[:, b, :], Xi[:, b, :], wide(lev[:, 7, :]), ALU.mult))
                tt(Xi[:, b, :], wide(ident), Xi[:, b, :], ALU.subtract).then_inc(S["x_upd"], 1)
            for m in range(1, 7):
                for t in range(TT):
                    dve.wait_ge(S["vt_mm"], 2 * m + t - 1)
                    b = slice(4 * t, 4 * t + 4)
                    if m < 6:
                        tt(Xi[:, b, :], Xi[:, b, :], tr_bank(0, 2 + t), ALU.subtract)
                    tt(XiT[:, b, :], XiT[:, b, :], tr_bank(0, 4 + t), ALU.subtract).then_inc(S["x_upd"], 1)
            dve.wait_ge(S["ks_mm"], 1)
            for n in range(H_B):
                last = stt(R[:, n, :], tr_bank(0, 0)[:, n, :], necum[:, 4 + n:5 + n], v1[:, n, :], ALU.mult, ALU.add)
            step(last)
            tt(R[:, :, :], R[:, :, :], per(beta[:, 4:8]), ALU.mult).then_inc(S["r1_done"], 1)
            dve.wait_ge(S["ks_mm"], 2)
            dve.wait_ge(S["o_part"], 2)
            for n in range(H_B):
                o = ob[:, 1, n * P:(n + 1) * P]
                last = stt(o, tr_bank(0, 1)[:, n, :], ecum[:, 4 + n:5 + n], o, ALU.mult, ALU.add)
            step(last)
            o8 = ob[:, :, :].rearrange("p t (n d) -> p (t n) d", d=P)
            q8 = osq[:, :, :].rearrange("p t (n d) -> p (t n) d", d=P)
            step(tt(osq[:, :, :], ob[:, :, :], ob[:, :, :], ALU.mult))
            step(dve.reduce_sum(rs8, q8, axis=AX_X))
            ts(rs8, rs8, 1.0 / P, EPS2, ALU.mult, ALU.add).then_inc(S["o_stat"], 1)
            dve.wait_ge(S["o_rstd"], 1)
            step(tt(o8, o8, per(rs8), ALU.mult))
            step(tt(o8, o8, rr["onorm"].rearrange("p (o n) -> p o n", o=1).to_broadcast([P, 8, P]), ALU.mult))
            tt(ob[:, :, :], ob[:, :, :], zb[:, :, :], ALU.mult).then_inc(S["o_scaled"], 1)
            for t in range(TT):
                dve.wait_ge(S["yb_hi"], t + 1)
                a = ybTh[:, :, t * P:(t + 1) * P]
                tt(ybTl[:, :, t * P:(t + 1) * P], tr_bank(0, 5 + t), a.bitcast(F32), ALU.subtract
                   ).then_inc(S["yb_lo"], 1)
            plain_splits(FIRST["up_a"], 4)

            dve.wait_ge(S["unit_done"], FIRST["wout2"])
            for t in range(TT):
                for c in range(2):
                    s = slice(512 * c, 512 * c + 512)
                    tt(mm_a[:, t, s], PS[:, 2 * c + t, :], gate_a[:, t, s], ALU.mult)
                    last = tt(gate_b[:, t, s], PS[:, 4 + 2 * c + t, :], gate_b[:, t, s], ALU.mult)
                last.then_inc(S["up_part"], 1)
            to_T(5)
            plain_splits(FIRST["wout2"], 4)

            def residual(r, last_unit, banks, gate):
                dve.wait_ge(S["unit_done"], last_unit)
                for t in range(TT):
                    for c in range(2):
                        s = slice(512 * c, 512 * c + 512)
                        last = tt(pre[:, t, s], PS[:, banks + 2 * c + t, :], gate[:, s], ALU.mult)
                    last.then_inc(S["res_t"], 1)

            residual(0, FIRST["mod5"], 0, mod[:, 2, :])
            rms(1)
            to_T(6, 0)
            mod_read(5, 4)

            def over(v, n):
                return v.rearrange("p (t o) -> p t o", o=1).to_broadcast([P, TT, n])

            def first_best(dst, v, best, tmp, n):
                step(tt(dst, v, over(best, n), ALU.is_equal))
                step(tt(dst, dst, rank[:, 0:n].rearrange("p (o n) -> p o n", o=1).to_broadcast([P, TT, n]), ALU.mult))
                step(dve.reduce_max(tmp, dst, axis=AX_X))
                step(tt(dst, dst, over(tmp, n), ALU.is_equal))

            dve.wait_ge(S["small_mm"], 6 + 1)
            tt(lg[:, :, :], PS[:, 0, 0:128].rearrange("p (t n) -> p t n", t=TT)[:, :, 0:36],
               rr["b_route"].rearrange("p (o n) -> p o n", o=1).to_broadcast([P, TT, 36]), ALU.add
               ).then_inc(S["lg_read"], 1)
            dve.wait_ge(S["lg_read"], 1)
            step(dve.reduce_max(rsc[:, 0:2], lg[:, :, 0:4], axis=AX_X))
            ts(rsc[:, 2:4], rsc[:, 0:2], -1.0, None, ALU.mult).then_inc(S["rt_max"], 1)
            oh_g, leg, oh1, oh2 = route[:, 0, :, 0:4], route[:, 2, :, :], route[:, 3, :, :], route[:, 4, :, :]
            first_best(oh_g, lg[:, :, 0:4], rsc[:, 0:2], rsc[:, 6:8], 4)
            for t in range(TT):
                g4 = oh_g[:, t, :].rearrange("p (g o) -> p g o", o=1).to_broadcast([P, 4, 8])
                step(tt(le[:, t, :].rearrange("p (g e) -> p g e", g=4),
                        lg[:, t, 4:36].rearrange("p (g e) -> p g e", g=4), g4, ALU.mult))
                step(dve.reduce_sum(leg[:, t, :], le[:, t, :].rearrange("p (g e) -> p e g", g=4), axis=AX_X))
            step(dve.reduce_max(rsc[:, 8:10], leg, axis=AX_X))
            first_best(oh1, leg, rsc[:, 8:10], rsc[:, 6:8], 8)
            step(stt(leg, oh1, NEG, leg, ALU.mult, ALU.add))
            step(dve.reduce_max(rsc[:, 10:12], leg, axis=AX_X))
            first_best(oh2, leg, rsc[:, 10:12], rsc[:, 6:8], 8)
            tt(rsc[:, 10:12], rsc[:, 10:12], rsc[:, 8:10], ALU.subtract).then_inc(S["rt_max"], 1)
            dve.wait_ge(S["rt_exp"], 3)
            step(ts(rsc[:, 12:14], rsc[:, 10:12], 1.0, None, ALU.add))
            step(tt(rsc[:, 12:14], rsc[:, 12:14], rsc[:, 4:6], ALU.mult))
            step(dve.reciprocal(rsc[:, 12:14], rsc[:, 12:14]))
            step(tt(rsc[:, 10:12], rsc[:, 10:12], rsc[:, 12:14], ALU.mult))
            step(tt(oh1, oh1, over(rsc[:, 12:14], 8), ALU.mult))
            step(tt(oh2, oh2, over(rsc[:, 10:12], 8), ALU.mult))
            step(tt(oh1, oh1, oh2, ALU.add))
            for t in range(TT):
                g4 = oh_g[:, t, :].rearrange("p (g o) -> p g o", o=1).to_broadcast([P, 4, 8])
                e4 = oh1[:, t, :].rearrange("p (o e) -> p o e", o=1).to_broadcast([P, 4, 8])
                last = tt(comb[:, t, :].rearrange("p (g e) -> p g e", g=4), g4, e4, ALU.mult)
            last.then_inc(S["rt_done"], 1)

            b = FIRST["moe"]

            def gated(q, s, e, n):
                dve.wait_ge(S["unit_done"], 4 * q + s + 1)
                dve.wait_ge(S["g_silu"], e + 1)
                tt(ubuf[n % 2][:, :], PS[:, 2 + n % 2, :], gbuf[n % 2][:, :], ALU.mult).then_inc(S["gu_done"], 1)

            def expert_low(e, n):
                dve.wait_ge(S["act_hi"], 32 + e + 1)
                tt(eTl[n % 2][:, :, :], ubuf[n % 2][:, :].rearrange("p (c t) -> p c t", c=2),
                   eTh[n % 2][:, :, :].bitcast(F32), ALU.subtract).then_inc(S["act_lo"], 1)

            def experts(i, n0, k):
                for n in range(n0, n0 + k):
                    g, u, d = (unit(b, 3 * n + m, i, 12) for m in (-1, 0, 1))
                    split(g[0] + 1, g[1])
                    gated(*u, 4 * i + n, n)
                    split(u[0] + 1, u[1])
                    expert_low(4 * i + n, n)
                    split(d[0] + 1, d[1])

            g, u = unit(b, 0), unit(b, 1)
            split(g[0] + 1, g[1])
            gated(*u, 0, 0)
            split(u[0] + 1, u[1])
            expert_low(0, 0)
            experts(0, 1, 4)
            with dve.Fori(1, 7) as i:
                experts(i, 1, 4)
            experts(7, 1, 3)
            residual(1, UNITS, 4, mod[:, 5, :])
            rms(2)

        @block.gpsimd
        def _(pool):
            pool.memset(mhalf, -0.5).then_inc(S["pool_init"], 1)
            pool.wait_ge(S["pool_init"], 1)

            def gated(hp):
                pool.wait_ge(S["y_read"], hp + 1)
                pool.tensor_tensor(zT[:, hp, :], ysk[hp % 2][:, :], zT[:, hp, :], ALU.mult).then_inc(S["yg_done"], 1)

            def y_rstd(g):
                pool.wait_ge(S["ms_read"], g + 1)
                a = yrs[:, 2 * g:2 * g + 2]
                pool.tensor_tensor(a, a, mhalf[:, 0:2], ALU.pow).then_inc(S["y_rstd"], 1)

            for hp in range(PAIRS):
                pool.wait_ge(S["exp_done"], hp + 1)
                pool.wait_ge(S["cb_read"], hp // 2 + 1)
                d = dec[hp % 3][:, :, :]
                pool.tensor_tensor(d, d, cbs[hp // 2 % 2][:, :].rearrange("p (o n) -> p o n", o=1
                                                                          ).to_broadcast([P, 2, 384]),
                                   ALU.mult).then_inc(S["m_ready"], 1)
                if hp >= 1:
                    gated(hp - 1)
                if hp % 2 == 0 and hp >= 6:
                    y_rstd((hp - 6) // 2)
            gated(PAIRS - 1)
            for g in range(5, GROUPS):
                y_rstd(g)

            def layer_norm(r, free):
                pool.wait_ge(*free)
                pool.dma_start(ln_row[:, :, :].rearrange("p a d -> p (a d)"),
                               ln_rows[r:r + 1, :].to_broadcast([P, 2 * D])).then_inc(S["row_in"], 16)
                if r == 0:
                    pool.dma_start(mod[:, :, :].rearrange("p a d -> p (a d)"), b_mod.to_broadcast([P, 6 * D])
                                   ).then_inc(S["mod_in"], 16)
                for t in range(TT):
                    pool.wait_ge(S["ln_var"], TT * r + t + 1)
                    pool.tensor_tensor(rstd[:, t:t + 1], veps[:, t:t + 1], mhalf[:, 0:1], ALU.pow
                                       ).then_inc(S["ln_rstd"], 1)
                pool.wait_ge(S["row_in"], 16 * r + 16)
                for t in range(TT):
                    pool.wait_ge(S["ln_gain"], TT * r + t + 1)
                    pool.tensor_tensor(h[:, t, :], pre[:, t, :], ln_row[:, 1, :], ALU.add).then_inc(S["h_ready"], 1)

            layer_norm(0, (S["unit_done"], FIRST["mod0"]))
            layer_norm(1, (S["h_ready"], TT))

            def masked(b):
                for c in range(2):
                    for a in (0, T):
                        last = pool.tensor_tensor(b[:, c, a:a + P], b[:, c, a:a + P], before, ALU.mult)
                return last

            for p in range(SB_PAIRS + 1):
                if p < SB_PAIRS:
                    pool.wait_ge(S["sb_zl"], p + 1)
                    masked(nbuf[p % 2]).then_inc(S["sb_mask"], 1)
                if p >= 1:
                    pool.wait_ge(S["sb_w"], p)
                    masked(wbuf[(p - 1) % 2]).then_inc(S["sb_wm"], 1)
            layer_norm(2, (S["h_ready"], 2 * TT))
            pool.wait_ge(S["unit_done"], FIRST["mod2"])
            pool.dma_start(rms_row[0][:, :], rms_rows[:, 0:D].to_broadcast([P, D])).then_inc(S["rms_rows_in"], 16)
            layer_norm(3, (S["h_ready"], 3 * TT))

            def rms(r):
                for t in range(TT):
                    pool.wait_ge(S["ln_var"], 8 + TT * r + t + 1)
                    pool.tensor_tensor(rstd[:, t:t + 1], veps[:, t:t + 1], mhalf[:, 0:1], ALU.pow
                                       ).then_inc(S["ln_rstd"], 1)
                if r < 2:
                    for t in range(TT):
                        pool.wait_ge(S["rms_t"], TT * r + t + 1)
                        pool.tensor_tensor(hn[:, t, :], hn[:, t, :], mod[:, 3 * r, :], ALU.add
                                           ).then_inc(S["hn_ready"], 1)

            pool.wait_ge(S["h_ready"], 4 * TT)
            pool.memset(relb[32:33, :], 1.0).then_inc(S["pool_init"], 1)
            pool.wait_ge(S["pool_init"], 1 + 1)
            pool.dma_start(relb[0:32, :], rel_bias).then_inc(S["tab_in"], 16)
            pool.dma_start(tabs[:, 0:TABLE_W], onehot).then_inc(S["tab_in"], 16)
            rms(0)
            pool.wait_ge(S["hn_ready"], 2)
            pool.dma_start(lev[:, :, :].rearrange("p a b -> p (a b)"), levels).then_inc(S["lev_in"], 16)
            pool.wait_ge(S["tab_sb"], 1)
            pool.dma_start(table_dram[:, :], tabs[0:H_A, TABLE_W:2 * TABLE_W]).then_inc(S["tab_out"], 16)
            pool.wait_ge(S["tab_out"], 16)
            pool.wait_ge(S["unit_done"], FIRST["mod4"])
            pool.dma_start(hank[:, :, 0:P], bass.AP(table_dram, P, [[1, P], [TABLE_W, H_A], [1, P]])
                           ).then_inc(S["hank_in"], 16)
            pool.dma_start(hank[:, :, P:384], bass.AP(table_dram, 0, [[1, P], [TABLE_W, H_A], [1, T]])
                           ).then_inc(S["hank_in"], 16)
            pool.dma_start(rms_row[1][:, :], rms_rows[:, D:2 * D].to_broadcast([P, D])).then_inc(S["rms_rows_in"], 16)
            pool.wait_ge(S["l2_ms"], 1)
            pool.tensor_tensor(l2r, l2r, mhalf[:, 0:1].to_broadcast([P, 16]), ALU.pow).then_inc(S["l2_rstd"], 1)

            def wide(m):
                return m.rearrange("p (o n) -> p o n", o=1).to_broadcast([P, 4, P])

            for t in range(TT):
                pool.wait_ge(S["kk_read"], t + 1)
                a = Ub[:, 4 * t:4 * t + 4, :]
                pool.tensor_tensor(a, a, wide(before), ALU.mult).then_inc(S["kk_masked"], 1)
            pool.wait_ge(S["vk_read"], 3)
            pool.wait_ge(S["lev_in"], 16)
            for m in range(1, 7):
                for t in range(TT):
                    pool.wait_ge(S["n_read"], t + 1)
                    if m >= 2:
                        pool.wait_ge(S["u_mm"], 2 * (m - 1) + t - 1)
                    b = slice(4 * t, 4 * t + 4)
                    pool.tensor_tensor(LT[:, b, :], NT[:, b, :], wide(lev[:, m, :]), ALU.mult
                                       ).then_inc(S["lt_done"], 1)
            pool.wait_ge(S["o_stat"], 1)
            pool.tensor_tensor(rs8, rs8, mhalf, ALU.pow).then_inc(S["o_rstd"], 1)
            for t in range(TT):
                pool.wait_ge(S["up_part"], t + 1)
                pool.tensor_tensor(mm_a[:, t, :], mm_a[:, t, :], gate_b[:, t, :], ALU.add).then_inc(S["mix_ready"], 1)

            def residual(r):
                for t in range(TT):
                    pool.wait_ge(S["res_t"], TT * r + t + 1)
                    pool.tensor_tensor(h[:, t, :], h[:, t, :], pre[:, t, :], ALU.add).then_inc(S["res_done"], 1)

            residual(0)
            rms(1)
            pool.wait_ge(S["tr_done"], 28)
            pool.dma_start(final_row[:, :], rms_rows[:, 2 * D:3 * D].to_broadcast([P, D])).then_inc(S["final_in"], 16)
            pool.wait_ge(S["cbT_sb"], 1)
            pool.dma_start(comb_dram[:, :], combT[:, :]).then_inc(S["cbT_out"], 16)
            pool.wait_ge(S["cbT_out"], 16)
            for n in range(4):
                pool.dma_start(cbc[:, 8 * n:8 * n + 8, :].rearrange("p e t -> p (e t)"),
                               bass.AP(comb_dram, 8 * n * T, [[0, P], [1, 8 * T]])).then_inc(S[f"cbc_in{min(n, 1)}"], 16)

            def expert(e, n):
                pool.wait_ge(S["gu_done"], e + 1)
                a = ubuf[n % 2][:, :].rearrange("p (c t) -> p c t", c=2)
                pool.tensor_tensor(a, a, cbc[:, bass.ds(e, 1), :].to_broadcast([P, 2, T]), ALU.mult
                                   ).then_inc(S["ga_done"], 1)

            pool.wait_ge(S["cbc_in0"], 16)
            for e in range(5):
                expert(e, e)
            pool.wait_ge(S["cbc_in1"], 48)
            with pool.Fori(1, 7) as i:
                for n in range(1, 5):
                    expert(4 * i + n, n)
            for n in range(29, 32):
                expert(n, n)
            residual(1)
            rms(2)


def _tiles(w, k):
    return w.reshape(k, P, -1).transpose(1, 0, 2).reshape(P, -1)


def _pack(np, inputs):
    units = []

    def wide(w):
        units.extend(_tiles(w[:, n:n + 256], KD) for n in range(0, w.shape[1], 256))

    def deep(w):
        units.extend(_tiles(w[k:k + 512, n:n + 512], 4)
                     for n in range(0, w.shape[1], 512) for k in range(0, w.shape[0], 512))

    def mlp(w1, w2):
        for j in range(CHUNKS + 1):
            if j < CHUNKS:
                units.append(_tiles(w1[:, 256 * j:256 * j + 256], KD))
            if j >= 1:
                units.append(_tiles(w2[256 * (j - 1):256 * j], 2))

    def mod(k):
        deep(inputs["w_mod_2"][0][:, D * k:D * k + D])

    w_in = inputs["ssm_w_in"][0]
    wide(w_in[:, D_INNER:3 * D_INNER])
    wide(w_in[:, 0:D_INNER])
    deep(inputs["ssm_w_out"][0])
    mod(0)
    mlp(inputs["mlp_w1"][0], inputs["mlp_w2"][0])
    mod(1)
    wide(inputs["sb_w_k"])
    wide(inputs["sb_w_q"][0])
    deep(inputs["sb_w_v"])
    deep(inputs["sb_w_o"][0])
    mod(2)
    mlp(inputs["mlp_w1"][1], inputs["mlp_w2"][1])
    mod(3)
    w2 = inputs["w_in_2"][0]
    wide(w2[:, 0:1024])
    deep(w2[:, 1024:1536])
    wide(w2[:, 1536:3072])
    deep(w2[:, 3072:3584])
    deep(w2[:, 3592:5640])
    mod(4)
    deep(inputs["w_up_a_2"][0])
    deep(inputs["w_up_b_2"][0])
    deep(inputs["w_out_2"][0])
    mod(5)
    gate, up, down = (inputs[f"w_e_{n}_2"][0].reshape((EXPERTS,) + inputs[f"w_e_{n}_2"].shape[3:])
                      for n in ("gate", "up", "down"))
    for e in range(EXPERTS + 1):
        if e < EXPERTS:
            units += [_tiles(gate[e], KD), _tiles(up[e], KD)]
        if e >= 1:
            units.append(_tiles(down[e - 1], 2))
    small = np.concatenate([w_in[:, 3 * D_INNER:], w2[:, 3584:3592], inputs["w_rg_2"][0], inputs["w_re_2"][0]], 1)
    cols = np.concatenate([
        inputs["ssm_conv_w"][0].reshape(4, 32, P).transpose(2, 1, 0).reshape(P, 128),
        inputs["ssm_conv_b"][0].reshape(32, P).T,
        np.repeat(inputs["ssm_d"][0], 64).reshape(16, P).T,
        inputs["ssm_norm_w"][0].reshape(16, P).T,
        inputs["conv_w_2"][0].reshape(4, 12, P).transpose(2, 1, 0).reshape(P, 48),
        inputs["c_2"].reshape(KD, P).T], 1)
    rows = np.concatenate([inputs[n].reshape(-1) for n in
                           ("ssm_dt_bias", "ssm_a_log", "a_log_2", "dt_bias_2", "onorm_w_2", "b_rg_2", "b_re_2")])
    ln = np.stack([np.concatenate([inputs[f"ln_{n}_g"][m], inputs[f"ln_{n}_b"][m]])
                   for m in range(2) for n in ("mix", "mlp")])
    rms = np.concatenate([inputs["norm1_w_2"][0], inputs["norm2_w_2"][0], inputs["final_norm_w_2"]])
    return {"x": inputs["x"][0], "weights": np.stack(units), "small": _tiles(small, KD), "cols": cols,
            "rows": rows[None], "ln_rows": ln, "rms_rows": rms[None], "b_mod": inputs["b_mod_2"],
            "rel_bias": inputs["rel_bias_2"]}


def _constants(np):
    i, j = np.arange(P)[:, None], np.arange(P)[None, :]
    consts = np.concatenate([i == j, i + j == P - 1, i <= j, i >= 0 * j, np.where(i <= j, 0.0, NEG),
                             0.0 * (i + j), i > j, i < j, np.broadcast_to(8 - np.arange(8), (P, 8))],
                            1).astype(np.float32)
    pairs = [((j >> m + 1) == (i >> m + 1)) & ((j >> m) > (i >> m)) for m in range(7)]
    levels = np.stack(pairs + [pairs[0].T], 1).astype(np.float32).reshape(P, 8 * P)
    dist = 255 - np.arange(TABLE_W)
    n = np.maximum(dist, 1).astype(np.float32)
    large = np.minimum(16 + (np.log(n / 16) / np.log(128 / 16) * 16).astype(np.int32), 31)
    bucket = np.where(dist < 16, dist, large)
    onehot = np.zeros((33, TABLE_W), np.float32)
    for x in range(TABLE_W):
        onehot[bucket[x] if dist[x] >= 0 else 32, x] = 1.0 if dist[x] >= 0 else NEG
    return {"consts": consts, "levels": levels, "onehot": onehot}


def kernel(**inputs):
    import numpy as np
    import concourse.bacc as bacc
    from concourse.bass_utils import run_bass_kernel_spmd

    arrays = {**_pack(np, {n: np.asarray(a) for n, a in inputs.items()}), **_constants(np)}
    arrays = {n: np.ascontiguousarray(a) for n, a in arrays.items()}
    nc = bacc.Bacc("TRN2", target_bir_lowering=False, num_devices=1)
    args = {n: nc.dram_tensor(n, a.shape, mybir.dt.from_np(a.dtype), kind="ExternalInput").ap()
            for n, a in arrays.items()}
    out = nc.dram_tensor("out", (T, D), F32, kind="ExternalOutput")
    build(nc, out=out.ap(), **args)
    r = run_bass_kernel_spmd(nc, [arrays], core_ids=[0])
    return r.results[0]["out"].reshape(1, T, D)
```

```python
from contextlib import ExitStack

import concourse.bass as bass
from concourse import mybir

F32 = mybir.dt.float32
F32R = mybir.dt.float32r
ACT = mybir.ActivationFunctionType
ALU = mybir.AluOpType
AX_X = mybir.AxisListType.X

P = 128
T = 256
TT = T // P
D = 1024
KD = D // P
ALPHA = 4.0 ** 0.25
LN_EPS = 1e-5
RMS_EPS = 1e-5
EPS2 = 1e-6
NEG = -1e30

D_INNER = 2048
XT_TILES = D_INNER // P
GROUPS = 8
PAIRS = 16
CHUNKS = 16
SB_PAIRS = 8
EXPERTS = 32
H_A = 8
H_B = 4

UNIT = 2048
RING = 4

COUNTS = [("in", 24), ("out", 8), ("mod0", 4), ("mlp0", 32), ("mod1", 4), ("k", 4), ("q", 4), ("v", 4), ("o", 4),
          ("mod2", 4), ("mlp1", 32), ("mod3", 4), ("qa", 2), ("ka", 2), ("va", 2), ("conv2", 6), ("zb", 2), ("gate", 8),
          ("mod4", 4), ("up_a", 2), ("up_b", 2), ("wout2", 4), ("mod5", 4), ("moe", 96)]
FIRST = {}
_n = 0
for _name, _count in COUNTS:
    FIRST[_name] = _n
    _n += _count
UNITS = _n

CONST = {}
_n = 0
for _name, _count in [("ident", 128), ("anti", 128), ("triu_ones", 256), ("mask_neg", 256), ("later", 128),
                      ("before", 128), ("rank", 8)]:
    CONST[_name] = (_n, _n + _count)
    _n += _count
CONST_W = _n
COLS = {}
_n = 0
for _name, _count in [("conv_w", 128), ("conv_b", 32), ("skip", 16), ("norm_w", 16), ("conv2_w", 48), ("c", 8)]:
    COLS[_name] = (_n, _n + _count)
    _n += _count
COLS_W = _n
ROWS = {}
_n = 0
for _name, _count in [("dt_bias", 32), ("a_log", 32), ("a_log2", 4), ("dt_bias2", 4), ("onorm", 128),
                      ("b_route", 36)]:
    ROWS[_name] = (_n, _n + _count)
    _n += _count
ROWS_W = _n
SMALL_W = 76
TABLE_W = 384
CROWD = P


def unit(first, p, i=0, per=0):
    u = first + p
    return u // RING + i * (per // RING), u % RING


def wait(eng, sem, value):
    if isinstance(value, int) and value <= 0:
        return
    eng.wait_ge(sem, value)


class Steps:

    def __init__(self, eng, sem):
        self.eng, self.sem, self.n = eng, sem, 0

    def __call__(self, instruction):
        self.n += 1
        instruction.then_inc(self.sem, 1)
        self.eng.wait_ge(self.sem, self.n)


def build(nc, x, weights, small, consts, levels, onehot, cols, rows, ln_rows, rms_rows, b_mod, rel_bias, out):
    with ExitStack() as ctx:
        def at(name, kib, shape, dt=F32):
            return nc.alloc_sbuf_tensor_at(name, shape, dt, offset=16512 + int(kib * 1024))

        def sem(name):
            return ctx.enter_context(nc.semaphore(name))

        ctx.enter_context(nc.sbuf_tensor("arena", [P, 212800 // 4], F32))
        PS = ctx.enter_context(nc.psum_tensor("banks", [P, 8, 512], F32))
        table_dram = nc.dram_tensor("bias_table", (H_A, TABLE_W), F32)

        raw = [at(f"raw{j}", 8 * j, [P, UNIT]) for j in range(RING)]
        hi = [at(f"w_hi{j}", 32 + 8 * j, [P, UNIT], F32R) for j in range(RING)]
        lo = [at(f"w_lo{j}", 64 + 8 * j, [P, UNIT], F32R) for j in range(RING)]
        h = at("h", 96, [P, TT, D])
        hTh = at("hT_hi", 104, [P, KD, T], F32R)
        hTl = at("hT_lo", 112, [P, KD, T], F32R)
        const = at("const", 120, [P, CONST_W])
        col = at("col", 124.25, [P, COLS_W])
        row = at("row", 125.25, [P, ROWS_W])
        tiny = at("tiny", 126.25, [P, 384])
        ln_row = at("ln_gain_bias", 128, [P, 2, D])
        ident = const[:, slice(*CONST["ident"])]
        anti = const[:, slice(*CONST["anti"])]
        triu_ones = const[:, slice(*CONST["triu_ones"])]
        triu, ones = triu_ones[:, 0:128], triu_ones[:, 128:256]
        mask_neg = const[:, slice(*CONST["mask_neg"])]
        later = const[:, slice(*CONST["later"])]
        before = const[:, slice(*CONST["before"])]
        rank = const[:, slice(*CONST["rank"])]
        cc = {n: col[:, a:b] for n, (a, b) in COLS.items()}
        rr = {n: row[:, a:b] for n, (a, b) in ROWS.items()}
        stats = tiny[:, 0:24].rearrange("p (t c s) -> p t c s", t=2, c=2)
        mv = tiny[:, 24:28].rearrange("p (t s) -> p t s", t=2)
        veps, rstd, nmean = tiny[:, 28:30], tiny[:, 30:32], tiny[:, 32:34]
        mhalf = tiny[:, 34:42]
        ms8, rs8 = tiny[:, 42:50], tiny[:, 50:58]
        ncs = tiny[:, 64:128]
        sx, st, su, sv = tiny[:, 128:192], tiny[:, 192:256], tiny[:, 256:320], tiny[:, 320:384]
        sw = at("softplus_ln", 202.75, [P, 64])[:, :]
        dt_all = at("dt", 202.25, [P, 64])[:, :]
        da_all = at("da", 202.5, [P, 64])[:, :]
        small_raw = at("w_small", 188, [P, KD * SMALL_W])
        small_hi = at("w_small_hi", 203, [P, KD * SMALL_W], F32R)
        small_lo = at("w_small_lo", 205.375, [P, KD * SMALL_W], F32R)
        wsh = small_hi[:, :].rearrange("p (k n) -> p k n", k=KD)
        wsl = small_lo[:, :].rearrange("p (k n) -> p k n", k=KD)

        xbcT = at("xbcT", 136, [P, 32, T])
        zT = at("zT", 168, [P, XT_TILES, T])
        X = at("X", 184, [P, TT, D_INNER])
        yTh = at("yT_hi", 152, [P, 2, GROUPS, T], F32R)
        yTl = at("yT_lo", 136, [P, XT_TILES, T], F32R)
        csT_hi = at("sums_hi", 128, [32, T], F32R)
        csT_lo = at("sums_lo", 129, [32, T], F32R)
        pick = at("pick", 130, [32, 32], F32R)
        acc = [at(f"conv{b}", 184 + 2 * b, [P, 2, T]) for b in range(2)]
        dec = [at(f"decay{b}", 104 + 3 * b, [P, 2, 384]) for b in range(3)]
        cbs = [at(f"cb{b}", 113 + 1.5 * b, [P, 384]) for b in range(2)]
        ysq = [at(f"y_sq{b}", 116 + 2 * b, [P, 2, T]) for b in range(2)]
        ysk = [at(f"y_skip{b}", 200 + b, [P, T]) for b in range(2)]

        rbuf = [at(f"relu{b}", 160 + 2 * b, [P, 512]) for b in range(2)]
        sbuf = [at(f"relu_sq{b}", 164 + 2 * b, [P, 512]) for b in range(2)]
        aTh = [at(f"act_hi{b}", 168 + 2 * b, [P, 2, T], F32R) for b in range(2)]
        aTl = [at(f"act_lo{b}", 172 + 2 * b, [P, 2, T], F32R) for b in range(2)]
        pre = at("pre_norm", 176, [P, TT, D])

        kT = at("kT", 160, [P, 8, T])
        qT = at("qT", 168, [P, 8, T])
        V = at("v", 176, [P, TT, D])
        oTh = at("oT_hi", 184, [P, 8, T], F32R)
        oTl = at("oT_lo", 192, [P, 8, T], F32R)
        abuf = [at("soft0", 200, [P, 2, 384]), at("soft1", 104, [P, 2, 384])]
        nbuf = [at(f"neg_log{b}", 107 + 3 * b, [P, 2, 384]) for b in range(2)]
        wbuf = [at(f"weight{b}", 113 + 3 * b, [P, 2, 384]) for b in range(2)]

        mod = at("mod", 136, [P, 6, D])
        c_hi = at("c_hi", 126.1875, [P, KD], F32R)
        c_lo = at("c_lo", 126.21875, [P, KD], F32R)
        rms_row = [at("rms_gain0", 184, [P, D]), at("rms_gain1", 116, [P, D])]
        hn = at("normed", 128, [P, TT, D])
        qaT = at("qaT", 160, [P, 4, T])
        kaT = at("kaT", 164, [P, 4, T])
        va = at("va", 168, [P, TT, 512])
        zb = at("z_b", 172, [P, TT, 512])
        qkvT = at("qkvT", 176, [P, 12, T])
        acc2 = [at(f"conv2_{b}", 188 + 2 * b, [P, 2, T]) for b in range(2)]
        gate_a = at("gate_a", 128, [P, TT, D])
        gate_b = at("gate_b", 188, [P, TT, D])
        yaTh = at("yaT_hi", 160, [P, 4, T], F32R)
        yaTl = at("yaT_lo", 164, [P, 4, T], F32R)
        hank = at("bias_rows", 104, [P, H_A, 384])
        prob = [at(f"prob{b}", 196 + 1.5 * b, [P, 384]) for b in range(2)]
        pTb = [at(f"probT{b}", 199 + 1.5 * b, [P, 384]) for b in range(2)]
        tabs = at("bias_table_sb", 196, [33, 2 * TABLE_W])
        relb = at("rel_bias_sb", 199, [33, H_A])
        tiny2 = at("tiny2", 127.75, [P, 64])
        mx, nmx, sums, l2r = (tiny2[:, 16 * n:16 * n + 16] for n in range(4))
        yrs = mx

        bg = tiny[:, 64:80].rearrange("p (t n) -> p t n", t=2)
        beta = tiny[:, 80:88]
        gdec = tiny[:, 88:96]
        ncum = tiny[:, 96:104]
        necum = tiny[:, 104:112]
        ecum = tiny[:, 112:120]
        rn = at("l2_rstd", 104, [P, 8, T])
        XiT = at("inverse_T", 104, [P, 8, P])
        Xi = at("inverse", 108, [P, 8, P])
        NT = at("system_T", 112, [P, 8, P])
        Ub = at("half_product", 116, [P, 8, P])
        lev = at("level_masks", 136, [P, 8, P])
        LT = at("level_T", 140, [P, 8, P])
        PT = at("score_T", 168, [P, 8, P])
        kd = at("k_decayed", 196, [P, 4, P])
        R = at("right_side", 198, [P, 4, P])
        S1 = at("state", 200, [P, 4, P])
        v1 = at("v_tile1", 184, [P, 4, P])
        vn0 = at("v_new0", 186, [P, 4, P])
        ob = at("o_delta", 112, [P, TT, 512])
        osq = at("o_sq", 108, [P, TT, 512])
        ybTh = at("ybT_hi", 104, [P, 4, T], F32R)
        ybTl = at("ybT_lo", 116, [P, 4, T], F32R)
        mm_a = at("mix", 176, [P, TT, D])

        lg = at("logits", 176, [P, TT, 36])
        route = at("route_tmp", 176.5, [P, 5, TT, 8])
        rsc = tiny[:, 128:144]
        le = at("route_le", 177.75, [P, TT, 32])
        comb = at("combine", 178, [P, TT, 32])
        gather = at("gather", 160, [P, 4, TT, P])
        scatter = at("scatter", 164, [P, 4, T])
        scat = at("scatter_now", 180, [P, T])
        slots = at("slot_numbers", 181, [P, P])
        slot_comb = at("slot_weights", 182, [P, EXPERTS])
        place = at("places", 182.25, [P, 16])
        most = at("most", 182.5, [P, 1], mybir.dt.int32)
        hgh = at("group_T_hi", 168, [P, KD, P], F32R)
        hgl = at("group_T_lo", 172, [P, KD, P], F32R)
        yg = at("group_y", 184, [P, D])
        gbuf = [at(f"gate_silu{b}", 188 + 2 * b, [P, 512]) for b in range(2)]
        ubuf = [at(f"gated{b}", 192 + 2 * b, [P, 512]) for b in range(2)]
        eTh = [at(f"exp_hi{b}", 136 + 2 * b, [P, 2, T], F32R) for b in range(2)]
        eTl = [at(f"exp_lo{b}", 140 + 2 * b, [P, 2, T], F32R) for b in range(2)]
        final_row = at("final_gain", 196, [P, D])
        fin = at("result", 144, [P, TT, D])

        class Signals(dict):

            def __missing__(self, name):
                self[name] = sem(name)
                return self[name]


        S = Signals()
        raw_ready = [S[f"raw_ready{j}"] for j in range(RING)]

        def tr_bank(b):
            return PS[:, b, :].rearrange("p (c t) -> p c t", c=4)

        block = ctx.enter_context(nc.Block())

        @block.sync
        def _(sp):
            sp.dma_start(h[:, :, :], x.rearrange("(t p) d -> p t d", p=P)).then_inc(S["x_in"], 16)
            sp.dma_start(const[:, :], consts).then_inc(S["x_in"], 16)
            for j in range(RING):
                sp.dma_start(raw[j][:, :], weights[j]).then_inc(raw_ready[j], 16)
                if j == 0:
                    sp.dma_start(col[:, :], cols).then_inc(S["const_in"], 16)
            sp.dma_start(small_raw[:, :], small).then_inc(S["const_in"], 16)
            sp.dma_start(row[:, :], rows.to_broadcast([P, ROWS_W])).then_inc(S["const_in"], 16)

            def load(q, j):
                sp.wait_ge(S["w_lo_done"], 4 * q + j - 3)
                sp.dma_start(raw[j][:, :], weights[bass.ds(4 * q + j, 1), :, :].rearrange("o p n -> (o p) n")
                             ).then_inc(raw_ready[j], 16)

            with sp.Fori(1, UNITS // RING) as q:
                for j in range(RING):
                    load(q, j)
            for j in range(UNITS % RING):
                load(UNITS // RING, j)

            for t in range(TT):
                sp.wait_ge(S["fin_ready"], t + 1)
                sp.dma_start(out[t * P:(t + 1) * P, :], fin[:, t, :]).then_inc(S["out_done"], 16)
            sp.wait_ge(S["out_done"], 16 * TT)

        @block.scalar
        def _(act):
            A = act.activation
            step = Steps(act, S["act_step"])

            def split(q, j):
                if isinstance(q, int) and 4 * q + j >= UNITS:
                    return
                act.wait_ge(raw_ready[j], 16 * q + 16)
                wait(act, S["unit_done"], 4 * q + j - 3)
                A(hi[j][:, :], raw[j][:, :], ACT.Copy).then_inc(S["w_hi_done"], 1)

            def to_T(r, banks=4):
                for n in range(4):
                    act.wait_ge(S["tr_done"], 4 * r + n + 1)
                    A(hTh[:, 4 * (n % 2):4 * (n % 2) + 4, n // 2 * P:(n // 2 + 1) * P],
                      tr_bank(banks + n), ACT.Copy).then_inc(S["tr_hi"], 1)

            def softplus(n, ready, before=0):
                act.wait_ge(S[ready[0]], ready[1])
                step(A(st[:, 0:n], sx[:, 0:n], ACT.Abs))
                A(st[:, 0:n], st[:, 0:n], ACT.Exp, scale=-1.0).then_inc(S[ready[2]], 1)
                act.wait_ge(S[ready[2]], before + 1)
                A(sw[:, 0:n], st[:, 0:n], ACT.Ln, bias=1.0).then_inc(S[ready[2]], 1)

            to_T(0)
            for j in range(RING):
                split(0, j)
            act.wait_ge(S["const_in"], 48)
            A(small_hi[:, :], small_raw[:, :], ACT.Copy).then_inc(S["small_hi_done"], 1)
            A(pick[:, :], const[0:32, 0:32], ACT.Copy).then_inc(S["small_hi_done"], 1)
            A(cc["c"], cc["c"], ACT.Silu).then_inc(S["c_ready"], 1)
            act.wait_ge(S["c_ready"], 1)
            A(c_hi[:, :], cc["c"], ACT.Copy).then_inc(S["c_ready"], 1)

            def conv(i, j):
                act.wait_ge(S["unit_done"], 4 * i + j + 1)
                for c in range(2):
                    ct = 8 * i + 2 * j + c
                    b = cc["conv_b"][:, bass.ds(ct, 1)]
                    w = cc["conv_w"][:, bass.ds(4 * ct + 3, 1)]
                    A(acc[j % 2][:, c, :], PS[:, j, c * T:(c + 1) * T], ACT.Identity, bias=b, scale=w
                      ).then_inc(S["conv_first"], 1)
                split(i + 1, j)
                act.wait_ge(S["conv_done"], 4 * i + j + 1)
                A(xbcT[:, bass.ds(8 * i + 2 * j, 2), :], acc[j % 2][:, :, :], ACT.Silu).then_inc(S["silu_done"], 1)

            with act.Fori(0, 4) as i:
                for j in range(RING):
                    conv(i, j)
            for i in range(4, 6):
                if i == 5:
                    step(A(rr["a_log"], rr["a_log"], ACT.Exp))
                    softplus(64, ("dt_read", 1, "dt_exp"))
                for j in range(RING):
                    n = 4 * i + j - 16
                    act.wait_ge(S["unit_done"], 4 * i + j + 1)
                    A(zT[:, 2 * n:2 * n + 2, :], PS[:, j, :].rearrange("p (c t) -> p c t", c=2), ACT.Silu
                      ).then_inc(S["z_done"], 1)
                    split(i + 1, j)

            act.wait_ge(S["small_mm"], 1 + 1)
            A(csT_hi[:, :], PS[0:32, 6, 0:T], ACT.Copy).then_inc(S["csT_done"], 1)

            def y_square(g):
                act.wait_ge(S["yg_done"], 2 * g + 2)
                wait(act, S["ms_done"], g - 1)
                A(ysq[g % 2][:, :, :], zT[:, 2 * g:2 * g + 2, :], ACT.Square).then_inc(S["sq_done"], 1)

            def y_high(g):
                for c in range(2):
                    act.wait_ge(S["yn_done"], 2 * g + c + 1)
                    A(yTh[:, c, g, :], zT[:, 2 * g + c, :], ACT.Copy).then_inc(S["yhi"], 1)

            for hp in range(PAIRS):
                g = hp // 2
                if hp % 2 == 0:
                    act.wait_ge(S["cb_mm"], g + 1)
                    wait(act, S["m_ready"], 2 * g - 2)
                    A(cbs[g % 2][:, :], PS[:, g % 2, 0:384], ACT.Copy).then_inc(S["cb_read"], 1)
                act.wait_ge(S["d_read"], hp + 1)
                A(dec[hp % 3][:, :, :], dec[hp % 3][:, :, :], ACT.Exp).then_inc(S["exp_done"], 1)
                if hp % 2 == 1 and hp >= 3:
                    y_square((hp - 3) // 2)
                if hp % 2 == 0 and hp >= 8:
                    y_high((hp - 8) // 2)
            y_square(GROUPS - 1)
            for g in range(4, GROUPS):
                y_high(g)

            def plain_splits(first, count):
                for p in range(count):
                    q, j = unit(first, p)
                    split(q + 1, j)

            def layer_norm(r):
                for t in range(TT):
                    act.wait_ge(S["ln_norm_in"], TT * r + t + 1)
                    A(pre[:, t, :], pre[:, t, :], ACT.Identity, bias=nmean[:, t:t + 1], scale=rstd[:, t:t + 1]
                      ).then_inc(S["ln_norm"], 1)

            def mlp(m, first):
                def relu(q, s, n):
                    act.wait_ge(S["unit_done"], 4 * q + s + 1)
                    A(rbuf[n % 2][:, :], PS[:, n % 4, :], ACT.Relu).then_inc(S["relu_done"], 1)

                def high(j, n):
                    act.wait_ge(S["sq2_done"], j + 1)
                    A(aTh[n % 2][:, :, :], sbuf[n % 2][:, :].rearrange("p (c t) -> p c t", c=2), ACT.Copy
                      ).then_inc(S["act_hi"], 1)

                j0 = CHUNKS * m
                q, s = unit(first, 0)
                relu(q, s, 0)
                split(q + 1, s)
                high(j0, 0)

                def round_of(i, n, k):
                    for e in range(n, n + k):
                        q, s = unit(first, 2 * e - 1, i, 8)
                        relu(q, s, e)
                        split(q + 1, s)
                        high(j0 + e + 4 * i, e)
                        q, s = unit(first, 2 * e, i, 8)
                        split(q + 1, s)

                with act.Fori(0, 3) as i:
                    round_of(i, 1, 4)
                round_of(3, 1, 3)
                q, s = unit(first, 31)
                split(q + 1, s)

            plain_splits(FIRST["out"], 8)
            layer_norm(0)
            to_T(1, 0)
            plain_splits(FIRST["mod0"], 4)
            mlp(0, FIRST["mlp0"])
            layer_norm(1)
            to_T(2)
            plain_splits(FIRST["mod1"], 4)

            for n in range(8):
                q, j = unit(FIRST["k"], n)
                act.wait_ge(S["unit_done"], 4 * q + j + 1)
                dst, scale = ((kT, 1.0), (qT, 0.125))[n // 4]
                A(dst[:, 2 * (n % 4):2 * (n % 4) + 2, :], PS[:, n % 4, :].rearrange("p (c t) -> p c t", c=2),
                  ACT.Copy, scale=scale).then_inc(S["kq_read"], 1)
                split(q + 1, j)
            for c in range(2):
                plain_splits(FIRST["v"] + 2 * c, 1)
                q, j = unit(FIRST["v"], 2 * c + 1)
                act.wait_ge(S["unit_done"], 4 * q + j + 1)
                for t in range(TT):
                    A(V[:, t, 512 * c:512 * c + 512], PS[:, 4 + 2 * c + t, :], ACT.Copy).then_inc(S["v_read"], 1)
                split(q + 1, j)

            def o_high(p):
                act.wait_ge(S["sb_o"], p + 1)
                A(oTh[:, p, :], PS[:, 6 + p % 2, 0:T], ACT.Copy).then_inc(S["oT_hi_done"], 1)

            for p in range(SB_PAIRS):
                z = PS[:, 2 * (p % 2):2 * (p % 2) + 2, 0:384]
                a = abuf[p % 2]
                act.wait_ge(S["sb_z"], p + 1)
                wait(act, S["sb_nlo"], p - 1)
                step(A(a[:, :, :], z, ACT.Abs))
                step(A(a[:, :, :], a[:, :, :], ACT.Exp, scale=-1.0))
                A(a[:, :, :], a[:, :, :], ACT.Ln, bias=1.0).then_inc(S["sb_abs"], 1)
                if p >= 1:
                    act.wait_ge(S["sb_lw"], p)
                    A(wbuf[(p - 1) % 2][:, :, :], wbuf[(p - 1) % 2][:, :, :], ACT.Exp).then_inc(S["sb_w"], 1)
                if p >= 2:
                    o_high(p - 2)
            act.wait_ge(S["sb_lw"], SB_PAIRS)
            A(wbuf[1][:, :, :], wbuf[1][:, :, :], ACT.Exp).then_inc(S["sb_w"], 1)
            o_high(SB_PAIRS - 2)
            o_high(SB_PAIRS - 1)
            plain_splits(FIRST["o"], 4)

            layer_norm(2)
            to_T(3, 0)
            plain_splits(FIRST["mod2"], 4)
            mlp(1, FIRST["mlp1"])
            layer_norm(3)

            def rms(r):
                for t in range(TT):
                    if r == 0:
                        act.wait_ge(S[("h_ready", "h1_ready")[t]], 4)
                    elif r == 1:
                        act.wait_ge(S["res_done"], t + 1)
                    else:
                        act.wait_ge(S["moe_done"], t + 1)
                    A(pre[:, t, :], h[:, t, :], ACT.Square, accum_out=ms8[:, t:t + 1]).then_inc(S["rms_sq"], 1)

            rms(0)
            to_T(4)
            plain_splits(FIRST["mod3"], 4)

            act.wait_ge(S["small_read"], 2 + 1)
            A(beta.rearrange("p (t n) -> p t n", t=TT), bg[:, :, 0:4], ACT.Sigmoid).then_inc(S["small_act"], 1)
            step(A(rr["a_log2"], rr["a_log2"], ACT.Exp))
            softplus(8, ("small_read", 4, "dt_exp"), 2)

            for n in range(4):
                q, j = unit(FIRST["qa"], n)
                act.wait_ge(S["unit_done"], 4 * q + j + 1)
                A((qaT, kaT)[n // 2][:, 2 * (n % 2):2 * (n % 2) + 2, :],
                  PS[:, n, :].rearrange("p (c t) -> p c t", c=2), ACT.Copy, scale=(0.125, 1.0)[n // 2]
                  ).then_inc(S["qk_read"], 1)
                split(q + 1, j)
            plain_splits(FIRST["va"], 1)
            q, j = unit(FIRST["va"], 1)
            act.wait_ge(S["unit_done"], 4 * q + j + 1)
            for t in range(TT):
                A(va[:, t, :], PS[:, 4 + t, :], ACT.Copy).then_inc(S["v_read"], 1)
            split(q + 1, j)
            for n in range(6):
                q, j = unit(FIRST["conv2"], n)
                act.wait_ge(S["unit_done"], 4 * q + j + 1)
                for c in range(2):
                    w = cc["conv2_w"][:, 4 * (2 * n + c) + 3:4 * (2 * n + c) + 4]
                    A(acc2[n % 2][:, c, :], PS[:, n % 4, c * T:(c + 1) * T], ACT.Copy, scale=w
                      ).then_inc(S["conv_first"], 1)
                split(q + 1, j)
                act.wait_ge(S["conv_done"], 16 + n + 1)
                A(qkvT[:, 2 * n:2 * n + 2, :], acc2[n % 2][:, :, :], ACT.Silu).then_inc(S["silu_done"], 1)
            plain_splits(FIRST["zb"], 1)
            q, j = unit(FIRST["zb"], 1)
            act.wait_ge(S["unit_done"], 4 * q + j + 1)
            for t in range(TT):
                A(zb[:, t, :], PS[:, 6 + t, :], ACT.Silu).then_inc(S["z_done"], 1)
            split(q + 1, j)
            for c in range(4):
                plain_splits(FIRST["gate"] + 2 * c, 1)
                q, j = unit(FIRST["gate"], 2 * c + 1)
                act.wait_ge(S["unit_done"], 4 * q + j + 1)
                for t in range(TT):
                    A((gate_a, gate_b)[c // 2][:, t, 512 * (c % 2):512 * (c % 2) + 512],
                      PS[:, 4 + 2 * (c % 2) + t, :], ACT.Sigmoid).then_inc(S["gate_read"], 1)
                split(q + 1, j)

            plain_splits(FIRST["mod4"], 4)

            def probT(n):
                act.wait_ge(S["s_tr"], n + 1)
                wait(act, S["s_o"], n - 1)
                A(pTb[n % 2][:, :], PS[:, 2 + n % 2, 0:384], ACT.Copy).then_inc(S["s_pT"], 1)

            def ya_high(p):
                act.wait_ge(S["s_o"], 2 * p + 2)
                A(yaTh[:, p, :], PS[:, 4 + p % 2, 0:T], ACT.Copy).then_inc(S["ya_hi"], 1)

            for n in range(H_A):
                act.wait_ge(S["s_max"], n + 1)
                wait(act, S["s_tr"], n - 1)
                for c, (a, b) in enumerate(((0, P), (P, 384))):
                    A(prob[n % 2][:, a:b], PS[:, n % 2, a:b], ACT.Exp, bias=nmx[:, 2 * n + c:2 * n + c + 1],
                      accum_out=sums[:, 2 * n + c:2 * n + c + 1]).then_inc(S["s_exp"], 1)
                if n >= 1:
                    probT(n - 1)
                if n % 2 == 1 and n >= 3:
                    ya_high((n - 3) // 2)
            probT(H_A - 1)
            ya_high(3)

            for n in range(4):
                A(rn[:, 2 * n:2 * n + 2, :], qkvT[:, 2 * n:2 * n + 2, :], ACT.Square).then_inc(S["l2_sq"], 1)
            act.wait_ge(S["small_read"], 4 + 1)
            A(ecum, ncum, ACT.Exp, scale=-1.0).then_inc(S["small_act"], 1)
            for t in range(TT):
                act.wait_ge(S["dec_arg"], t + 1)
                d = LT[:, 4 * t:4 * t + 4, :]
                A(d, d, ACT.Exp).then_inc(S["dec_exp"], 1)
            for t in range(TT):
                act.wait_ge(S["n_tr"], t + 1)
                A(NT[:, 4 * t:4 * t + 4, :], tr_bank(6 + t), ACT.Copy).then_inc(S["n_read"], 1)
            for m in range(1, 7):
                for t in range(TT):
                    act.wait_ge(S["u_mm"], 2 * m + t - 1)
                    if m >= 2:
                        act.wait_ge(S["vt_mm"], 2 * (m - 1) + t - 1)
                    A(Ub[:, 4 * t:4 * t + 4, :], tr_bank(t), ACT.Copy).then_inc(S["u_read"], 1)
            for n, dst, b in ((1, vn0, 6), (2, S1, 7), (3, R, 2)):
                act.wait_ge(S["vn_mm"], n)
                A(dst[:, :, :], tr_bank(b), ACT.Copy).then_inc(S["vn_sb"], 1)
            for t in range(TT):
                act.wait_ge(S["o_mm"], t + 1)
                A(ob[:, t, :], PS[:, 3 + t, :], ACT.Copy).then_inc(S["o_part"], 1)
            for t in range(TT):
                act.wait_ge(S["yb_tr"], t + 1)
                A(ybTh[:, :, t * P:(t + 1) * P], tr_bank(5 + t), ACT.Copy).then_inc(S["yb_hi"], 1)
            plain_splits(FIRST["up_a"], 4)
            to_T(5)
            plain_splits(FIRST["wout2"], 4)
            rms(1)
            to_T(6, 0)
            plain_splits(FIRST["mod5"], 4)

            act.wait_ge(S["rt_max"], 1)
            for t in range(TT):
                A(route[:, 1, t, 0:4], lg[:, t, 0:4], ACT.Exp, bias=rsc[:, 2 + t:3 + t], accum_out=rsc[:, 4 + t:5 + t]
                  ).then_inc(S["small_act"], 1)
            act.wait_ge(S["rt_max"], 2)
            A(rsc[:, 10:12], rsc[:, 10:12], ACT.Exp).then_inc(S["small_act"], 1)

            b = FIRST["moe"]

            def moe(nt):
                def high(e, n):
                    act.wait_ge(S["e_tr"], e + 1)
                    A(eTh[n % 2][:, :, 0:nt * P], PS[:, 2, 0:2 * nt * P].rearrange("p (c t) -> p c t", c=2), ACT.Copy
                      ).then_inc(S["act_hi"], 1)

                def silu(q, s, e, n):
                    act.wait_ge(S["unit_done"], 4 * q + s + 1)
                    for t in range(nt):
                        A(gbuf[n % 2][:, 256 * t:256 * t + 256], PS[:, n % 2 if nt == 1 else t, 0:256], ACT.Silu
                          ).then_inc(S["g_silu"], 1)

                def group_high(g):
                    for c in range(2):
                        act.wait_ge(S["tr_done"], 28 + 2 * g + c + 1)
                        A(hgh[:, 4 * c:4 * c + 4, :], tr_bank(7), ACT.Copy).then_inc(S["tr_hi"], 1)

                def scatter_now(g):
                    wait(act, S["sc_mm"], 2 * g)
                    A(scat[:, :], scatter[:, bass.ds(g, 1), :].rearrange("p o t -> p (o t)"), ACT.Copy
                      ).then_inc(S["scat_done"], 1)

                def group(g):
                    for n in range(8):
                        q, s = unit(b, max(3 * n - 1, 0), g, 24)
                        if n >= 1:
                            high(8 * g + n - 1, n - 1)
                        elif nt == 1 and not (isinstance(g, int) and g == 0):
                            scatter_now(g - 1)
                        split(q + 1, s)
                        q, s = unit(b, max(3 * n, 1), g, 24)
                        silu(q, s, 8 * g + n, n)
                        split(q + 1, s)
                        if n >= 1:
                            q, s = unit(b, 3 * n + 1, g, 24)
                            split(q + 1, s)
                    high(8 * g + 7, 7)
                    if nt == 1 and not (isinstance(g, int) and g == 3):
                        group_high(g + 1)
                    q, s = unit(b, 23, g, 24)
                    split(q + 1, s)

                if nt == 1:
                    group_high(0)
                    for n in range(2):
                        act.wait_ge(S["sct_mm"], n + 1)
                        A(scatter[:, 2 * n:2 * n + 2, :], PS[:, 5 + n, :].rearrange("p (g t) -> p g t", g=2), ACT.Copy
                          ).then_inc(S["sct_sb"], 1)
                    act.wait_ge(S["sct_sb"], 2)
                group(0)
                with act.Fori(1, 3) as g:
                    group(g)
                group(3)
                if nt == 1:
                    scatter_now(3)

            act.wait_ge(S["small_read"], 6 + 1)
            crowd = act.value_load(most[0:1, 0:1], min_val=0, max_val=T)
            with act.If(crowd <= CROWD):
                moe(1)
            with act.Else():
                moe(2)
            rms(2)

        @block.tensor
        def _(pe):
            mm = pe.matmul

            def product(out, a, b, start, stop):
                mm(out, a[0], b[0], start=start, stop=False)
                mm(out, a[0], b[1], start=False, stop=False)
                return mm(out, a[1], b[0], start=False, stop=stop)

            def unit_T(q, j, xT, outs):
                pe.wait_ge(S["w_lo_done"], 4 * q + j + 1)
                w = [t[:, :].rearrange("p (k f) -> p k f", k=KD) for t in (hi[j], lo[j])]
                for c in range(2):
                    for k in range(KD):
                        last = product(outs[c], [t[:, k, c * P:(c + 1) * P] for t in w],
                                       [f(k) for f in xT], k == 0, k == KD - 1)
                last.then_inc(S["unit_done"], 1)

            def unit_N(q, j, xT, k0, ks, outs, start, stop, nt=TT):
                pe.wait_ge(S["w_lo_done"], 4 * q + j + 1)
                w = [t[:, :].rearrange("p (k f) -> p k f", k=ks) for t in (hi[j], lo[j])]
                for t in range(nt):
                    for c in range(4 // ks):
                        for k in range(ks):
                            last = product(outs[c][t], [f(k0 + k)[:, t * P:(t + 1) * P] for f in xT],
                                           [s[:, k, 512 * c:512 * c + 512] for s in w],
                                           start and k == 0, stop and k == ks - 1)
                last.then_inc(S["unit_done"], 1)

            def to_T(r, source, ready, banks=4):
                for n in range(4):
                    t, k = n // 2, 4 * (n % 2)
                    if k == 0:
                        pe.wait_ge(S[ready[t][0]], ready[t][1])
                    for c in range(4):
                        last = pe.transpose(tr_bank(banks + n)[:, c, :], source[:, t, (k + c) * P:(k + c + 1) * P],
                                            ident)
                    last.then_inc(S["tr_done"], 1)
                pe.wait_ge(S["tr_lo"], 4 * r + 4)

            def tiles(*parts):
                return [lambda k, s=s: s[:, k, :] for s in parts]

            hT = tiles(hTh, hTl)
            to_T(0, h, (("x_in", 32), ("x_in", 32)))

            def small_product(outs, c0, n):
                for t in range(TT):
                    for k in range(KD):
                        last = product(outs[t], [f(k)[:, t * P:(t + 1) * P] for f in hT],
                                       [s[:, k, c0:c0 + n] for s in (wsh, wsl)], k == 0, k == KD - 1)
                return last

            def in_unit(q, j):
                unit_T(q, j, hT, [PS[:, j, c * T:(c + 1) * T] for c in range(2)])

            for j in range(RING):
                in_unit(0, j)
            with pe.Fori(1, 5) as i:
                for j in range(RING):
                    pe.wait_ge(S["conv_done"], 4 * i + j - 3)
                    in_unit(i, j)
            pe.wait_ge(S["small_lo_done"], 1)
            small_product([PS[:, 4, 0:32], PS[:, 4, 32:64]], 0, 32).then_inc(S["small_mm"], 1)
            for j in range(RING):
                pe.wait_ge(S["z_done"], j + 1)
                in_unit(5, j)

            da = da_all.rearrange("p (t n) -> p t n", t=TT)
            pe.wait_ge(S["da_done"], 1)
            mm(PS[:, 5, 0:32], triu, da[:, 0, :], start=True, stop=True)
            mm(PS[:, 5, 32:64], ones, da[:, 0, :], start=True, stop=False)
            mm(PS[:, 5, 32:64], triu, da[:, 1, :], start=False, stop=True)
            mm(PS[0:32, 6, 0:T], da[:, 0, :], triu_ones, start=True, stop=False)
            mm(PS[0:32, 6, P:T], da[:, 1, :], triu, start=False, stop=True).then_inc(S["small_mm"], 1)
            pe.wait_ge(S["small_read"], 2)

            pe.wait_ge(S["silu_done"], 16)
            for n in range(8):
                wait(pe, S["x_read"], n - 3)
                t, k = n // 4, 4 * (n % 4)
                for c in range(4):
                    last = pe.transpose(tr_bank(4 + n % 4)[:, c, :], xbcT[:, k + c, t * P:(t + 1) * P], ident)
                last.then_inc(S["xtr_done"], 1)
            pe.wait_ge(S["x_read"], 8)
            pe.wait_ge(S["z_done"], 8)

            def scores(g):
                wait(pe, S["cb_read"], g - 1)
                b, c = xbcT[:, 16 + g, :], xbcT[:, 24 + g, :]
                mm(PS[:, g % 2, 0:256], b[:, 0:P], c, start=True, stop=True)
                mm(PS[:, g % 2, 256:384], b[:, P:T], c[:, P:T], start=True, stop=True).then_inc(S["cb_mm"], 1)

            def running(hp):
                wait(pe, S["d_read"], hp - 1)
                for c in range(2):
                    o, one = PS[:, 2 + hp % 2, c * T:(c + 1) * T], pick[:, 2 * hp + c:2 * hp + c + 1].to_broadcast([32, P])
                    mm(o, one, csT_hi[:, :], start=True, stop=False)
                    last = mm(o, one, csT_lo[:, :], start=False, stop=True)
                last.then_inc(S["csb_done"], 1)

            def head_y(hp):
                pe.wait_ge(S["m_ready"], hp + 1)
                wait(pe, S["y_read"], hp - 1)
                for c in range(2):
                    o, n, m = PS[64 * c:64 * c + 64, 4 + hp % 2, 0:T], 2 * hp + c, dec[hp % 3][:, c, :]
                    mm(o, X[:, 0, 64 * n:64 * n + 64], m[:, 0:T], start=True, stop=False)
                    last = mm(o[:, P:T], X[:, 1, 64 * n:64 * n + 64], m[:, T:T + P], start=False, stop=True)
                last.then_inc(S["y_done"], 1)

            def group_sums(g):
                pe.wait_ge(S["sq_done"], g + 1)
                wait(pe, S["yn_done"], 2 * g - 2)
                for t in range(TT):
                    for c in range(2):
                        last = mm(PS[:, 6 + g % 2, t:t + 1], ysq[g % 2][:, c, t * P:(t + 1) * P], ones[:, 0:1],
                                  start=c == 0, stop=c == 1)
                last.then_inc(S["ms_done"], 1)

            def group_scale(g):
                pe.wait_ge(S["y_rstd"], g + 1)
                for t in range(TT):
                    last = mm(PS[:, 6 + g % 2, T + t * P:T + (t + 1) * P],
                              yrs[:, 2 * g + t:2 * g + t + 1].to_broadcast([P, P]), ident, start=True, stop=True)
                last.then_inc(S["ms_wide"], 1)

            scores(0)
            running(0)
            running(1)
            for hp in range(PAIRS):
                if hp % 2 == 1 and hp < PAIRS - 1:
                    scores((hp + 1) // 2)
                if hp < PAIRS - 2:
                    running(hp + 2)
                head_y(hp)
                if hp % 2 == 1 and hp >= 5:
                    group_sums((hp - 5) // 2)
                if hp % 2 == 0 and hp >= 6:
                    group_scale((hp - 6) // 2)

            def out_unit(n):
                pe.wait_ge(S["ylo"], 4 * (n % 4) + 4)
                q, j = unit(FIRST["out"], n)
                unit_N(q, j, [lambda k: yTh[:, k % 2, k // 2, :], lambda k: yTl[:, k, :]], 4 * (n % 4), 4,
                       [[PS[:, 2 * (n // 4) + t, :] for t in range(TT)]], n % 4 == 0, n % 4 == 3)

            group_scale(GROUPS - 3)
            group_sums(GROUPS - 2)
            pe.wait_ge(S["cb_read"], GROUPS)
            out_unit(0)
            group_scale(GROUPS - 2)
            group_sums(GROUPS - 1)
            out_unit(1)
            group_scale(GROUPS - 1)
            for n in range(2, 8):
                out_unit(n)

            def mod_units(k, bank):
                for n in range(4):
                    q, j = unit(FIRST[f"mod{k}"], n)
                    pe.wait_ge(S["w_lo_done"], 4 * q + j + 1)
                    for s in range(4):
                        a = [c[:, 4 * (n % 2) + s:4 * (n % 2) + s + 1].to_broadcast([P, P]) for c in (c_hi, c_lo)]
                        last = product(PS[:, bank + n // 2, :], a, [w[:, 512 * s:512 * s + 512] for w in (hi[j], lo[j])],
                                       n % 2 == 0 and s == 0, n % 2 == 1 and s == 3)
                    last.then_inc(S["unit_done"], 1)

            pe.wait_ge(S["c_ready"], 3)
            pe.wait_ge(S["yn_done"], XT_TILES)
            mod_units(0, 4)

            def mlp(m, first):
                outs = [[PS[:, 4 + 2 * c + t, :] for t in range(TT)] for c in range(2)]

                def up(q, s, n):
                    unit_T(q, s, hT, [PS[:, n % 4, c * T:(c + 1) * T] for c in range(2)])

                def down(q, s, n, start=False, stop=False):
                    unit_N(q, s, tiles(aTh[n % 2], aTl[n % 2]), 0, 2, outs, start, stop)

                def round_of(i, n, k):
                    for e in range(n, n + k):
                        if not (isinstance(i, int) and 4 * i + e < 4):
                            pe.wait_ge(S["relu_done"], CHUNKS * m + 4 * i + e - 3)
                        up(*unit(first, 2 * e - 1, i, 8), e)
                        if isinstance(i, int) and 4 * i + e == 1:
                            pe.wait_ge(S["mod_read"], 2 if m == 0 else 6)
                        pe.wait_ge(S["act_lo"], CHUNKS * m + 4 * i + e)
                        down(*unit(first, 2 * e, i, 8), e - 1, isinstance(i, int) and 4 * i + e == 1)

                up(*unit(first, 0), 0)
                round_of(0, 1, 4)
                with pe.Fori(1, 3) as i:
                    round_of(i, 1, 4)
                round_of(3, 1, 3)
                pe.wait_ge(S["act_lo"], CHUNKS * m + CHUNKS)
                down(*unit(first, 31), 15, False, True)

            to_T(1, h, (("h_ready", 1), ("h1_ready", 1)), 0)
            mlp(0, FIRST["mlp0"])
            pe.wait_ge(S["relu_done"], CHUNKS)
            mod_units(1, 2)
            to_T(2, h, (("h_ready", 2), ("h1_ready", 2)))

            for n in range(8):
                wait(pe, S["kq_read"], n - 3)
                if n == 2:
                    pe.wait_ge(S["mod_read"], 4)
                unit_T(*unit(FIRST["k"], n), hT, [PS[:, n % 4, c * T:(c + 1) * T] for c in range(2)])
            for n in range(4):
                unit_N(*unit(FIRST["v"], n), hT, 4 * (n % 2), 4,
                       [[PS[:, 4 + 2 * (n // 2) + t, :] for t in range(TT)]], n % 2 == 0, n % 2 == 1)

            def sb_scores(p):
                wait(pe, S["sb_zl"], p - 1)
                for c in range(2):
                    k, r, o = kT[64 * c:64 * c + 64, p, :], qT[64 * c:64 * c + 64, p, :], PS[:, 2 * (p % 2) + c, :]
                    mm(o[:, 0:T], k[:, 0:P], r, start=True, stop=True)
                    last = mm(o[:, T:T + P], k[:, P:T], r[:, P:T], start=True, stop=True)
                last.then_inc(S["sb_z"], 1)

            def sb_sums(p):
                pe.wait_ge(S["sb_mask"], p + 1)
                wait(pe, S["sb_lw"], p)
                for c in range(2):
                    o, n = PS[:, 4 + c, :], nbuf[p % 2][:, c, :]
                    mm(o[:, 0:T], later, n[:, 0:T], start=True, stop=False)
                    mm(o[:, P:T], ones, n[:, T:T + P], start=False, stop=True)
                    last = mm(o[:, T:T + P], later, n[:, T:T + P], start=True, stop=True)
                last.then_inc(S["sb_after"], 1)

            def sb_values(p):
                pe.wait_ge(S["sb_wm"], p + 1)
                wait(pe, S["oT_lo_done"], p - 1)
                for c in range(2):
                    o, n, w = PS[64 * c:64 * c + 64, 6 + p % 2, 0:T], 64 * (2 * p + c), wbuf[p % 2][:, c, :]
                    mm(o, V[:, 0, n:n + 64], w[:, 0:T], start=True, stop=False)
                    last = mm(o[:, P:T], V[:, 1, n:n + 64], w[:, T:T + P], start=False, stop=True)
                last.then_inc(S["sb_o"], 1)

            pe.wait_ge(S["kq_read"], 8)
            pe.wait_ge(S["v_read"], 4)
            sb_scores(0)
            for p in range(SB_PAIRS):
                if p < SB_PAIRS - 1:
                    sb_scores(p + 1)
                sb_sums(p)
                if p >= 1:
                    sb_values(p - 1)
            sb_values(SB_PAIRS - 1)
            for n in range(4):
                pe.wait_ge(S["oT_lo_done"], 4 * (n % 2) + 4)
                unit_N(*unit(FIRST["o"], n), tiles(oTh, oTl), 4 * (n % 2), 4,
                       [[PS[:, 2 * (n // 2) + t, :] for t in range(TT)]], n % 2 == 0, n % 2 == 1)

            mod_units(2, 4)
            to_T(3, h, (("h_ready", 3), ("h1_ready", 3)), 0)
            mlp(1, FIRST["mlp1"])
            pe.wait_ge(S["relu_done"], 2 * CHUNKS)
            mod_units(3, 0)

            to_T(4, hn, (("h_ready", 4 + 1), ("h1_ready", 4 + 1)))
            pe.wait_ge(S["mod_read"], 8)
            small_product([PS[:, 6, 0:8], PS[:, 6, 8:16]], 32, 8).then_inc(S["small_mm"], 1)
            pe.wait_ge(S["tab_in"], 32)
            pe.wait_ge(S["pool_init"], 1 + 1)
            mm(PS[0:H_A, 7, 0:TABLE_W], relb[:, :], tabs[:, 0:TABLE_W], start=True, stop=True
               ).then_inc(S["small_mm"], 1)
            for n in range(4):
                unit_T(*unit(FIRST["qa"], n), hT, [PS[:, n, c * T:(c + 1) * T] for c in range(2)])
            for n in range(2):
                unit_N(*unit(FIRST["va"], n), hT, 4 * n, 4, [[PS[:, 4 + t, :] for t in range(TT)]], n == 0, n == 1)
            for n in range(6):
                pe.wait_ge(*(S["qk_read"], n + 1) if n < 4 else (S["conv_done"], 16 + n - 3))
                unit_T(*unit(FIRST["conv2"], n), hT, [PS[:, n % 4, c * T:(c + 1) * T] for c in range(2)])
            pe.wait_ge(S["small_read"], 2 + 1)
            pe.wait_ge(S["tab_sb"], 1)
            for n in range(2):
                unit_N(*unit(FIRST["zb"], n), hT, 4 * n, 4, [[PS[:, 6 + t, :] for t in range(TT)]], n == 0, n == 1)
            for n in range(8):
                c = n // 2
                if n % 2 == 0:
                    pe.wait_ge(*((S["v_read"], 4 + 2), (S["z_done"], 8 + 2), (S["gate_read"], 2), (S["gate_read"], 4))[c])
                unit_N(*unit(FIRST["gate"], n), hT, 4 * (n % 2), 4,
                       [[PS[:, 4 + 2 * (c % 2) + t, :] for t in range(TT)]], n % 2 == 0, n % 2 == 1)

            def s_scores(n):
                p, r = n // 2, slice(64 * (n % 2), 64 * (n % 2) + 64)
                wait(pe, S["s_exp"], 2 * n - 2)
                s = PS[:, n % 2, :]
                mm(s[:, 0:P], qaT[r, p, 0:P], kaT[r, p, 0:P], start=True, stop=False)
                mm(s[:, 0:P], anti, hank[:, n, 0:P], start=False, stop=True)
                mm(s[:, P:384], qaT[r, p, P:T], kaT[r, p, :], start=True, stop=False)
                mm(s[:, P:384], anti, hank[:, n, P:384], start=False, stop=True).then_inc(S["s_mm"], 1)

            def s_probT(n):
                pe.wait_ge(S["s_norm"], n + 1)
                wait(pe, S["s_pT"], n - 1)
                for c in range(3):
                    last = pe.transpose(tr_bank(2 + n % 2)[:, c, :], prob[n % 2][:, c * P:(c + 1) * P], ident)
                last.then_inc(S["s_tr"], 1)

            def s_values(n):
                p = n // 2
                pe.wait_ge(S["s_pT"], n + 1)
                wait(pe, S["ya_lo"], p - 1)
                o, f = PS[64 * (n % 2):64 * (n % 2) + 64, 4 + p % 2, 0:T], slice(64 * n, 64 * n + 64)
                mm(o, va[:, 0, f], pTb[n % 2][:, 0:T], start=True, stop=False)
                mm(o[:, P:T], va[:, 1, f], pTb[n % 2][:, T:384], start=False, stop=True).then_inc(S["s_o"], 1)

            pe.wait_ge(S["conv_done"], 16 + 6)
            mod_units(4, 2)
            pe.wait_ge(S["mod_read"], 10)
            pe.wait_ge(S["gate_read"], 8)
            pe.wait_ge(S["hank_in"], 32)
            s_scores(0)
            for n in range(H_A):
                if n < H_A - 1:
                    s_scores(n + 1)
                s_probT(n)
                if n >= 1:
                    s_values(n - 1)
            s_values(H_A - 1)

            for n in range(8):
                pe.wait_ge(S["l2_sq"], n // 2 + 1)
                for t in range(TT):
                    last = mm(PS[:, 0, 2 * n + t:2 * n + t + 1], rn[:, n, t * P:(t + 1) * P], ones[:, 0:1],
                              start=True, stop=True)
            last.then_inc(S["small_mm"], 1)
            pe.wait_ge(S["g_done"], 1)
            pe.wait_ge(S["ya_lo"], 4)
            for t in range(TT):
                last = mm(PS[:, 1, 4 * t:4 * t + 4], triu, gdec[:, 4 * t:4 * t + 4], start=True, stop=True)
            last.then_inc(S["small_mm"], 1)
            for t in range(TT):
                for n in range(H_B):
                    last = mm(PS[:, 4 + t, n * P:(n + 1) * P], gdec[:, 4 * t + n:4 * t + n + 1].to_broadcast([P, P]),
                              triu, start=True, stop=True)
                last.then_inc(S["gb_mm"], 1)
            pe.wait_ge(S["l2_rstd"], 1)
            pe.wait_ge(S["small_read"], 4 + 1)
            for n in range(8):
                b = (0, 1, 2, 3)[n // 2]
                for t in range(TT):
                    last = mm(PS[:, b, (n % 2) * T + t * P:(n % 2) * T + (t + 1) * P],
                              l2r[:, 2 * n + t:2 * n + t + 1].to_broadcast([P, P]), ident, start=True, stop=True)
                if n % 2 == 1:
                    last.then_inc(S["l2_bc"], 1)
            pe.wait_ge(S["l2_done"], 4)

            def tile(n, t):
                return qkvT[:, n, t * P:(t + 1) * P]

            for t in range(TT):
                for n in range(H_B):
                    last = mm(tr_bank(t)[:, n, :], tile(4 + n, t), tile(4 + n, t), start=True, stop=True)
                last.then_inc(S["kk_mm"], 1)
            for t in range(TT):
                for n in range(H_B):
                    last = mm(tr_bank(2 + t)[:, n, :], tile(4 + n, t), tile(n, t), start=True, stop=True)
                last.then_inc(S["qk_mm"], 1)
            pe.wait_ge(S["silu_done"], 16 + 6)
            for b, n0, t in ((6, 8, 0), (7, 8, 1), (0, 4, 0)):
                if b == 0:
                    pe.wait_ge(S["kk_read"], 1)
                for n in range(H_B):
                    last = pe.transpose(tr_bank(b)[:, n, :], tile(n0 + n, t), ident)
                last.then_inc(S["vk_tr"], 1)
            for t in range(TT):
                pe.wait_ge(S["kk_masked"], t + 1)
                for n in range(H_B):
                    last = pe.transpose(tr_bank(4 + t)[:, n, :], Ub[:, 4 * t + n, :], ident)
                last.then_inc(S["m_tr"], 1)
            pe.wait_ge(S["vk_read"], 3)
            for t in range(TT):
                pe.wait_ge(S["m_read"], t + 1)
                for n in range(H_B):
                    last = pe.transpose(tr_bank(6 + t)[:, n, :], Xi[:, 4 * t + n, :], ident)
                last.then_inc(S["n_tr"], 1)

            def four(b, t, lhsT, rhs):
                for n in range(H_B):
                    last = mm(tr_bank(b)[:, n, :], lhsT(4 * t + n), rhs(4 * t + n), start=True, stop=True)
                return last

            for m in range(1, 7):
                for t in range(TT):
                    pe.wait_ge(S["lt_done"], 2 * m + t - 1)
                    pe.wait_ge(S["x_upd"], 2 * m + t - 1)
                    four(t, t, lambda n: LT[:, n, :], lambda n: Xi[:, n, :]).then_inc(S["u_mm"], 1)
                for t in range(TT):
                    pe.wait_ge(S["u_read"], 2 * m + t - 1)
                    if m < 6:
                        four(2 + t, t, lambda n: XiT[:, n, :], lambda n: Ub[:, n, :])
                    four(4 + t, t, lambda n: Ub[:, n, :], lambda n: XiT[:, n, :]).then_inc(S["vt_mm"], 1)
            pe.wait_ge(S["x_upd"], 14)
            four(6, 0, lambda n: XiT[:, n, :], lambda n: R[:, n, :]).then_inc(S["vn_mm"], 1)
            pe.wait_ge(S["vn_sb"], 1)
            four(7, 0, lambda n: kd[:, n, :], lambda n: vn0[:, n, :]).then_inc(S["vn_mm"], 1)
            pe.wait_ge(S["vn_sb"], 2)
            four(0, 0, lambda n: tile(4 + n, 1), lambda n: S1[:, n, :]).then_inc(S["ks_mm"], 1)
            four(1, 0, lambda n: tile(n, 1), lambda n: S1[:, n, :]).then_inc(S["ks_mm"], 1)
            four(3, 0, lambda n: PT[:, n, :], lambda n: vn0[:, n, :]).then_inc(S["o_mm"], 1)
            pe.wait_ge(S["r1_done"], 1)
            four(2, 1, lambda n: XiT[:, n, :], lambda n: R[:, n - 4, :]).then_inc(S["vn_mm"], 1)
            pe.wait_ge(S["vn_sb"], 3)
            four(4, 1, lambda n: PT[:, n, :], lambda n: R[:, n - 4, :]).then_inc(S["o_mm"], 1)
            pe.wait_ge(S["o_scaled"], 1)
            for t in range(TT):
                for n in range(H_B):
                    last = pe.transpose(tr_bank(5 + t)[:, n, :], ob[:, t, n * P:(n + 1) * P], ident)
                last.then_inc(S["yb_tr"], 1)
            pe.wait_ge(S["yb_lo"], 2)
            for n in range(4):
                unit_N(*unit(FIRST["up_a"], n), (tiles(yaTh, yaTl), tiles(ybTh, ybTl))[n // 2], 0, 4,
                       [[PS[:, 4 * (n // 2) + 2 * (n % 2) + t, :] for t in range(TT)]], True, True)
            to_T(5, mm_a, (("mix_ready", 2), ("mix_ready", 2)))
            for n in range(4):
                unit_N(*unit(FIRST["wout2"], n), hT, 4 * (n % 2), 4,
                       [[PS[:, 2 * (n // 2) + t, :] for t in range(TT)]], n % 2 == 0, n % 2 == 1)
            mod_units(5, 4)
            to_T(6, hn, (("h_ready", 4 + 2), ("h1_ready", 4 + 2)), 0)
            small_product([PS[:, 0, 0:36], PS[:, 0, 64:100]], 40, 36).then_inc(S["small_mm"], 1)
            pe.wait_ge(S["rt_done"], 1)
            oh = route[:, 0, :, 0:4]
            mm(PS[:, 2, 0:4], before, oh[:, 0, :], start=True, stop=True)
            mm(PS[:, 2, 4:8], ones, oh[:, 0, :], start=True, stop=False)
            mm(PS[:, 2, 4:8], before, oh[:, 1, :], start=False, stop=True)
            mm(PS[:, 2, 8:12], ones, oh[:, 0, :], start=True, stop=False)
            mm(PS[:, 2, 8:12], ones, oh[:, 1, :], start=False, stop=True).then_inc(S["small_mm"], 1)

            b = FIRST["moe"]

            def moe(nt):
                xT = tiles(hgh, hgl) if nt == 1 else hT
                outs = [[PS[:, 3 + (c if nt == 1 else 2 * c + t), :] for t in range(nt)] for c in range(2)]

                def gate_up(q, s, half, n):
                    unit_N(q, s, xT, 4 * half, 4, [[PS[:, n % 2 if nt == 1 else t, :] for t in range(nt)]],
                           half == 0, half == 1, nt)

                def transposes(e, n):
                    pe.wait_ge(S["gu_done"], nt * (e + 1))
                    if not (isinstance(e, int) and e == 0):
                        pe.wait_ge(S["act_lo"], 32 + e)
                    for t in range(nt):
                        for c in range(2):
                            last = pe.transpose(PS[:, 2, (nt * c + t) * P:(nt * c + t + 1) * P],
                                                ubuf[n % 2][:, 256 * t + c * P:256 * t + (c + 1) * P], ident)
                    last.then_inc(S["e_tr"], 1)

                def down(q, s, e, n, start, stop):
                    pe.wait_ge(S["act_lo"], 32 + e + 1)
                    unit_N(q, s, tiles(eTh[n % 2], eTl[n % 2]), 0, 2, outs, start, stop, nt)

                def gather_group(g):
                    for half in range(2):
                        if half or not (isinstance(g, int) and g == 0):
                            pe.wait_ge(S["tr_lo"], 28 + 2 * g + half)
                        for c in range(4):
                            for t in range(TT):
                                d = (4 * half + c) * P
                                last = mm(tr_bank(7)[:, c, :], hn[:, t, d:d + P],
                                          gather[:, bass.ds(g, 1), t, :].rearrange("p o s -> p (o s)"),
                                          start=t == 0, stop=t == 1)
                        last.then_inc(S["tr_done"], 1)

                def scatter_group(g):
                    pe.wait_ge(S["yg_sb"], g + 1)
                    pe.wait_ge(S["scat_done"], g + 1)
                    for t in range(TT):
                        if t or not (isinstance(g, int) and g == 0):
                            pe.wait_ge(S["sc_read"], 2 * g + t)
                        for c in range(2):
                            last = mm(PS[:, 5 + c, :], scat[:, t * P:(t + 1) * P], yg[:, 512 * c:512 * c + 512],
                                      start=True, stop=True)
                        last.then_inc(S["sc_mm"], 1)

                def group(g):
                    first, end = (isinstance(g, int) and g == 0), (isinstance(g, int) and g == 3)
                    start, stop = (True, True) if nt == 1 else (first, end)
                    if nt == 1:
                        pe.wait_ge(S["tr_lo"], 28 + 2 * g + 2)
                    for n in range(8):
                        e = 8 * g + n
                        if nt == 1 and not (first and n < 2):
                            pe.wait_ge(S["gu_done"], e - 1)
                        if nt == 2 and not (first and n < 1):
                            pe.wait_ge(S["gu_done"], 2 * e)
                        gate_up(*unit(b, max(3 * n - 1, 0), g, 24), 0, n)
                        if n >= 1:
                            transposes(e - 1, n - 1)
                        gate_up(*unit(b, max(3 * n, 1), g, 24), 1, n)
                        if n == 0 and nt == 1 and not first:
                            scatter_group(g - 1)
                        if n >= 1:
                            down(*unit(b, 3 * n + 1, g, 24), e - 1, n - 1, start and n == 1, False)
                    transposes(8 * g + 7, 7)
                    if nt == 1 and not end:
                        gather_group(g + 1)
                    down(*unit(b, 23, g, 24), 8 * g + 7, 7, False, stop)

                pe.wait_ge(S["mod_read"], 12)
                if nt == 1:
                    pe.wait_ge(S["gather_ready"], 1)
                    gather_group(0)
                    pe.wait_ge(S["gather_ready"], 2)
                    for g in range(4):
                        for t in range(TT):
                            last = mm(PS[:, 2, 8 * g:8 * g + 8], gather[:, g, t, :], comb[:, t, 8 * g:8 * g + 8],
                                      start=t == 0, stop=t == 1)
                    last.then_inc(S["small_mm"], 1)
                    for g in range(4):
                        for t in range(TT):
                            o = (g % 2) * T + t * P
                            last = pe.transpose(PS[:, 5 + g // 2, o:o + P], gather[:, g, t, :], ident)
                        if g % 2:
                            last.then_inc(S["sct_mm"], 1)
                group(0)
                with pe.Fori(1, 3) as g:
                    group(g)
                group(3)
                if nt == 1:
                    scatter_group(3)

            pe.wait_ge(S["small_read"], 6 + 1)
            crowd = pe.value_load(most[0:1, 0:1], min_val=0, max_val=T)
            with pe.If(crowd <= CROWD):
                moe(1)
            with pe.Else():
                moe(2)

        @block.vector
        def _(dve):
            tt, ts, stt = dve.tensor_tensor, dve.tensor_scalar, dve.scalar_tensor_tensor
            step = Steps(dve, S["dve_step"])

            def split(q, j):
                if isinstance(q, int) and 4 * q + j >= UNITS:
                    return
                dve.wait_ge(S["w_hi_done"], 4 * q + j + 1)
                tt(lo[j][:, :], raw[j][:, :], hi[j][:, :].bitcast(F32), ALU.subtract).then_inc(S["w_lo_done"], 1)

            def to_T(r, banks=4):
                for n in range(4):
                    dve.wait_ge(S["tr_hi"], 4 * r + n + 1)
                    a = (slice(None), slice(4 * (n % 2), 4 * (n % 2) + 4), slice(n // 2 * P, (n // 2 + 1) * P))
                    tt(hTl[a], tr_bank(banks + n), hTh[a].bitcast(F32), ALU.subtract).then_inc(S["tr_lo"], 1)

            def softplus(out, n, s, before=0):
                dve.wait_ge(s, before + 1)
                step(ts(su[:, 0:n], st[:, 0:n], 1.0, None, ALU.add))
                step(ts(sv[:, 0:n], su[:, 0:n], -1.0, None, ALU.add))
                step(tt(sv[:, 0:n], st[:, 0:n], sv[:, 0:n], ALU.subtract))
                step(dve.reciprocal(su[:, 0:n], su[:, 0:n]))
                step(tt(sv[:, 0:n], sv[:, 0:n], su[:, 0:n], ALU.mult))
                dve.wait_ge(s, before + 2)
                step(tt(sv[:, 0:n], sv[:, 0:n], sw[:, 0:n], ALU.add))
                step(stt(out, sx[:, 0:n], 0.0, sv[:, 0:n], ALU.max, ALU.add))

            to_T(0)
            for j in range(RING):
                split(0, j)
            dve.wait_ge(S["small_hi_done"], 2)
            tt(small_lo[:, :], small_raw[:, :], small_hi[:, :].bitcast(F32), ALU.subtract
               ).then_inc(S["small_lo_done"], 1)
            dve.wait_ge(S["c_ready"], 2)
            tt(c_lo[:, :], cc["c"], c_hi[:, :].bitcast(F32), ALU.subtract).then_inc(S["c_ready"], 1)

            with dve.Fori(0, 4) as i:
                for j in range(RING):
                    dve.wait_ge(S["conv_first"], 8 * i + 2 * j + 2)
                    for c in range(2):
                        ct = 8 * i + 2 * j + c
                        for b in range(1, 4):
                            a = acc[j % 2][:, c, b:T]
                            last = stt(a, PS[:, j, c * T:(c + 1) * T - b], cc["conv_w"][:, bass.ds(4 * ct + 3 - b, 1)],
                                       a, ALU.mult, ALU.add)
                            if not (c == 1 and b == 3):
                                last.then_inc(S["conv_tap"], 1)
                                dve.wait_ge(S["conv_tap"], 20 * i + 5 * j + 3 * c + b)
                    last.then_inc(S["conv_done"], 1)
                    split(i + 1, j)
            for j in range(RING):
                split(5, j)

            dve.wait_ge(S["small_mm"], 1)
            tt(sx.rearrange("p (t n) -> p t n", t=TT), PS[:, 4, 0:64].rearrange("p (t n) -> p t n", t=TT),
               rr["dt_bias"].rearrange("p (o n) -> p o n", o=1).to_broadcast([P, TT, 32]), ALU.add
               ).then_inc(S["dt_read"], 1)
            softplus(dt_all, 64, S["dt_exp"])
            stt(da_all.rearrange("p (t n) -> p t n", t=TT), dt_all.rearrange("p (t n) -> p t n", t=TT), -1.0,
                rr["a_log"].rearrange("p (o n) -> p o n", o=1).to_broadcast([P, TT, 32]), ALU.mult, ALU.mult
                ).then_inc(S["da_done"], 1)
            for j in range(RING):
                split(6, j)

            dve.wait_ge(S["small_mm"], 1 + 1)
            ts(ncs, PS[:, 5, 0:64], -1.0, None, ALU.mult).then_inc(S["small_read"], 1)
            dve.wait_ge(S["csT_done"], 1)
            tt(csT_lo[:, :], PS[0:32, 6, 0:T], csT_hi[:, :].bitcast(F32), ALU.subtract).then_inc(S["small_read"], 1)
            for n in range(8):
                t, k = n // 4, 4 * (n % 4)
                dve.wait_ge(S["xtr_done"], n + 1)
                tt(X[:, t, k * P:(k + 4) * P].rearrange("p (n d) -> p n d", d=64),
                   PS[:, 4 + n % 4, :].rearrange("p (n d) -> p n d", d=64),
                   dt_all[:, 32 * t + 2 * k:32 * t + 2 * k + 8].rearrange("p (n o) -> p n o", o=1
                                                                         ).to_broadcast([P, 8, 64]),
                   ALU.mult).then_inc(S["x_read"], 1)

            def decay_arg(hp):
                dve.wait_ge(S["csb_done"], hp + 1)
                wait(dve, S["y_done"], hp - 2)
                for c in range(2):
                    n, o = 2 * hp + c, PS[:, 2 + hp % 2, c * T:(c + 1) * T]
                    stt(dec[hp % 3][:, c, 0:T], o, ncs[:, n:n + 1], mask_neg, ALU.add, ALU.add)
                    last = stt(dec[hp % 3][:, c, T:T + P], o[:, P:T], ncs[:, 32 + n:33 + n], mask_neg[:, 0:P],
                               ALU.add, ALU.add)
                last.then_inc(S["d_read"], 1)

            def skip(hp):
                dve.wait_ge(S["y_done"], hp + 1)
                wait(dve, S["yg_done"], hp - 1)
                stt(ysk[hp % 2][:, :], xbcT[:, hp, :], cc["skip"][:, hp:hp + 1], PS[:, 4 + hp % 2, 0:T], ALU.mult,
                    ALU.add).then_inc(S["y_read"], 1)

            def mean_square(g):
                dve.wait_ge(S["ms_done"], g + 1)
                ts(yrs[:, 2 * g:2 * g + 2], PS[:, 6 + g % 2, 0:2], 1.0 / 256, RMS_EPS, ALU.mult, ALU.add
                   ).then_inc(S["ms_read"], 1)

            def y_norm(g):
                dve.wait_ge(S["ms_wide"], g + 1)
                for c in range(2):
                    ct = 2 * g + c
                    stt(zT[:, ct, :], zT[:, ct, :], cc["norm_w"][:, ct:ct + 1], PS[:, 6 + g % 2, T:2 * T], ALU.mult,
                        ALU.mult).then_inc(S["yn_done"], 1)

            def y_low(g):
                for c in range(2):
                    dve.wait_ge(S["yhi"], 2 * g + c + 1)
                    tt(yTl[:, 2 * g + c, :], zT[:, 2 * g + c, :], yTh[:, c, g, :].bitcast(F32), ALU.subtract
                       ).then_inc(S["ylo"], 1)

            decay_arg(0)
            decay_arg(1)
            for hp in range(PAIRS):
                if hp < PAIRS - 2:
                    decay_arg(hp + 2)
                skip(hp)
                if hp % 2 == 1 and hp >= 5:
                    mean_square((hp - 5) // 2)
                if hp % 2 == 0 and hp >= 6:
                    y_norm((hp - 6) // 2)
                if hp % 2 == 1 and hp >= 9:
                    y_low((hp - 9) // 2)
            y_norm(GROUPS - 3)
            y_low(GROUPS - 4)
            mean_square(GROUPS - 2)
            y_low(GROUPS - 3)
            y_norm(GROUPS - 2)
            mean_square(GROUPS - 1)
            y_low(GROUPS - 2)
            y_norm(GROUPS - 1)
            y_low(GROUPS - 1)

            def plain_splits(first, count):
                for p in range(count):
                    q, j = unit(first, p)
                    split(q + 1, j)

            def layer_norm(r, last_unit, banks):
                dve.wait_ge(S["unit_done"], last_unit)
                for t in range(TT):
                    for c in range(2):
                        s = slice(512 * c, 512 * c + 512)
                        last = stt(pre[:, t, s], h[:, t, s], ALPHA, PS[:, banks + 2 * c + t, :], ALU.mult, ALU.add)
                    step(last)
                    for c in range(2):
                        last = dve.bn_stats(stats[:, t, c, :], pre[:, t, 512 * c:512 * c + 512])
                    step(last)
                    step(dve.bn_aggr(mv[:, t, :], stats[:, t, :, :].rearrange("p c s -> p (c s)")))
                    ts(veps[:, t:t + 1], mv[:, t, 1:2], LN_EPS, None, ALU.add).then_inc(S["ln_var"], 1)
                for t in range(TT):
                    dve.wait_ge(S["ln_rstd"], TT * r + t + 1)
                    stt(nmean[:, t:t + 1], mv[:, t, 0:1], -1.0, rstd[:, t:t + 1], ALU.mult, ALU.mult
                        ).then_inc(S["ln_norm_in"], 1)
                dve.wait_ge(S["row_in"], 16 * r + 16)
                dve.wait_ge(S["ln_norm"], TT * r + 1)
                tt(pre[:, 0, :], pre[:, 0, :], ln_row[:, 0, :], ALU.mult).then_inc(S["ln_gain"], 1)
                dve.wait_ge(S["ln_norm"], TT * r + 2)
                step(tt(pre[:, 1, :], pre[:, 1, :], ln_row[:, 0, :], ALU.mult))
                tt(h[:, 1, :], pre[:, 1, :], ln_row[:, 1, :], ALU.add).then_inc(S["h1_ready"], 1)

            def mlp(m, first):
                def square(j, n):
                    dve.wait_ge(S["relu_done"], j + 1)
                    tt(sbuf[n % 2][:, :], rbuf[n % 2][:, :], rbuf[n % 2][:, :], ALU.mult).then_inc(S["sq2_done"], 1)

                def low(j, n):
                    dve.wait_ge(S["act_hi"], j + 1)
                    tt(aTl[n % 2][:, :, :], sbuf[n % 2][:, :].rearrange("p (c t) -> p c t", c=2),
                       aTh[n % 2][:, :, :].bitcast(F32), ALU.subtract).then_inc(S["act_lo"], 1)

                j0 = CHUNKS * m
                square(j0, 0)
                q, s = unit(first, 0)
                split(q + 1, s)
                low(j0, 0)

                def round_of(i, n, k):
                    for e in range(n, n + k):
                        q, s = unit(first, 2 * e - 1, i, 8)
                        square(j0 + e + 4 * i, e)
                        split(q + 1, s)
                        low(j0 + e + 4 * i, e)
                        q, s = unit(first, 2 * e, i, 8)
                        split(q + 1, s)

                with dve.Fori(0, 3) as i:
                    round_of(i, 1, 4)
                round_of(3, 1, 3)
                q, s = unit(first, 31)
                split(q + 1, s)

            def mod_read(k, bank):
                dve.wait_ge(S["mod_in"], 16)
                dve.wait_ge(S["unit_done"], FIRST[f"mod{k}"] + 4)
                for c in range(2):
                    a = mod[:, k, 512 * c:512 * c + 512]
                    tt(a, a, PS[:, bank + c, :], ALU.add).then_inc(S["mod_read"], 1)
                plain_splits(FIRST[f"mod{k}"], 4)

            plain_splits(FIRST["out"], 8)
            layer_norm(0, FIRST["mod0"], 0)
            to_T(1, 0)
            mod_read(0, 4)
            mlp(0, FIRST["mlp0"])
            layer_norm(1, FIRST["mod1"], 4)
            to_T(2)
            mod_read(1, 2)
            plain_splits(FIRST["k"], 12)

            def o_low(p):
                dve.wait_ge(S["oT_hi_done"], p + 1)
                tt(oTl[:, p, :], PS[:, 6 + p % 2, 0:T], oTh[:, p, :].bitcast(F32), ALU.subtract
                   ).then_inc(S["oT_lo_done"], 1)

            for p in range(SB_PAIRS + 1):
                if p < SB_PAIRS:
                    z, n = PS[:, 2 * (p % 2):2 * (p % 2) + 2, 0:384], nbuf[p % 2]
                    dve.wait_ge(S["sb_abs"], p + 1)
                    wait(dve, S["sb_after"], p - 1)
                    stt(n[:, :, :], z, 0.0, abuf[p % 2][:, :, :], ALU.max, ALU.add).then_inc(S["sb_nlo"], 1)
                    dve.wait_ge(S["sb_nlo"], p + 1)
                    wait(dve, S["sb_o"], p - 1)
                    tt(wbuf[p % 2][:, :, :], z, n[:, :, :], ALU.subtract).then_inc(S["sb_zl"], 1)
                if p >= 1:
                    dve.wait_ge(S["sb_after"], p)
                    w = wbuf[(p - 1) % 2][:, :, :]
                    tt(w, w, PS[:, 4:6, 0:384], ALU.subtract).then_inc(S["sb_lw"], 1)
                if p >= 3:
                    o_low(p - 3)
            for p in range(SB_PAIRS - 2, SB_PAIRS):
                o_low(p)
            plain_splits(FIRST["o"], 4)
            layer_norm(2, FIRST["mod2"], 0)
            to_T(3, 0)
            mod_read(2, 4)
            mlp(1, FIRST["mlp1"])

            def norm_gain(r):
                dve.wait_ge(S["rms_rows_in"], 16 * r + 16)
                dve.wait_ge(S["mod_read"], 4 if r == 0 else 10)
                step(stt(mod[:, 3 * r + 1, :], mod[:, 3 * r + 1, :], 1.0, rms_row[r][:, :], ALU.add, ALU.mult))

            norm_gain(0)
            layer_norm(3, FIRST["mod3"], 4)

            def rms(r):
                for t in range(TT):
                    dve.wait_ge(S["rms_sq"], TT * r + t + 1)
                    ts(veps[:, t:t + 1], ms8[:, t:t + 1], 1.0 / D, EPS2, ALU.mult, ALU.add).then_inc(S["ln_var"], 1)
                for t in range(TT):
                    dve.wait_ge(S["ln_rstd"], 8 + TT * r + t + 1)
                    if r < 2:
                        normed = stt(hn[:, t, :], h[:, t, :], rstd[:, t:t + 1], mod[:, 3 * r + 1, :], ALU.mult,
                                     ALU.mult)
                        if t == 0:
                            normed.then_inc(S["rms_t"], 1)
                        else:
                            step(normed)
                            tt(hn[:, 1, :], hn[:, 1, :], mod[:, 3 * r, :], ALU.add).then_inc(S["h1_ready"], 1)
                    else:
                        dve.wait_ge(S["final_in"], 16)
                        stt(fin[:, t, :], h[:, t, :], rstd[:, t:t + 1], final_row[:, :], ALU.mult, ALU.mult
                            ).then_inc(S["fin_ready"], 1)

            rms(0)
            to_T(4)
            mod_read(3, 0)
            dve.wait_ge(S["small_mm"], 2 + 1)
            dve.tensor_copy(bg, PS[:, 6, 0:16].rearrange("p (t n) -> p t n", t=TT)).then_inc(S["small_read"], 1)
            dve.wait_ge(S["small_read"], 2 + 1)
            tt(sx[:, 0:8].rearrange("p (t n) -> p t n", t=TT), bg[:, :, 4:8],
               rr["dt_bias2"].rearrange("p (o n) -> p o n", o=1).to_broadcast([P, TT, 4]), ALU.add
               ).then_inc(S["small_read"], 1)
            softplus(gdec, 8, S["dt_exp"], 2)
            stt(gdec.rearrange("p (t n) -> p t n", t=TT), gdec.rearrange("p (t n) -> p t n", t=TT), -1.0,
                rr["a_log2"].rearrange("p (o n) -> p o n", o=1).to_broadcast([P, TT, 4]), ALU.mult, ALU.mult
                ).then_inc(S["g_done"], 1)
            dve.wait_ge(S["small_mm"], 3 + 1)
            dve.tensor_copy(tabs[0:H_A, TABLE_W:2 * TABLE_W], PS[0:H_A, 7, 0:TABLE_W]).then_inc(S["tab_sb"], 1)
            plain_splits(FIRST["qa"], 6)
            taps = 0
            for n in range(6):
                q, j = unit(FIRST["conv2"], n)
                dve.wait_ge(S["conv_first"], 32 + 2 * n + 2)
                for c in range(2):
                    for b in range(1, 4):
                        k = 4 * (2 * n + c) + 3 - b
                        a = acc2[n % 2][:, c, b:T]
                        last = stt(a, PS[:, n % 4, c * T:(c + 1) * T - b], cc["conv2_w"][:, k:k + 1], a, ALU.mult,
                                   ALU.add)
                        if not (c == 1 and b == 3):
                            step(last)
                last.then_inc(S["conv_done"], 1)
                split(q + 1, j)
            plain_splits(FIRST["zb"], 10)
            mod_read(4, 2)

            def s_max(n):
                dve.wait_ge(S["s_mm"], n + 1)
                for c, (a, b) in enumerate(((0, P), (P, 384))):
                    last = dve.reduce_max(mx[:, 2 * n + c:2 * n + c + 1], PS[:, n % 2, a:b], axis=AX_X)
                step(last)
                ts(nmx[:, 2 * n:2 * n + 2], mx[:, 2 * n:2 * n + 2], -1.0, None, ALU.mult).then_inc(S["s_max"], 1)

            def ya_low(p):
                dve.wait_ge(S["ya_hi"], p + 1)
                tt(yaTl[:, p, :], PS[:, 4 + p % 2, 0:T], yaTh[:, p, :].bitcast(F32), ALU.subtract
                   ).then_inc(S["ya_lo"], 1)

            s_max(0)
            for n in range(H_A):
                if n < H_A - 1:
                    s_max(n + 1)
                dve.wait_ge(S["s_exp"], 2 * n + 2)
                step(dve.reciprocal(sums[:, 2 * n:2 * n + 2], sums[:, 2 * n:2 * n + 2]))
                for c, (a, b) in enumerate(((0, P), (P, 384))):
                    last = ts(prob[n % 2][:, a:b], prob[n % 2][:, a:b], sums[:, 2 * n + c:2 * n + c + 1], None,
                              ALU.mult)
                last.then_inc(S["s_norm"], 1)
                if n % 2 == 1 and n >= 3:
                    ya_low((n - 3) // 2)
            ya_low(3)
            norm_gain(1)

            def per(v, n=P):
                return v.rearrange("p (n o) -> p n o", o=1).to_broadcast([P, v.shape[1], n])

            dve.wait_ge(S["small_mm"], 4 + 1)
            ts(l2r, PS[:, 0, 0:16], EPS2, None, ALU.add).then_inc(S["l2_ms"], 1)
            dve.wait_ge(S["small_mm"], 5 + 1)
            ts(ncum, PS[:, 1, 0:8], -1.0, None, ALU.mult).then_inc(S["small_read"], 1)
            dve.wait_ge(S["small_read"], 4 + 1)
            for t in range(TT):
                dve.wait_ge(S["gb_mm"], t + 1)
                for n in range(H_B):
                    m = 4 * t + n
                    last = stt(LT[:, m, :], tr_bank(4 + t)[:, n, :], ncum[:, m:m + 1], mask_neg[:, 0:P], ALU.add,
                               ALU.add)
                last.then_inc(S["dec_arg"], 1)
            dve.wait_ge(S["small_act"], 1 + 1)
            step(ts(necum, ecum, -1.0, None, ALU.mult))
            dve.wait_ge(S["silu_done"], 16 + 4)
            for n in range(4):
                dve.wait_ge(S["l2_bc"], n + 1)
                a = qkvT[:, 2 * n:2 * n + 2, :]
                stt(a, a, 128.0 ** -0.5 if n < 2 else 1.0, PS[:, n, :].rearrange("p (c t) -> p c t", c=2), ALU.mult,
                    ALU.mult).then_inc(S["l2_done"], 1)
            dve.wait_ge(S["small_act"], 1)
            for t in range(TT):
                dve.wait_ge(S["kk_mm"], t + 1)
                dve.wait_ge(S["dec_exp"], t + 1)
                b = slice(4 * t, 4 * t + 4)
                tt(Ub[:, b, :], tr_bank(t), LT[:, b, :], ALU.mult).then_inc(S["kk_read"], 1)
            for t in range(TT):
                dve.wait_ge(S["qk_mm"], t + 1)
                b = slice(4 * t, 4 * t + 4)
                tt(PT[:, b, :], tr_bank(2 + t), LT[:, b, :], ALU.mult).then_inc(S["pt_done"], 1)
            dve.wait_ge(S["vk_tr"], 2)
            tt(R[:, :, :], tr_bank(6), per(beta[:, 0:4]), ALU.mult).then_inc(S["vk_read"], 1)
            dve.tensor_copy(v1[:, :, :], tr_bank(7)).then_inc(S["vk_read"], 1)
            dve.wait_ge(S["vk_tr"], 3)
            tt(kd[:, :, :], tr_bank(0), LT[:, 0:4, P - 1:P].to_broadcast([P, 4, P]), ALU.mult
               ).then_inc(S["vk_read"], 1)
            for t in range(TT):
                dve.wait_ge(S["m_tr"], t + 1)
                tt(Xi[:, 4 * t:4 * t + 4, :], tr_bank(4 + t), per(beta[:, 4 * t:4 * t + 4]), ALU.mult
                   ).then_inc(S["m_read"], 1)
            dve.wait_ge(S["lev_in"], 16)

            def wide(m):
                return m.rearrange("p (o n) -> p o n", o=1).to_broadcast([P, 4, P])

            for t in range(TT):
                dve.wait_ge(S["n_read"], t + 1)
                b = slice(4 * t, 4 * t + 4)
                step(tt(XiT[:, b, :], NT[:, b, :], wide(lev[:, 0, :]), ALU.mult))
                step(tt(XiT[:, b, :], wide(ident), XiT[:, b, :], ALU.subtract))
                step(tt(Xi[:, b, :], Xi[:, b, :], wide(lev[:, 7, :]), ALU.mult))
                tt(Xi[:, b, :], wide(ident), Xi[:, b, :], ALU.subtract).then_inc(S["x_upd"], 1)
            for m in range(1, 7):
                for t in range(TT):
                    dve.wait_ge(S["vt_mm"], 2 * m + t - 1)
                    b = slice(4 * t, 4 * t + 4)
                    if m < 6:
                        tt(Xi[:, b, :], Xi[:, b, :], tr_bank(2 + t), ALU.subtract)
                    tt(XiT[:, b, :], XiT[:, b, :], tr_bank(4 + t), ALU.subtract).then_inc(S["x_upd"], 1)
            dve.wait_ge(S["ks_mm"], 1)
            for n in range(H_B):
                last = stt(R[:, n, :], tr_bank(0)[:, n, :], necum[:, 4 + n:5 + n], v1[:, n, :], ALU.mult, ALU.add)
            step(last)
            tt(R[:, :, :], R[:, :, :], per(beta[:, 4:8]), ALU.mult).then_inc(S["r1_done"], 1)
            dve.wait_ge(S["ks_mm"], 2)
            dve.wait_ge(S["o_part"], 2)
            for n in range(H_B):
                o = ob[:, 1, n * P:(n + 1) * P]
                last = stt(o, tr_bank(1)[:, n, :], ecum[:, 4 + n:5 + n], o, ALU.mult, ALU.add)
            step(last)
            o8 = ob[:, :, :].rearrange("p t (n d) -> p (t n) d", d=P)
            q8 = osq[:, :, :].rearrange("p t (n d) -> p (t n) d", d=P)
            step(tt(osq[:, :, :], ob[:, :, :], ob[:, :, :], ALU.mult))
            step(dve.reduce_sum(rs8, q8, axis=AX_X))
            ts(rs8, rs8, 1.0 / P, EPS2, ALU.mult, ALU.add).then_inc(S["o_stat"], 1)
            dve.wait_ge(S["o_rstd"], 1)
            step(tt(o8, o8, per(rs8), ALU.mult))
            step(tt(o8, o8, rr["onorm"].rearrange("p (o n) -> p o n", o=1).to_broadcast([P, 8, P]), ALU.mult))
            tt(ob[:, :, :], ob[:, :, :], zb[:, :, :], ALU.mult).then_inc(S["o_scaled"], 1)
            for t in range(TT):
                dve.wait_ge(S["yb_hi"], t + 1)
                a = ybTh[:, :, t * P:(t + 1) * P]
                tt(ybTl[:, :, t * P:(t + 1) * P], tr_bank(5 + t), a.bitcast(F32), ALU.subtract
                   ).then_inc(S["yb_lo"], 1)
            plain_splits(FIRST["up_a"], 4)

            dve.wait_ge(S["unit_done"], FIRST["wout2"])
            for t in range(TT):
                for c in range(2):
                    s = slice(512 * c, 512 * c + 512)
                    tt(mm_a[:, t, s], PS[:, 2 * c + t, :], gate_a[:, t, s], ALU.mult)
                    last = tt(gate_b[:, t, s], PS[:, 4 + 2 * c + t, :], gate_b[:, t, s], ALU.mult)
                last.then_inc(S["up_part"], 1)
            to_T(5)
            plain_splits(FIRST["wout2"], 4)

            def residual(r, last_unit, banks, gate):
                dve.wait_ge(S["unit_done"], last_unit)
                for t in range(TT):
                    for c in range(2):
                        s = slice(512 * c, 512 * c + 512)
                        last = tt(pre[:, t, s], PS[:, banks + 2 * c + t, :], gate[:, s], ALU.mult)
                    last.then_inc(S["res_t"], 1)

            residual(0, FIRST["mod5"], 0, mod[:, 2, :])
            rms(1)
            to_T(6, 0)
            mod_read(5, 4)

            def over(v, n):
                return v.rearrange("p (t o) -> p t o", o=1).to_broadcast([P, TT, n])

            def first_best(dst, v, best, tmp, n):
                step(tt(dst, v, over(best, n), ALU.is_equal))
                step(tt(dst, dst, rank[:, 0:n].rearrange("p (o n) -> p o n", o=1).to_broadcast([P, TT, n]), ALU.mult))
                step(dve.reduce_max(tmp, dst, axis=AX_X))
                step(tt(dst, dst, over(tmp, n), ALU.is_equal))

            dve.wait_ge(S["small_mm"], 6 + 1)
            tt(lg[:, :, :], PS[:, 0, 0:128].rearrange("p (t n) -> p t n", t=TT)[:, :, 0:36],
               rr["b_route"].rearrange("p (o n) -> p o n", o=1).to_broadcast([P, TT, 36]), ALU.add
               ).then_inc(S["small_read"], 1)
            dve.wait_ge(S["small_read"], 5 + 1)
            step(dve.reduce_max(rsc[:, 0:2], lg[:, :, 0:4], axis=AX_X))
            ts(rsc[:, 2:4], rsc[:, 0:2], -1.0, None, ALU.mult).then_inc(S["rt_max"], 1)
            oh_g, leg, oh1, oh2 = route[:, 0, :, 0:4], route[:, 2, :, :], route[:, 3, :, :], route[:, 4, :, :]
            first_best(oh_g, lg[:, :, 0:4], rsc[:, 0:2], rsc[:, 6:8], 4)
            for t in range(TT):
                g4 = oh_g[:, t, :].rearrange("p (g o) -> p g o", o=1).to_broadcast([P, 4, 8])
                step(tt(le[:, t, :].rearrange("p (g e) -> p g e", g=4),
                        lg[:, t, 4:36].rearrange("p (g e) -> p g e", g=4), g4, ALU.mult))
                step(dve.reduce_sum(leg[:, t, :], le[:, t, :].rearrange("p (g e) -> p e g", g=4), axis=AX_X))
            step(dve.reduce_max(rsc[:, 8:10], leg, axis=AX_X))
            first_best(oh1, leg, rsc[:, 8:10], rsc[:, 6:8], 8)
            step(stt(leg, oh1, NEG, leg, ALU.mult, ALU.add))
            step(dve.reduce_max(rsc[:, 10:12], leg, axis=AX_X))
            first_best(oh2, leg, rsc[:, 10:12], rsc[:, 6:8], 8)
            tt(rsc[:, 10:12], rsc[:, 10:12], rsc[:, 8:10], ALU.subtract).then_inc(S["rt_max"], 1)
            dve.wait_ge(S["small_act"], 2 + 3)
            step(ts(rsc[:, 12:14], rsc[:, 10:12], 1.0, None, ALU.add))
            step(tt(rsc[:, 12:14], rsc[:, 12:14], rsc[:, 4:6], ALU.mult))
            step(dve.reciprocal(rsc[:, 12:14], rsc[:, 12:14]))
            step(tt(rsc[:, 10:12], rsc[:, 10:12], rsc[:, 12:14], ALU.mult))
            step(tt(oh1, oh1, over(rsc[:, 12:14], 8), ALU.mult))
            step(tt(oh2, oh2, over(rsc[:, 10:12], 8), ALU.mult))
            step(tt(oh1, oh1, oh2, ALU.add))
            for t in range(TT):
                g4 = oh_g[:, t, :].rearrange("p (g o) -> p g o", o=1).to_broadcast([P, 4, 8])
                e4 = oh1[:, t, :].rearrange("p (o e) -> p o e", o=1).to_broadcast([P, 4, 8])
                last = tt(comb[:, t, :].rearrange("p (g e) -> p g e", g=4), g4, e4, ALU.mult)
            last.then_inc(S["rt_done"], 1)

            dve.wait_ge(S["small_mm"], 7 + 1)
            step(dve.tensor_copy(place[:, 0:12], PS[:, 2, 0:12]))
            step(dve.reduce_max(place[:, 12:13], place[:, 8:12], axis=AX_X))
            dve.tensor_copy(most[:, :], place[:, 12:13]).then_inc(S["small_read"], 1)
            dve.wait_ge(S["small_read"], 6 + 1)

            b = FIRST["moe"]

            def moe(nt):
                def low(e, n):
                    dve.wait_ge(S["act_hi"], 32 + e + 1)
                    tt(eTl[n % 2][:, :, 0:nt * P], PS[:, 2, 0:2 * nt * P].rearrange("p (c t) -> p c t", c=2),
                       eTh[n % 2][:, :, 0:nt * P].bitcast(F32), ALU.subtract).then_inc(S["act_lo"], 1)

                def gated(e, n):
                    for t in range(nt):
                        dve.wait_ge(S["g_silu"], nt * e + t + 1)
                        w = (slot_comb[:, bass.ds(e, 1)] if nt == 1
                             else comb[:, t, bass.ds(e, 1)])
                        s = slice(256 * t, 256 * t + 256)
                        stt(ubuf[n % 2][:, s], PS[:, n % 2 if nt == 1 else t, 256:512], w, gbuf[n % 2][:, s],
                            ALU.mult, ALU.mult).then_inc(S["gu_done"], 1)

                def group_low(g):
                    for c in range(2):
                        dve.wait_ge(S["tr_hi"], 28 + 2 * g + c + 1)
                        tt(hgl[:, 4 * c:4 * c + 4, :], tr_bank(7), hgh[:, 4 * c:4 * c + 4, :].bitcast(F32),
                           ALU.subtract).then_inc(S["tr_lo"], 1)

                def add_group(g):
                    for t in range(TT):
                        dve.wait_ge(S["sc_mm"], 2 * g + t + 1)
                        a = h[:, t, :].rearrange("p (c n) -> p c n", c=2)
                        tt(a, a, PS[:, 5:7, :], ALU.add).then_inc(S["sc_read"], 1)

                def group(g):
                    for n in range(8):
                        e = 8 * g + n
                        if n >= 1:
                            low(e - 1, n - 1)
                        q, s = unit(b, max(3 * n - 1, 0), g, 24)
                        split(q + 1, s)
                        gated(e, n)
                        q, s = unit(b, max(3 * n, 1), g, 24)
                        split(q + 1, s)
                        if n == 0 and nt == 1 and not (isinstance(g, int) and g == 0):
                            add_group(g - 1)
                        if n >= 1:
                            q, s = unit(b, 3 * n + 1, g, 24)
                            split(q + 1, s)
                    low(8 * g + 7, 7)
                    if nt == 1 and not (isinstance(g, int) and g == 3):
                        group_low(g + 1)
                    q, s = unit(b, 23, g, 24)
                    if nt == 1:
                        dve.wait_ge(S["unit_done"], 4 * q + s + 1)
                        tt(yg[:, :].rearrange("p (c n) -> p c n", c=2), PS[:, 3:5, :],
                           mod[:, 5, :].rearrange("p (c n) -> p c n", c=2), ALU.mult).then_inc(S["yg_sb"], 1)
                    split(q + 1, s)

                dve.wait_ge(S["pool_init"], 2 + 1)
                if nt == 1:
                    for g in range(4):
                        for t in range(TT):
                            n = 4 * t + g
                            last = ts(gather[:, g, t, :], slots[:, :], place[:, n:n + 1], route[:, 0, t, g:g + 1],
                                      ALU.is_equal, ALU.mult)
                        if g in (0, 3):
                            last.then_inc(S["gather_ready"], 1)
                    group_low(0)
                    dve.wait_ge(S["small_mm"], 8 + 1)
                    dve.tensor_copy(slot_comb[:, :], PS[:, 2, 0:32]).then_inc(S["small_read"], 1)
                    dve.wait_ge(S["small_read"], 7 + 1)
                group(0)
                with dve.Fori(1, 3) as g:
                    group(g)
                group(3)
                if nt == 1:
                    add_group(3)
                    dve.wait_ge(S["sc_read"], 8)
                    dve.engine_nop().then_inc(S["moe_done"], 2)
                else:
                    dve.wait_ge(S["unit_done"], UNITS)
                    for t in range(TT):
                        for c in range(2):
                            s = slice(512 * c, 512 * c + 512)
                            dense(tt(pre[:, t, s], PS[:, 3 + 2 * c + t, :], mod[:, 5, s], ALU.mult), 2 * t + c + 1)
                        tt(h[:, t, :], h[:, t, :], pre[:, t, :], ALU.add).then_inc(S["moe_done"], 1)

            def dense(instruction, n):
                instruction.then_inc(S["dense_step"], 1)
                dve.wait_ge(S["dense_step"], n)

            crowd = dve.value_load(most[0:1, 0:1], min_val=0, max_val=T)
            with dve.If(crowd <= CROWD):
                moe(1)
            with dve.Else():
                moe(2)
            dve.wait_ge(S["moe_done"], 2)
            rms(2)

        @block.gpsimd
        def _(pool):
            pool.memset(mhalf, -0.5).then_inc(S["pool_init"], 1)
            pool.wait_ge(S["pool_init"], 1)

            def gated(hp):
                pool.wait_ge(S["y_read"], hp + 1)
                pool.tensor_tensor(zT[:, hp, :], ysk[hp % 2][:, :], zT[:, hp, :], ALU.mult).then_inc(S["yg_done"], 1)

            def y_rstd(g):
                pool.wait_ge(S["ms_read"], g + 1)
                a = yrs[:, 2 * g:2 * g + 2]
                pool.tensor_tensor(a, a, mhalf[:, 0:2], ALU.pow).then_inc(S["y_rstd"], 1)

            for hp in range(PAIRS):
                pool.wait_ge(S["exp_done"], hp + 1)
                pool.wait_ge(S["cb_read"], hp // 2 + 1)
                d = dec[hp % 3][:, :, :]
                pool.tensor_tensor(d, d, cbs[hp // 2 % 2][:, :].rearrange("p (o n) -> p o n", o=1
                                                                          ).to_broadcast([P, 2, 384]),
                                   ALU.mult).then_inc(S["m_ready"], 1)
                if hp >= 1:
                    gated(hp - 1)
                if hp % 2 == 0 and hp >= 6:
                    y_rstd((hp - 6) // 2)
            gated(PAIRS - 1)
            for g in range(5, GROUPS):
                y_rstd(g)

            def layer_norm(r, free):
                for signal, value in free:
                    pool.wait_ge(signal, value)
                pool.dma_start(ln_row[:, :, :].rearrange("p a d -> p (a d)"),
                               ln_rows[r:r + 1, :].to_broadcast([P, 2 * D])).then_inc(S["row_in"], 16)
                if r == 0:
                    pool.dma_start(mod[:, :, :].rearrange("p a d -> p (a d)"), b_mod.to_broadcast([P, 6 * D])
                                   ).then_inc(S["mod_in"], 16)
                for t in range(TT):
                    pool.wait_ge(S["ln_var"], TT * r + t + 1)
                    pool.tensor_tensor(rstd[:, t:t + 1], veps[:, t:t + 1], mhalf[:, 0:1], ALU.pow
                                       ).then_inc(S["ln_rstd"], 1)
                pool.wait_ge(S["row_in"], 16 * r + 16)
                pool.wait_ge(S["ln_gain"], r + 1)
                pool.tensor_tensor(h[:, 0, :], pre[:, 0, :], ln_row[:, 1, :], ALU.add).then_inc(S["h_ready"], 1)

            layer_norm(0, [(S["unit_done"], FIRST["mod0"])])
            layer_norm(1, [(S["h_ready"], 1), (S["h1_ready"], 1)])

            def masked(b):
                for c in range(2):
                    for a in (0, T):
                        last = pool.tensor_tensor(b[:, c, a:a + P], b[:, c, a:a + P], before, ALU.mult)
                return last

            for p in range(SB_PAIRS + 1):
                if p < SB_PAIRS:
                    pool.wait_ge(S["sb_zl"], p + 1)
                    masked(nbuf[p % 2]).then_inc(S["sb_mask"], 1)
                if p >= 1:
                    pool.wait_ge(S["sb_w"], p)
                    masked(wbuf[(p - 1) % 2]).then_inc(S["sb_wm"], 1)
            layer_norm(2, [(S["h_ready"], 2), (S["h1_ready"], 2)])
            pool.wait_ge(S["unit_done"], FIRST["mod2"])
            pool.dma_start(rms_row[0][:, :], rms_rows[:, 0:D].to_broadcast([P, D])).then_inc(S["rms_rows_in"], 16)
            layer_norm(3, [(S["h_ready"], 3), (S["h1_ready"], 3)])

            def rms(r):
                for t in range(TT):
                    pool.wait_ge(S["ln_var"], 8 + TT * r + t + 1)
                    pool.tensor_tensor(rstd[:, t:t + 1], veps[:, t:t + 1], mhalf[:, 0:1], ALU.pow
                                       ).then_inc(S["ln_rstd"], 1)
                if r < 2:
                    pool.wait_ge(S["rms_t"], r + 1)
                    pool.tensor_tensor(hn[:, 0, :], hn[:, 0, :], mod[:, 3 * r, :], ALU.add
                                       ).then_inc(S["h_ready"], 1)

            pool.wait_ge(S["h_ready"], 4)
            pool.memset(relb[32:33, :], 1.0).then_inc(S["pool_init"], 1)
            pool.wait_ge(S["pool_init"], 1 + 1)
            pool.dma_start(relb[0:32, :], rel_bias).then_inc(S["tab_in"], 16)
            pool.dma_start(tabs[:, 0:TABLE_W], onehot).then_inc(S["tab_in"], 16)
            rms(0)
            pool.wait_ge(S["h_ready"], 4 + 1)
            pool.wait_ge(S["h1_ready"], 4 + 1)
            pool.dma_start(lev[:, :, :].rearrange("p a b -> p (a b)"), levels).then_inc(S["lev_in"], 16)
            pool.wait_ge(S["tab_sb"], 1)
            pool.dma_start(table_dram[:, :], tabs[0:H_A, TABLE_W:2 * TABLE_W]).then_inc(S["tab_out"], 16)
            pool.wait_ge(S["tab_out"], 16)
            pool.wait_ge(S["unit_done"], FIRST["mod4"])
            pool.dma_start(hank[:, :, 0:P], bass.AP(table_dram, P, [[1, P], [TABLE_W, H_A], [1, P]])
                           ).then_inc(S["hank_in"], 16)
            pool.dma_start(hank[:, :, P:384], bass.AP(table_dram, 0, [[1, P], [TABLE_W, H_A], [1, T]])
                           ).then_inc(S["hank_in"], 16)
            pool.dma_start(rms_row[1][:, :], rms_rows[:, D:2 * D].to_broadcast([P, D])).then_inc(S["rms_rows_in"], 16)
            pool.wait_ge(S["l2_ms"], 1)
            pool.tensor_tensor(l2r, l2r, mhalf[:, 0:1].to_broadcast([P, 16]), ALU.pow).then_inc(S["l2_rstd"], 1)

            def wide(m):
                return m.rearrange("p (o n) -> p o n", o=1).to_broadcast([P, 4, P])

            for t in range(TT):
                pool.wait_ge(S["kk_read"], t + 1)
                a = Ub[:, 4 * t:4 * t + 4, :]
                pool.tensor_tensor(a, a, wide(before), ALU.mult).then_inc(S["kk_masked"], 1)
            pool.wait_ge(S["vk_read"], 3)
            pool.wait_ge(S["lev_in"], 16)
            for m in range(1, 7):
                for t in range(TT):
                    pool.wait_ge(S["n_read"], t + 1)
                    if m >= 2:
                        pool.wait_ge(S["u_mm"], 2 * (m - 1) + t - 1)
                    b = slice(4 * t, 4 * t + 4)
                    pool.tensor_tensor(LT[:, b, :], NT[:, b, :], wide(lev[:, m, :]), ALU.mult
                                       ).then_inc(S["lt_done"], 1)
            pool.wait_ge(S["o_stat"], 1)
            pool.tensor_tensor(rs8, rs8, mhalf, ALU.pow).then_inc(S["o_rstd"], 1)
            for t in range(TT):
                pool.wait_ge(S["up_part"], t + 1)
                pool.tensor_tensor(mm_a[:, t, :], mm_a[:, t, :], gate_b[:, t, :], ALU.add).then_inc(S["mix_ready"], 1)

            def residual(r):
                for t in range(TT):
                    pool.wait_ge(S["res_t"], TT * r + t + 1)
                    pool.tensor_tensor(h[:, t, :], h[:, t, :], pre[:, t, :], ALU.add).then_inc(S["res_done"], 1)

            residual(0)
            rms(1)
            pool.wait_ge(S["h_ready"], 4 + 2)
            pool.wait_ge(S["h1_ready"], 4 + 2)
            pool.iota(slots[:, :], pattern=[[1, P]], base=0, channel_multiplier=0,
                      allow_small_or_imprecise_dtypes=True).then_inc(S["pool_init"], 1)
            pool.dma_start(final_row[:, :], rms_rows[:, 2 * D:3 * D].to_broadcast([P, D])).then_inc(S["final_in"], 16)
            pool.wait_ge(S["pool_init"], 2 + 1)
            rms(2)


def _tiles(w, k):
    return w.reshape(k, P, -1).transpose(1, 0, 2).reshape(P, -1)


def _pack(np, inputs):
    units = []

    def wide(w):
        units.extend(_tiles(w[:, n:n + 256], KD) for n in range(0, w.shape[1], 256))

    def deep(w):
        units.extend(_tiles(w[k:k + 512, n:n + 512], 4)
                     for n in range(0, w.shape[1], 512) for k in range(0, w.shape[0], 512))

    def mlp(w1, w2):
        for j in range(CHUNKS + 1):
            if j < CHUNKS:
                units.append(_tiles(w1[:, 256 * j:256 * j + 256], KD))
            if j >= 1:
                units.append(_tiles(w2[256 * (j - 1):256 * j], 2))

    def mod(k):
        deep(inputs["w_mod_2"][0][:, D * k:D * k + D])

    w_in = inputs["ssm_w_in"][0]
    wide(w_in[:, D_INNER:3 * D_INNER])
    wide(w_in[:, 0:D_INNER])
    deep(inputs["ssm_w_out"][0])
    mod(0)
    mlp(inputs["mlp_w1"][0], inputs["mlp_w2"][0])
    mod(1)
    wide(inputs["sb_w_k"])
    wide(inputs["sb_w_q"][0])
    deep(inputs["sb_w_v"])
    deep(inputs["sb_w_o"][0])
    mod(2)
    mlp(inputs["mlp_w1"][1], inputs["mlp_w2"][1])
    mod(3)
    w2 = inputs["w_in_2"][0]
    wide(w2[:, 0:1024])
    deep(w2[:, 1024:1536])
    wide(w2[:, 1536:3072])
    deep(w2[:, 3072:3584])
    deep(w2[:, 3592:5640])
    mod(4)
    deep(inputs["w_up_a_2"][0])
    deep(inputs["w_up_b_2"][0])
    deep(inputs["w_out_2"][0])
    mod(5)
    gate, up, down = (inputs[f"w_e_{n}_2"][0].reshape((EXPERTS,) + inputs[f"w_e_{n}_2"].shape[3:])
                      for n in ("gate", "up", "down"))
    for g in range(0, EXPERTS, 8):
        for e in range(g, g + 9):
            if e < g + 8:
                deep(np.concatenate([gate[e], up[e]], 1))
            if e > g:
                units.append(_tiles(down[e - 1], 2))
    small = np.concatenate([w_in[:, 3 * D_INNER:], w2[:, 3584:3592], inputs["w_rg_2"][0], inputs["w_re_2"][0]], 1)
    cols = np.concatenate([
        inputs["ssm_conv_w"][0].reshape(4, 32, P).transpose(2, 1, 0).reshape(P, 128),
        inputs["ssm_conv_b"][0].reshape(32, P).T,
        np.repeat(inputs["ssm_d"][0], 64).reshape(16, P).T,
        inputs["ssm_norm_w"][0].reshape(16, P).T,
        inputs["conv_w_2"][0].reshape(4, 12, P).transpose(2, 1, 0).reshape(P, 48),
        inputs["c_2"].reshape(KD, P).T], 1)
    rows = np.concatenate([inputs[n].reshape(-1) for n in
                           ("ssm_dt_bias", "ssm_a_log", "a_log_2", "dt_bias_2", "onorm_w_2", "b_rg_2", "b_re_2")])
    ln = np.stack([np.concatenate([inputs[f"ln_{n}_g"][m], inputs[f"ln_{n}_b"][m]])
                   for m in range(2) for n in ("mix", "mlp")])
    rms = np.concatenate([inputs["norm1_w_2"][0], inputs["norm2_w_2"][0], inputs["final_norm_w_2"]])
    return {"x": inputs["x"][0], "weights": np.stack(units), "small": _tiles(small, KD), "cols": cols,
            "rows": rows[None], "ln_rows": ln, "rms_rows": rms[None], "b_mod": inputs["b_mod_2"],
            "rel_bias": inputs["rel_bias_2"]}


def _constants(np):
    i, j = np.arange(P)[:, None], np.arange(P)[None, :]
    consts = np.concatenate([i == j, i + j == P - 1, i <= j, i >= 0 * j, np.where(i <= j, 0.0, NEG),
                             0.0 * (i + j), i > j, i < j, np.broadcast_to(8 - np.arange(8), (P, 8))],
                            1).astype(np.float32)
    pairs = [((j >> m + 1) == (i >> m + 1)) & ((j >> m) > (i >> m)) for m in range(7)]
    levels = np.stack(pairs + [pairs[0].T], 1).astype(np.float32).reshape(P, 8 * P)
    dist = 255 - np.arange(TABLE_W)
    n = np.maximum(dist, 1).astype(np.float32)
    large = np.minimum(16 + (np.log(n / 16) / np.log(128 / 16) * 16).astype(np.int32), 31)
    bucket = np.where(dist < 16, dist, large)
    onehot = np.zeros((33, TABLE_W), np.float32)
    for x in range(TABLE_W):
        onehot[bucket[x] if dist[x] >= 0 else 32, x] = 1.0 if dist[x] >= 0 else NEG
    return {"consts": consts, "levels": levels, "onehot": onehot}


def kernel(**inputs):
    import numpy as np
    import concourse.bacc as bacc
    from concourse.bass_utils import run_bass_kernel_spmd

    arrays = {**_pack(np, {n: np.asarray(a) for n, a in inputs.items()}), **_constants(np)}
    arrays = {n: np.ascontiguousarray(a) for n, a in arrays.items()}
    nc = bacc.Bacc("TRN2", target_bir_lowering=False, num_devices=1)
    args = {n: nc.dram_tensor(n, a.shape, mybir.dt.from_np(a.dtype), kind="ExternalInput").ap()
            for n, a in arrays.items()}
    out = nc.dram_tensor("out", (T, D), F32, kind="ExternalOutput")
    build(nc, out=out.ap(), **args)
    r = run_bass_kernel_spmd(nc, [arrays], core_ids=[0])
    return r.results[0]["out"].reshape(1, T, D)
```
